# Optimizing a Trainium2 kernel written in Bass

```python
import jax, jax.numpy as jnp
from jax import lax
import numpy as np
import math
import jax
import jax.numpy as jnp

D_MODEL = 1024
BATCH = 1
SEQ = 1024
DEPTH = 1

D_MIX = D_MODEL
D_A = D_MIX // 2
D_B = D_MIX - D_A
HEAD_DIM = 64
N_GROUPS_A = D_A // HEAD_DIM
N_GROUPS_B = D_B // HEAD_DIM
K_SHORT = 3
K_CONFORMER = 31
K_FFN = 3
D_FF = 2816
D_IN = 3 * D_A + 2 * D_B
RMS_EPS = 1e-6
LN_EPS = 1e-5


def rmsnorm(x, g):
    xf = x.astype(jnp.float32)
    y = xf * lax.rsqrt(jnp.mean(xf * xf, axis=-1, keepdims=True) + RMS_EPS)
    return (y * g.astype(jnp.float32)).astype(x.dtype)

def layernorm(x, g, b):
    xf = x.astype(jnp.float32)
    mu = jnp.mean(xf, axis=-1, keepdims=True)
    var = jnp.mean(jnp.square(xf - mu), axis=-1, keepdims=True)
    y = (xf - mu) * lax.rsqrt(var + LN_EPS)
    return (y * g.astype(jnp.float32) + b.astype(jnp.float32)).astype(x.dtype)

def dwconv(x, w):
    k, c = w.shape
    rhs = w[:, None, :].astype(x.dtype)
    return lax.conv_general_dilated(
        x, rhs, window_strides=(1,), padding=[(k // 2, k // 2)],
        dimension_numbers=("NWC", "WIO", "NWC"), feature_group_count=c)

def first_inputs(seed: int = 0) -> dict:
    key = jax.random.key(seed)
    ks = jax.random.split(key, 16)
    f32 = jnp.float32

    def nrm(k, shape, scale):
        return jax.random.normal(k, shape, f32) * scale

    return {
        "x": jax.random.normal(ks[0], (BATCH, SEQ, D_MODEL), f32),
        "norm_mix_g": 1.0 + nrm(ks[1], (DEPTH, D_MODEL), 0.05),
        "w_in": nrm(ks[2], (DEPTH, D_MODEL, D_IN), D_MODEL ** -0.5),
        "conv_a_w": nrm(ks[3], (DEPTH, K_SHORT, D_A), K_SHORT ** -0.5),
        "conv_b_w": nrm(ks[4], (DEPTH, K_CONFORMER, D_B), K_CONFORMER ** -0.5),
        "conv_b_b": nrm(ks[5], (DEPTH, D_B), 0.02),
        "ln_b_g": 1.0 + nrm(ks[6], (DEPTH, D_B), 0.05),
        "ln_b_b": nrm(ks[7], (DEPTH, D_B), 0.02),
        "w_out": nrm(ks[8], (DEPTH, D_MIX, D_MODEL), D_MIX ** -0.5),
        "norm_ffn_g": 1.0 + nrm(ks[9], (DEPTH, D_MODEL), 0.05),
        "w_gate": nrm(ks[10], (DEPTH, D_MODEL, D_FF), D_MODEL ** -0.5),
        "w_up": nrm(ks[11], (DEPTH, D_MODEL, D_FF), D_MODEL ** -0.5),
        "conv_ffn_w": nrm(ks[12], (DEPTH, K_FFN, D_FF), K_FFN ** -0.5),
        "w_down": nrm(ks[13], (DEPTH, D_FF, D_MODEL), D_FF ** -0.5),
        "norm_final_g": 1.0 + nrm(ks[14], (D_MODEL,), 0.05),
    }

def first_block(x, norm_mix_g, w_in, conv_a_w, conv_b_w, conv_b_b, ln_b_g, ln_b_b,
              w_out, norm_ffn_g, w_gate, w_up, conv_ffn_w, w_down, norm_final_g):
    for l in range(DEPTH):
        h = rmsnorm(x, norm_mix_g[l])
        z = jnp.einsum("bsd,de->bse", h, w_in[l])
        a_h, a_bg, a_cg, b_val, b_gate = jnp.split(
            z, [D_A, 2 * D_A, 3 * D_A, 3 * D_A + D_B], axis=-1)
        y_a = a_bg * dwconv(a_cg * a_h, conv_a_w[l])
        u = b_val * jax.nn.sigmoid(b_gate)
        u = dwconv(u, conv_b_w[l]) + conv_b_b[l].astype(u.dtype)
        y_b = jax.nn.silu(layernorm(u, ln_b_g[l], ln_b_b[l]))
        y = jnp.concatenate([y_a, y_b], axis=-1)
        x = x + jnp.einsum("bse,ed->bsd", y, w_out[l])

        h = rmsnorm(x, norm_ffn_g[l])
        g = dwconv(jnp.einsum("bsd,df->bsf", h, w_gate[l]), conv_ffn_w[l])
        v = jnp.einsum("bsd,df->bsf", h, w_up[l])
        x = x + jnp.einsum("bsf,fd->bsd", jax.nn.silu(g) * v, w_down[l])

    return rmsnorm(x, norm_final_g)


N_META = 16
CHUNK = 64
EPS = 1e-6
HG_HEADS = 4
HG_DIM = 128
HG_WIDTH = HG_HEADS * HG_DIM
GD_HEADS = 4
GD_DK = 128
GD_DV = 128
CONV_W = 4
N_GROUPS = 4
EXPERTS_PER_GROUP = 8
N_EXPERTS = N_GROUPS * EXPERTS_PER_GROUP
TOP_K_FINE = 2
D_FF_EXPERT = 512
MOE_BLOCK = 128
PROJ_SIZES = (HG_WIDTH, HG_WIDTH, HG_WIDTH, HG_WIDTH,
              GD_HEADS * GD_DK, GD_HEADS * GD_DK, GD_HEADS * GD_DV, GD_HEADS * GD_DV,
              GD_HEADS, GD_HEADS, D_MODEL, D_MODEL)
D_PROJ = sum(PROJ_SIZES)


def rmsnorm_2(x, g):
    xf = x.astype(jnp.float32)
    y = xf * lax.rsqrt(jnp.mean(xf * xf, axis=-1, keepdims=True) + EPS) * g.astype(jnp.float32)
    return y.astype(x.dtype)

def head_rmsnorm(o, g):
    return o * lax.rsqrt(jnp.mean(o * o, axis=-1, keepdims=True) + EPS) * g.astype(jnp.float32)

def l2norm(t):
    return t * lax.rsqrt(jnp.sum(t * t, axis=-1, keepdims=True) + EPS)

def causal_depthwise_conv(x, w):
    return lax.conv_general_dilated(
        x, w[:, None, :].astype(x.dtype), window_strides=(1,), padding=[(CONV_W - 1, 0)],
        dimension_numbers=('NWC', 'WIO', 'NWC'), feature_group_count=x.shape[-1])

def run_chunked(step, state0, seqs):
    bsz, length = seqs[0].shape[:2]
    n_chunks = (length - N_META) // CHUNK
    state, out_meta = step(state0, tuple(s[:, :N_META] for s in seqs))
    real = tuple(jnp.moveaxis(s[:, N_META:].reshape(bsz, n_chunks, CHUNK, *s.shape[2:]), 1, 0) for s in seqs)
    _, out_real = lax.scan(step, state, real)
    out_real = jnp.moveaxis(out_real, 0, 1).reshape(bsz, n_chunks * CHUNK, *out_real.shape[3:])
    return jnp.concatenate([out_meta, out_real], axis=1)

def hgrn2_chunk(S, inp):
    q, k, v, logf = inp
    C = q.shape[1]
    b = jnp.cumsum(logf, axis=1)
    incl = jnp.tril(jnp.ones((C, C), dtype=bool))
    decay = jnp.exp(jnp.where(incl[None, :, :, None, None], b[:, :, None] - b[:, None, :], -jnp.inf))
    attn = jnp.einsum('bthk,bshk,btshk->bhts', q, k, decay)
    o = jnp.einsum('bthk,bhkv->bthv', q * jnp.exp(b), S) + jnp.einsum('bhts,bshv->bthv', attn, v)
    b_end = b[:, -1:]
    S_new = jnp.exp(b_end[:, 0])[..., None] * S + jnp.einsum('bshk,bshv->bhkv', k * jnp.exp(b_end - b), v)
    return S_new, o

def gdn_chunk(S, inp):
    q, k, v, beta, g = inp
    C = q.shape[1]
    q, k, v = (t.transpose(0, 2, 1, 3) for t in (q, k, v))
    beta = beta.transpose(0, 2, 1)
    G = jnp.cumsum(g, axis=1).transpose(0, 2, 1)
    incl = jnp.tril(jnp.ones((C, C), dtype=bool))
    strict = jnp.tril(jnp.ones((C, C), dtype=bool), -1)
    ratio = jnp.exp(jnp.where(incl, G[..., :, None] - G[..., None, :], -jnp.inf))
    L = jnp.where(strict, beta[..., :, None] * ratio * jnp.einsum('bhtk,bhsk->bhts', k, k), 0.0)
    rhs = jnp.concatenate([beta[..., None] * v, (beta * jnp.exp(G))[..., None] * k], axis=-1)
    sol = lax.linalg.triangular_solve(jnp.eye(C, dtype=L.dtype) + L, rhs,
                                      left_side=True, lower=True, unit_diagonal=True)
    u0, w = sol[..., :GD_DV], sol[..., GD_DV:]
    u = u0 - jnp.einsum('bhtk,bhkv->bhtv', w, S)
    attn = jnp.einsum('bhtk,bhsk->bhts', q, k) * ratio
    o = jnp.exp(G)[..., None] * jnp.einsum('bhtk,bhkv->bhtv', q, S) + jnp.einsum('bhts,bhsv->bhtv', attn, u)
    G_end = G[..., -1:]
    S_new = jnp.exp(G_end)[..., None] * S + jnp.einsum('bhsk,bhsv->bhkv', k * jnp.exp(G_end - G)[..., None], u)
    return S_new, o.transpose(0, 2, 1, 3)

def token_mixer(h, lb, w_in, conv_w, A_log, dt_bias, hg_norm_g, gd_norm_g, hg_up, gd_up, w_out):
    f32 = jnp.float32
    bsz, length, _ = h.shape
    idx = []
    acc = 0
    for s in PROJ_SIZES[:-1]:
        acc += s
        idx.append(acc)
    proj = h @ w_in.astype(h.dtype)
    hq, hf, hi, hg, gq, gk, gv, gz, gbeta, ga, pre_ga, pre_gb = jnp.split(proj, idx, axis=-1)

    def heads(t, n_h, d):
        return t.reshape(bsz, length, n_h, d)
    fgate = lb + (1.0 - lb) * jax.nn.sigmoid(hf.astype(f32))
    q_a = heads(jax.nn.silu(hq.astype(f32)), HG_HEADS, HG_DIM)
    k_a = heads(1.0 - fgate, HG_HEADS, HG_DIM)
    logf = heads(jnp.log(fgate), HG_HEADS, HG_DIM)
    v_a = heads(hi.astype(f32), HG_HEADS, HG_DIM)
    S0a = jnp.zeros((bsz, HG_HEADS, HG_DIM, HG_DIM), f32)
    o_a = run_chunked(hgrn2_chunk, S0a, (q_a, k_a, logf and v_a, logf) if False else (q_a, k_a, v_a, logf))
    o_a = head_rmsnorm(o_a, hg_norm_g) * jax.nn.silu(heads(hg.astype(f32), HG_HEADS, HG_DIM))
    o_a = o_a.reshape(bsz, length, HG_WIDTH).astype(h.dtype)

    qkv = jax.nn.silu(causal_depthwise_conv(jnp.concatenate([gq, gk, gv], axis=-1), conv_w)).astype(f32)
    cq, ck, cv = jnp.split(qkv, [GD_HEADS * GD_DK, 2 * GD_HEADS * GD_DK], axis=-1)
    q_b = l2norm(heads(cq, GD_HEADS, GD_DK)) * (GD_DK ** -0.5)
    k_b = l2norm(heads(ck, GD_HEADS, GD_DK))
    v_b = heads(cv, GD_HEADS, GD_DV)
    beta = jax.nn.sigmoid(gbeta.astype(f32))
    g = -jnp.exp(A_log.astype(f32)) * jax.nn.softplus(ga.astype(f32) + dt_bias.astype(f32))
    S0b = jnp.zeros((bsz, GD_HEADS, GD_DK, GD_DV), f32)
    o_b = run_chunked(gdn_chunk, S0b, (q_b, k_b, v_b, beta, g))
    o_b = head_rmsnorm(o_b, gd_norm_g) * jax.nn.silu(heads(gz.astype(f32), GD_HEADS, GD_DV))
    o_b = o_b.reshape(bsz, length, GD_HEADS * GD_DV).astype(h.dtype)

    merged = (jax.nn.sigmoid(pre_ga) * (o_a @ hg_up.astype(h.dtype))
              + jax.nn.sigmoid(pre_gb) * (o_b @ gd_up.astype(h.dtype)))
    return merged @ w_out.astype(h.dtype)

def hierarchical_moe(h, rg_w, rg_b, re_w, re_b, w_gate, w_up, w_down):
    bsz, length, d = h.shape
    T = bsz * length
    xf = h.reshape(T, d)
    g_logits = (xf @ rg_w.astype(h.dtype)).astype(jnp.float32) + rg_b.astype(jnp.float32)
    g_prob = jax.nn.softmax(g_logits, axis=-1)
    grp = jnp.argmax(g_logits, axis=-1)
    p_grp = jnp.take_along_axis(g_prob, grp[:, None], axis=-1)
    e_logits = ((xf @ re_w.astype(h.dtype)).astype(jnp.float32) + re_b.astype(jnp.float32))
    e_logits = e_logits.reshape(T, N_GROUPS, EXPERTS_PER_GROUP)
    sel = jnp.take_along_axis(e_logits, grp[:, None, None], axis=1)[:, 0]
    top_p, top_i = lax.top_k(jax.nn.softmax(sel, axis=-1), TOP_K_FINE)
    weights = p_grp * top_p / jnp.sum(top_p, axis=-1, keepdims=True)
    expert_ids = grp[:, None] * EXPERTS_PER_GROUP + top_i

    A = T * TOP_K_FINE
    e_flat = expert_ids.reshape(A).astype(jnp.int32)
    tok_flat = jnp.repeat(jnp.arange(T, dtype=jnp.int32), TOP_K_FINE)
    w_flat = weights.reshape(A)
    order = jnp.argsort(e_flat)
    e_s, tok_s, w_s = e_flat[order], tok_flat[order], w_flat[order]
    counts = jnp.bincount(e_flat, length=N_EXPERTS)
    start = jnp.cumsum(counts) - counts
    padded = ((counts + MOE_BLOCK - 1) // MOE_BLOCK) * MOE_BLOCK
    pend = jnp.cumsum(padded)
    pstart = pend - padded
    dest = pstart[e_s] + (jnp.arange(A, dtype=jnp.int32) - start[e_s])
    n_blocks = -(-A // MOE_BLOCK) + N_EXPERTS
    P = n_blocks * MOE_BLOCK
    row_tok = jnp.full((P,), T, dtype=jnp.int32).at[dest].set(tok_s)
    x_ext = jnp.concatenate([xf, jnp.zeros((1, d), xf.dtype)], axis=0)
    x_buf = x_ext[row_tok].reshape(n_blocks, MOE_BLOCK, d)
    blk_expert = jnp.clip(jnp.searchsorted(pend, jnp.arange(n_blocks) * MOE_BLOCK, side='right'), 0, N_EXPERTS - 1)

    def expert_block(args):
        xb, e = args
        a = xb @ w_gate[e].astype(xb.dtype)
        u = xb @ w_up[e].astype(xb.dtype)
        return (jax.nn.silu(a) * u) @ w_down[e].astype(xb.dtype)

    y_buf = lax.map(expert_block, (x_buf, blk_expert)).reshape(P, d)
    y_s = (y_buf[dest].astype(jnp.float32) * w_s[:, None]).astype(h.dtype)
    out = jnp.zeros((T, d), h.dtype).at[tok_s].add(y_s)
    return out.reshape(bsz, length, d)

def second_inputs(seed: int = 0) -> dict:
    key = jax.random.key(seed)
    ks = jax.random.split(key, 24)
    f32 = jnp.float32
    nrm = lambda k, shape, scale: jax.random.normal(k, shape, f32) * scale
    dt = jnp.exp(jax.random.uniform(ks[7], (DEPTH, GD_HEADS), f32, math.log(1e-3), math.log(1e-1)))
    return {
        'x': nrm(ks[0], (BATCH, SEQ, D_MODEL), 1.0),
        'meta_tokens': nrm(ks[1], (N_META, D_MODEL), 1.0),
        'hg_lb_logits': nrm(ks[2], (DEPTH + 1, HG_WIDTH), 0.5),
        'norm_mix_g': 1.0 + nrm(ks[3], (DEPTH, D_MODEL), 0.01),
        'w_in': nrm(ks[4], (DEPTH, D_MODEL, D_PROJ), D_MODEL ** -0.5),
        'gd_conv_w': nrm(ks[5], (DEPTH, CONV_W, 2 * GD_HEADS * GD_DK + GD_HEADS * GD_DV), CONV_W ** -0.5),
        'gd_A_log': jnp.log(jax.random.uniform(ks[6], (DEPTH, GD_HEADS), f32, 1.0, 16.0)),
        'gd_dt_bias': dt + jnp.log(-jnp.expm1(-dt)),
        'hg_norm_g': 1.0 + nrm(ks[8], (DEPTH, HG_DIM), 0.01),
        'gd_norm_g': 1.0 + nrm(ks[9], (DEPTH, GD_DV), 0.01),
        'hg_up': nrm(ks[10], (DEPTH, HG_WIDTH, D_MODEL), HG_WIDTH ** -0.5),
        'gd_up': nrm(ks[11], (DEPTH, GD_HEADS * GD_DV, D_MODEL), (GD_HEADS * GD_DV) ** -0.5),
        'w_out': nrm(ks[12], (DEPTH, D_MODEL, D_MODEL), D_MODEL ** -0.5),
        'norm_ffn_g': 1.0 + nrm(ks[13], (DEPTH, D_MODEL), 0.01),
        'router_group_w': nrm(ks[14], (DEPTH, D_MODEL, N_GROUPS), D_MODEL ** -0.5),
        'router_group_b': nrm(ks[15], (DEPTH, N_GROUPS), 0.01),
        'router_expert_w': nrm(ks[16], (DEPTH, D_MODEL, N_EXPERTS), D_MODEL ** -0.5),
        'router_expert_b': nrm(ks[17], (DEPTH, N_EXPERTS), 0.01),
        'w_gate': nrm(ks[18], (DEPTH, N_EXPERTS, D_MODEL, D_FF_EXPERT), D_MODEL ** -0.5),
        'w_up': nrm(ks[19], (DEPTH, N_EXPERTS, D_MODEL, D_FF_EXPERT), D_MODEL ** -0.5),
        'w_down': nrm(ks[20], (DEPTH, N_EXPERTS, D_FF_EXPERT, D_MODEL), D_FF_EXPERT ** -0.5),
        'final_norm_g': 1.0 + nrm(ks[21], (D_MODEL,), 0.01),
    }

def second_block(x, meta_tokens, hg_lb_logits, norm_mix_g, w_in, gd_conv_w, gd_A_log, gd_dt_bias,
              hg_norm_g, gd_norm_g, hg_up, gd_up, w_out, norm_ffn_g, router_group_w, router_group_b,
              router_expert_w, router_expert_b, w_gate, w_up, w_down, final_norm_g):
    bsz = x.shape[0]
    meta = jnp.broadcast_to(meta_tokens[None].astype(x.dtype), (bsz, N_META, x.shape[-1]))
    h = jnp.concatenate([meta, x], axis=1)
    lb_table = jnp.cumsum(jax.nn.softmax(hg_lb_logits.astype(jnp.float32), axis=0), axis=0)
    for l in range(DEPTH):
        h = h + token_mixer(rmsnorm_2(h, norm_mix_g[l]), lb_table[l], w_in[l], gd_conv_w[l], gd_A_log[l],
                            gd_dt_bias[l], hg_norm_g[l], gd_norm_g[l], hg_up[l], gd_up[l], w_out[l])
        h = h + hierarchical_moe(rmsnorm_2(h, norm_ffn_g[l]), router_group_w[l], router_group_b[l],
                                 router_expert_w[l], router_expert_b[l], w_gate[l], w_up[l], w_down[l])
    h = rmsnorm_2(h, final_norm_g)
    return h[:, N_META:]


def setup_inputs(seed=0):
    out = dict(first_inputs(seed))
    for name, value in second_inputs(seed + 1).items():
        if name != "x":
            out[name + "_2"] = value
    return out


def reference(
    x, norm_mix_g, w_in, conv_a_w, conv_b_w, conv_b_b, ln_b_g, ln_b_b, w_out, norm_ffn_g,
    w_gate, w_up, conv_ffn_w, w_down, norm_final_g, meta_tokens_2, hg_lb_logits_2, norm_mix_g_2,
    w_in_2, gd_conv_w_2, gd_A_log_2, gd_dt_bias_2, hg_norm_g_2, gd_norm_g_2, hg_up_2, gd_up_2,
    w_out_2, norm_ffn_g_2, router_group_w_2, router_group_b_2, router_expert_w_2,
    router_expert_b_2, w_gate_2, w_up_2, w_down_2, final_norm_g_2,
):
    x = first_block(
        x, norm_mix_g, w_in, conv_a_w, conv_b_w, conv_b_b, ln_b_g, ln_b_b, w_out, norm_ffn_g,
        w_gate, w_up, conv_ffn_w, w_down, norm_final_g,
    )
    return second_block(
        x, meta_tokens_2, hg_lb_logits_2, norm_mix_g_2, w_in_2, gd_conv_w_2, gd_A_log_2,
        gd_dt_bias_2, hg_norm_g_2, gd_norm_g_2, hg_up_2, gd_up_2, w_out_2, norm_ffn_g_2,
        router_group_w_2, router_group_b_2, router_expert_w_2, router_expert_b_2, w_gate_2,
        w_up_2, w_down_2, final_norm_g_2,
    )


_drawn_inputs = setup_inputs


def setup_inputs(seed=0):
    import zlib

    import numpy as np

    out = dict(_drawn_inputs(seed))
    spreads = {}
    factors = {'ln_b_b': 2.946,
     'norm_mix_g_2': 3.013,
     'hg_norm_g_2': 17.985,
     'gd_norm_g_2': 15.189,
     'norm_ffn_g_2': 7.686,
     'router_group_b_2': 10.187,
     'router_expert_b_2': 9.733,
     'final_norm_g_2': 32.279}
    for name, (base, spread) in spreads.items():
        noise = np.random.default_rng([zlib.crc32(name.encode()), seed]).standard_normal(out[name].shape)
        drawn = base * np.exp(spread * noise) if base else spread * noise
        out[name] = jnp.asarray(drawn.astype(out[name].dtype))
    for name, factor in factors.items():
        out[name] = (out[name] * factor).astype(out[name].dtype)
    return out
```

```python
import numpy as np
import concourse.bass as bass
from concourse import mybir
from contextlib import ExitStack

FP32 = mybir.dt.float32
I32 = mybir.dt.int32
ALU = mybir.AluOpType
ACT = mybir.ActivationFunctionType
AX = mybir.AxisListType

P = 128
D = 1024
KD = D // P
SEQ = 1024
HALF = 512
DFF = 2816
NF = DFF // P
EPS_RMS = 1e-6
EPS_LN = 1e-5


class Pack:
    pass


def semaphores(nc, K, *names):
    got = [nc.alloc_semaphore(name=n) for n in names]
    K.sems.extend(got)
    return got


def retire_semaphores(nc, K):
    nc.clear_and_free_semaphores(K.sems)
    nc.all_engine_barrier()
    K.sems = []


def pair(ps, slot):
    return ps[:, 2 * slot:2 * slot + 2, :].rearrange("p b n -> p (b n)")


def project(pe, ps, bank0, w, src, nk, groups, lo=0):
    for g, n in enumerate(groups):
        at = lo + sum(groups[:g])
        for k in range(nk):
            last = pe.matmul(ps[:, bank0 + g, 0:n], w[:, k, :], src[:, k, at:at + n],
                             start=(k == 0), stop=(k == nk - 1))
    return last



PARAM_ROWS = [
    [("conv_b_w", 124), ("conv_b_b", 4)],
    [("conv_ffn_w", 66), ("conv_a_w", 12), ("norm_mix_g", 8), ("norm_ffn_g", 8), ("norm_final_g", 8),
     ("norm_mix_g_2", 8), ("ln_b_g", 4), ("ln_b_b", 4), ("hg_norm_g_2", 1), ("gd_norm_g_2", 1),
     ("hg_lb_logits_2", 8)],
    [("gd_conv_w_2", 48), ("norm_ffn_g_2", 8)],
]


def stage_constants(nc, K):
    with ExitStack() as ctx:
        rows_in, zeroed, made, turned, out_of = semaphores(
            nc, K, "par_rows_in", "par_zeroed", "const_made", "par_turned", "par_out")
        rows = ctx.enter_context(nc.sbuf_tensor("par_rows", [P, len(PARAM_ROWS), P], FP32))
        n_in = sum(len(g) for g in PARAM_ROWS)
        with nc.Block(no_gpsimd_drain=True) as block:

            @block.sync
            def _(sync):
                sync.wait_ge(zeroed, 1)
                at = 0
                for t, group in enumerate(PARAM_ROWS):
                    r = 0
                    for name, n in group:
                        K.col[name] = at + r
                        src = K.dram[name]
                        flat = src.rearrange(" a b c -> (a b c)") if len(src.shape) == 3 else (
                            src.rearrange("a b -> (a b)") if len(src.shape) == 2 else src)
                        sync.dma_start(rows[r:r + n, t, :], flat.rearrange("(r c) -> r c", c=P)).then_inc(rows_in, 16)
                        r += n
                    at += P

            @block.gpsimd
            def _(gp):
                gp.memset(rows[:], 0.0).then_inc(zeroed, 1)
                gp.memset(K.ones[:], 1.0)
                gp.memset(K.eps_rms[:], EPS_RMS)
                gp.memset(K.eps_ln[:], EPS_LN)
                gp.memset(K.ident[:], 0.0).then_inc(made, 1)
                gp.memset(K.upper[:], 1.0).then_inc(made, 1)
                gp.memset(K.level[:], 0.0).then_inc(made, 1)
                gp.memset(K.chunk_keep[:], 1.0).then_inc(made, 1)
                gp.wait_ge(made, 4)
                gp.memset(K.chunk_keep[:].rearrange("p (c t) -> p c t", t=P)[:, :, 0:1], 0.0)
                gp.affine_select(out=K.ident[:], in_=K.ident[:], compare_op=ALU.not_equal, fill=1.0,
                                 base=0, pattern=[[-1, P]], channel_multiplier=1).then_inc(made, 1)
                gp.affine_select(out=K.upper[:], in_=K.upper[:], compare_op=ALU.is_ge, fill=0.0,
                                 base=0, pattern=[[1, P]], channel_multiplier=-1).then_inc(made, 1)
                n = 6
                for lev in range(1, 8):
                    m = 1 << lev
                    right = K.level[:, lev, :].rearrange("p (b h i) -> p b h i", h=2, i=m // 2)[:, :, 1, :]
                    gp.memset(right, 1.0).then_inc(made, 1)
                    n += 1
                    gp.wait_ge(made, n)
                    gp.affine_select(out=right, in_=right, compare_op=ALU.is_ge, fill=0.0, base=0,
                                     pattern=[[-m, P // m], [0, m // 2]], channel_multiplier=1).then_inc(made, 1)
                    n += 1
                    gp.wait_ge(made, n)
                    gp.affine_select(out=right, in_=right, compare_op=ALU.is_ge, fill=0.0, base=m // 2 - 1,
                                     pattern=[[m, P // m], [0, m // 2]], channel_multiplier=-1).then_inc(made, 1)
                    n += 1
                gp.wait_ge(made, n)
                gp.tensor_copy(K.level[:, 0, :], K.ident[:]).then_inc(made, 1)
                gp.wait_ge(made, n + 1)

            @block.tensor
            def _(pe):
                pe.wait_ge(made, 5)
                pe.wait_ge(rows_in, 16 * n_in)
                for t in range(len(PARAM_ROWS)):
                    last = pe.transpose(K.ps[:, t, 0:P], rows[:, t, :], K.ident[:])
                last.then_inc(turned, 1)

            @block.scalar
            def _(act):
                act.wait_ge(turned, 1)
                for t in range(len(PARAM_ROWS)):
                    act.activation(K.par[:, t * P:(t + 1) * P], K.ps[:, t, 0:P], ACT.Copy).then_inc(out_of, 1)


def param(K, name, i=0):
    c = K.col[name] + i
    return K.par[:, bass.ds(c, 1)]



def stage_load_x(nc, K):
    n_tok = SEQ // P
    with ExitStack() as ctx:
        loaded, turned, freed = semaphores(nc, K, "x_loaded", "x_turned", "x_turned_out")
        rows = ctx.enter_context(nc.sbuf_tensor("x_rows", [P, n_tok, D], FP32))
        with nc.Block(no_gpsimd_drain=True) as block:

            @block.sync
            def _(sync):
                for t in range(n_tok):
                    sync.dma_start(rows[:, t, :], K.dram["x"][0, t * P:(t + 1) * P, :]).then_inc(loaded, 16)
                sync.wait_ge(loaded, 16 * n_tok)

            @block.tensor
            def _(pe):
                pe.wait_ge(loaded, 16 * n_tok)
                for k in range(KD):
                    for g in range(2):
                        n = 2 * k + g
                        if n >= 8:
                            pe.wait_ge(freed, n - 7)
                        for t in range(4):
                            last = pe.transpose(K.ps[:, n % 8, t * P:(t + 1) * P],
                                                rows[:, 4 * g + t, k * P:(k + 1) * P], K.ident[:])
                        last.then_inc(turned, 1)

            @block.scalar
            def _(act):
                for n in range(2 * KD):
                    act.wait_ge(turned, n + 1)
                    act.activation(K.xT[:, n // 2, (n % 2) * HALF:(n % 2 + 1) * HALF], K.ps[:, n % 8, :],
                                   ACT.Copy).then_inc(freed, 1)


def stage_rmsnorm(nc, K, tag, gain, parts, width=D):
    nk = width // P
    with ExitStack() as ctx:
        squared, summed, rooted, inverted, scaled = semaphores(
            nc, K, f"{tag}_nrm_squared", f"{tag}_nrm_summed", f"{tag}_nrm_rooted", f"{tag}_nrm_inverted", f"{tag}_nrm_scaled")
        sq = ctx.enter_context(nc.sbuf_tensor(f"{tag}_nrm_sq", [P, 4, HALF], FP32))
        root = ctx.enter_context(nc.sbuf_tensor(f"{tag}_nrm_root", [P, len(parts), HALF], FP32))
        inv = ctx.enter_context(nc.sbuf_tensor(f"{tag}_nrm_inv", [P, len(parts), HALF], FP32))
        with nc.Block(no_gpsimd_drain=True) as block:

            @block.scalar
            def _(act):
                for g, (s, s_at, _, _, n) in enumerate(parts):
                    for k in range(nk):
                        m = g * nk + k
                        if m >= 4:
                            act.wait_ge(summed, m - 3)
                        act.activation(sq[:, m % 4, 0:n], s[:, k, s_at:s_at + n], ACT.Square).then_inc(squared, 1)
                for g, (_, _, _, _, n) in enumerate(parts):
                    act.wait_ge(summed, (g + 1) * nk)
                    act.activation(root[:, g, 0:n], K.ps[:, g, 0:n], ACT.Sqrt, bias=K.eps_rms[:, 0:1],
                                   scale=1.0 / width).then_inc(rooted, 1)

            @block.tensor
            def _(pe):
                for g, (_, _, _, _, n) in enumerate(parts):
                    for k in range(nk):
                        m = g * nk + k
                        pe.wait_ge(squared, m + 1)
                        pe.matmul(K.ps[:, g, 0:n], K.ones[:], sq[:, m % 4, 0:n], start=(k == 0),
                                  stop=(k == nk - 1)).then_inc(summed, 1)

            @block.vector
            def _(dve):
                for g, (s, s_at, d, d_at, n) in enumerate(parts):
                    dve.wait_ge(rooted, g + 1)
                    dve.reciprocal(inv[:, g, 0:n], root[:, g, 0:n]).then_inc(inverted, 1)
                    dve.wait_ge(inverted, g + 1)
                    for k in range(nk):
                        dve.scalar_tensor_tensor(out=d[:, k, d_at:d_at + n], in0=s[:, k, s_at:s_at + n],
                                                 scalar=param(K, gain, k), in1=inv[:, g, 0:n],
                                                 op0=ALU.mult, op1=ALU.mult).then_inc(scaled, 1)


def halves(src, dst):
    return [(src, h * HALF, dst, h * HALF, HALF) for h in range(2)]


def stage_mixer(nc, K, hT, y):
    TAPS = 31
    PAD = TAPS // 2
    with ExitStack() as ctx:
        wl = semaphores(nc, K, *[f"mx_w_in{q}" for q in range(4)])
        done = semaphores(nc, K, *[f"mx_done{q}" for q in range(4)])
        free = semaphores(nc, K, *[f"mx_free{q}" for q in range(4)])
        padded, step = semaphores(nc, K, "mx_padded", "mx_step")
        w = ctx.enter_context(nc.sbuf_tensor("mx_w", [P, 4, KD, P], FP32))
        sg = ctx.enter_context(nc.sbuf_tensor("mx_sg", [P, 2, SEQ], FP32))
        u = ctx.enter_context(nc.sbuf_tensor("mx_u", [P, 4, SEQ + 2 * PAD], FP32))
        ca = ctx.enter_context(nc.sbuf_tensor("mx_ca", [P, 2, SEQ], FP32))
        w_v = K.dram["w_in"][0].rearrange("(k p) e -> p k e", p=P)
        GATED = (12, 16)
        SHORT = (0, 8, 4)
        with nc.Block(no_gpsimd_drain=True) as block:

            @block.sync
            def _(sync):
                with sync.Fori(0, 2) as it:
                    for q in range(4):
                        sync.wait_ge(done[q], it + 1)
                        sync.dma_start(w[:, q, :, :], w_v[:, :, bass.ds((GATED[q % 2] + q // 2) * P + it * (2 * P), P)]
                                       ).then_inc(wl[q], 16)
                with sync.Fori(0, 4) as i:
                    for q in range(3):
                        sync.wait_ge(done[q], i + 3)
                        sync.dma_start(w[:, q, :, :], w_v[:, :, bass.ds(SHORT[q] * P + i * P, P)]).then_inc(wl[q], 16)

            @block.gpsimd
            def _(gp):
                gp.memset(u[:, :, 0:PAD], 0.0)
                gp.memset(u[:, :, PAD + SEQ:], 0.0).then_inc(padded, 1)

            @block.tensor
            def _(pe):
                for q in range(4):
                    pe.sem_inc(done[q], 1)
                with pe.Fori(0, 2) as it:
                    for q in range(4):
                        pe.wait_ge(wl[q], 16 * it + 16)
                        pe.wait_ge(free[q], it + 1)
                        project(pe, K.ps, 2 * q, w[:, q], hT, KD, [HALF, HALF]).then_inc(done[q], 1)
                with pe.Fori(0, 4) as i:
                    for q in range(3):
                        pe.wait_ge(wl[q], 16 * i + 48)
                        pe.wait_ge(free[q], i + 3)
                        project(pe, K.ps, 2 * q, w[:, q], hT, KD, [HALF, HALF]).then_inc(done[q], 1)

            @block.scalar
            def _(act):
                with act.Fori(0, 2) as it:
                    for v in range(2):
                        act.wait_ge(done[2 * v + 1], it + 2)
                        act.wait_ge(free[2 * v], it + 1)
                        act.activation(sg[:, v, :], pair(K.ps, 2 * v + 1), ACT.Sigmoid).then_inc(free[2 * v + 1], 1)
                with act.Fori(0, 4) as i:
                    act.wait_ge(done[0], i + 4)
                    act.wait_ge(free[1], i + 3)
                    act.activation(sg[:, 0, :], pair(K.ps, 0), ACT.Copy).then_inc(free[0], 1)

            @block.vector
            def _(dve):
                for q in range(4):
                    dve.sem_inc(free[q], 1)
                dve.wait_ge(padded, 1)
                with dve.Fori(0, 2) as it:
                    for v in range(2):
                        dve.wait_ge(done[2 * v], it + 2)
                        dve.wait_ge(free[2 * v + 1], it + 2)
                        dve.tensor_tensor(u[:, bass.ds(2 * it + v, 1), PAD:PAD + SEQ], pair(K.ps, 2 * v), sg[:, v, :],
                                          ALU.mult).then_inc(free[2 * v], 1)
                        dve.wait_ge(free[2 * v], it + 2)
                        acc = y[:, bass.ds(4 + v + 2 * it, 1), :]
                        for k in range(TAPS):
                            src = u[:, bass.ds(2 * it + v, 1), k:k + SEQ]
                            tap = K.par[:, bass.ds(K.col["conv_b_w"] + 4 * k + v + 2 * it, 1)]
                            if k == 0:
                                bias = K.par[:, bass.ds(K.col["conv_b_b"] + v + 2 * it, 1)]
                                dve.tensor_scalar(acc, src, tap, bias, ALU.mult, ALU.add).then_inc(step, 1)
                            else:
                                dve.scalar_tensor_tensor(out=acc, in0=src, scalar=tap, in1=acc, op0=ALU.mult,
                                                         op1=ALU.add).then_inc(step, 1)
                            dve.wait_ge(step, (2 * it + v) * TAPS + k + 1)
                with dve.Fori(0, 4) as i:
                    n0 = 4 * TAPS
                    dve.wait_ge(done[1], i + 4)
                    dve.wait_ge(free[0], i + 4)
                    dve.tensor_tensor(ca[:, 0, :], pair(K.ps, 1), sg[:, 0, :], ALU.mult).then_inc(free[1], 1)
                    dve.wait_ge(free[1], i + 4)
                    conv3(dve, K, ca[:, 1, :], ca[:, 0, :], "conv_a_w", 4, i, step, n0 + 3 * i)
                    dve.wait_ge(done[2], i + 4)
                    dve.tensor_tensor(y[:, bass.ds(i, 1), :], pair(K.ps, 2), ca[:, 1, :], ALU.mult).then_inc(free[2], 1)
                dve.wait_ge(free[2], 7)


def conv3(dve, K, out, src, name, tiles, i, step, at):
    n = SEQ

    def tap(k):
        return K.par[:, bass.ds(K.col[name] + tiles * k + i, 1)]
    dve.tensor_scalar(out, src, tap(1), None, ALU.mult).then_inc(step, 1)
    dve.wait_ge(step, at + 1)
    dve.scalar_tensor_tensor(out=out[:, 1:n], in0=src[:, 0:n - 1], scalar=tap(0), in1=out[:, 1:n],
                             op0=ALU.mult, op1=ALU.add).then_inc(step, 1)
    dve.wait_ge(step, at + 2)
    dve.scalar_tensor_tensor(out=out[:, 0:n - 1], in0=src[:, 1:n], scalar=tap(2), in1=out[:, 0:n - 1],
                             op0=ALU.mult, op1=ALU.add).then_inc(step, 1)
    dve.wait_ge(step, at + 3)


def stage_layernorm_silu(nc, K, yb):
    NT = 4
    W = NT * P
    with ExitStack() as ctx:
        summed, meaned, centred, squared, ssummed, rooted, inverted, normed, out = semaphores(
            nc, K, "ln_summed", "ln_meaned", "ln_centred", "ln_squared", "ln_ssummed", "ln_rooted",
            "ln_inverted", "ln_normed", "ln_out")
        mu = ctx.enter_context(nc.sbuf_tensor("ln_mu", [P, 2, HALF], FP32))
        sq = ctx.enter_context(nc.sbuf_tensor("ln_sq", [P, 2, NT, HALF], FP32))
        inv = ctx.enter_context(nc.sbuf_tensor("ln_inv", [P, 2, 2, HALF], FP32))
        part = [[yb[:, i, h * HALF:(h + 1) * HALF] for i in range(NT)] for h in range(2)]
        with nc.Block(no_gpsimd_drain=True) as block:

            @block.tensor
            def _(pe):
                for h in range(2):
                    for i in range(NT):
                        last = pe.matmul(K.ps[:, h, :], K.ones[:], part[h][i], start=(i == 0), stop=(i == NT - 1))
                    last.then_inc(summed, 1)
                for h in range(2):
                    for i in range(NT):
                        pe.wait_ge(squared, h * NT + i + 1)
                        last = pe.matmul(K.ps[:, 2 + h, :], K.ones[:], sq[:, h, i, :], start=(i == 0),
                                         stop=(i == NT - 1))
                    last.then_inc(ssummed, 1)

            @block.scalar
            def _(act):
                for h in range(2):
                    for i in range(NT):
                        act.wait_ge(centred, h * NT + i + 1)
                        act.activation(sq[:, h, i, :], part[h][i], ACT.Square).then_inc(squared, 1)
                for h in range(2):
                    act.wait_ge(ssummed, h + 1)
                    act.activation(inv[:, h, 0, :], K.ps[:, 2 + h, :], ACT.Sqrt, bias=K.eps_ln[:, 0:1],
                                   scale=1.0 / W).then_inc(rooted, 1)
                for h in range(2):
                    for i in range(NT):
                        act.wait_ge(normed, h * NT + i + 1)
                        act.activation(part[h][i], part[h][i], ACT.Silu, bias=param(K, "ln_b_b", i),
                                       scale=param(K, "ln_b_g", i)).then_inc(out, 1)

            @block.vector
            def _(dve):
                for h in range(2):
                    dve.wait_ge(summed, h + 1)
                    dve.tensor_scalar(mu[:, h, :], K.ps[:, h, :], 1.0 / W, None, ALU.mult).then_inc(meaned, 1)
                    dve.wait_ge(meaned, h + 1)
                    for i in range(NT):
                        dve.tensor_tensor(part[h][i], part[h][i], mu[:, h, :], ALU.subtract).then_inc(centred, 1)
                for h in range(2):
                    dve.wait_ge(rooted, h + 1)
                    dve.reciprocal(inv[:, h, 1, :], inv[:, h, 0, :]).then_inc(inverted, 1)
                    dve.wait_ge(inverted, h + 1)
                    dve.wait_ge(squared, (h + 1) * NT)
                    for i in range(NT):
                        dve.tensor_tensor(part[h][i], part[h][i], inv[:, h, 1, :], ALU.mult).then_inc(normed, 1)


def stage_residual(nc, K, tag, src, w_dram, nk):
    with ExitStack() as ctx:
        wl = semaphores(nc, K, *[f"{tag}_w_in{q}" for q in range(2)])
        done = semaphores(nc, K, *[f"{tag}_done{q}" for q in range(2)])
        free = semaphores(nc, K, *[f"{tag}_free{q}" for q in range(2)])
        w = ctx.enter_context(nc.sbuf_tensor(f"{tag}_w", [P, 2, nk, P], FP32))
        w_v = w_dram.rearrange("(k p) e -> p k e", p=P)
        with nc.Block(no_gpsimd_drain=True) as block:

            @block.sync
            def _(sync):
                with sync.Fori(0, KD // 2) as it:
                    for q in range(2):
                        sync.wait_ge(done[q], it + 1)
                        sync.dma_start(w[:, q, :, :], w_v[:, :, bass.ds(q * P + it * (2 * P), P)]).then_inc(wl[q], 16)

            @block.tensor
            def _(pe):
                for q in range(2):
                    pe.sem_inc(done[q], 1)
                with pe.Fori(0, KD // 2) as it:
                    for q in range(2):
                        pe.wait_ge(wl[q], 16 * it + 16)
                        pe.wait_ge(free[q], it + 1)
                        project(pe, K.ps, 2 * q, w[:, q], src, nk, [HALF, HALF]).then_inc(done[q], 1)

            @block.vector
            def _(dve):
                for q in range(2):
                    dve.sem_inc(free[q], 1)
                with dve.Fori(0, KD // 2) as it:
                    for q in range(2):
                        dve.wait_ge(done[q], it + 2)
                        x = K.xT[:, bass.ds(2 * it + q, 1), :]
                        dve.tensor_tensor(x, pair(K.ps, q), x, ALU.add).then_inc(free[q], 1)


def stage_ffn(nc, K, hT, p):
    with ExitStack() as ctx:
        wl = semaphores(nc, K, *[f"ff_w_in{q}" for q in range(4)])
        done = semaphores(nc, K, *[f"ff_done{q}" for q in range(4)])
        free = semaphores(nc, K, *[f"ff_free{q}" for q in range(4)])
        step, silu, zeroed, y_filled = semaphores(nc, K, "ff_step", "ff_silu", "ff_zeroed", "ff_y_filled")
        zero = ctx.enter_context(nc.sbuf_tensor("ff_zero", [P, D], FP32))
        w = ctx.enter_context(nc.sbuf_tensor("ff_w", [P, 4, KD, P], FP32))
        g = ctx.enter_context(nc.sbuf_tensor("ff_g", [P, 2, SEQ], FP32))
        w_v = [K.dram[n][0].rearrange("(k p) e -> p k e", p=P) for n in ("w_gate", "w_up")]
        with nc.Block(no_gpsimd_drain=True) as block:

            @block.sync
            def _(sync):
                with sync.Fori(0, NF // 2) as it:
                    for q in range(4):
                        sync.wait_ge(done[q], it + 1)
                        sync.dma_start(w[:, q, :, :], w_v[q % 2][:, :, bass.ds(q // 2 * P + it * (2 * P), P)]
                                       ).then_inc(wl[q], 16)

            @block.tensor
            def _(pe):
                for q in range(4):
                    pe.sem_inc(done[q], 1)
                with pe.Fori(0, NF // 2) as it:
                    for q in range(4):
                        pe.wait_ge(wl[q], 16 * it + 16)
                        pe.wait_ge(free[q], it + 1)
                        project(pe, K.ps, 2 * q, w[:, q], hT, KD, [HALF, HALF]).then_inc(done[q], 1)

            @block.gpsimd
            def _(gp):
                gp.memset(zero[:], 0.0).then_inc(zeroed, 1)
                gp.wait_ge(zeroed, 1)
                gp.dma_start(K.scr["y"].rearrange("(j p) d -> p j d", p=P),
                             zero[:].rearrange("p (a d) -> p a d", a=1).to_broadcast([P, N_BLOCK, D])).then_inc(y_filled, 16)
                gp.wait_ge(y_filled, 16)

            @block.scalar
            def _(act):
                with act.Fori(0, NF // 2) as it:
                    for v in range(2):
                        act.wait_ge(free[2 * v], it + 2)
                        act.activation(g[:, v, :], g[:, v, :], ACT.Silu).then_inc(silu, 1)

            @block.vector
            def _(dve):
                for q in range(4):
                    dve.sem_inc(free[q], 1)
                with dve.Fori(0, NF // 2) as it:
                    for v in range(2):
                        dve.wait_ge(done[2 * v], it + 2)
                        conv3(dve, K, g[:, v, :], pair(K.ps, 2 * v), "conv_ffn_w", NF, 2 * it + v, step,
                              6 * it + 3 * v)
                        dve.sem_inc(free[2 * v], 1)
                    for v in range(2):
                        dve.wait_ge(done[2 * v + 1], it + 2)
                        dve.wait_ge(silu, 2 * it + v + 1)
                        dve.tensor_tensor(p[:, bass.ds(2 * it + v, 1), :], pair(K.ps, 2 * v + 1), g[:, v, :],
                                          ALU.mult).then_inc(free[2 * v + 1], 1)
                    dve.wait_ge(free[3], it + 2)
                    dve.wait_ge(free[1], it + 2)


def common(nc, ctx, K):
    def sb(name, shape, dt=FP32):
        return ctx.enter_context(nc.sbuf_tensor(name, shape, dt))
    K.col = {}
    K.sems = []
    K.ps = ctx.enter_context(nc.psum_tensor("ps", [P, 8, HALF], FP32))
    K.ones = sb("ones", [P, P])
    K.ident = sb("ident", [P, P])
    K.upper = sb("upper", [P, P])
    K.level = sb("level", [P, 8, P])
    K.eps_rms = sb("eps_rms", [P, 1])
    K.eps_ln = sb("eps_ln", [P, 1])
    K.chunk_keep = sb("chunk_keep", [P, 9 * P])
    K.par = sb("par", [P, len(PARAM_ROWS) * P])
    K.xT = sb("xT", [P, KD, SEQ])


def first_block(nc, K):
    stage_load_x(nc, K)
    with ExitStack() as ctx:
        hT = ctx.enter_context(nc.sbuf_tensor("hT", [P, KD, SEQ], FP32))
        with ExitStack() as inner:
            y = inner.enter_context(nc.sbuf_tensor("y", [P, KD, SEQ], FP32))
            stage_rmsnorm(nc, K, "n1", "norm_mix_g", halves(K.xT, hT))
            stage_mixer(nc, K, hT, y)
            stage_layernorm_silu(nc, K, y[:, 4:8, :])
            stage_residual(nc, K, "wo", y, K.dram["w_out"][0], KD)
        stage_rmsnorm(nc, K, "n2", "norm_ffn_g", halves(K.xT, hT))
        p = ctx.enter_context(nc.sbuf_tensor("p", [P, NF, SEQ], FP32))
        stage_ffn(nc, K, hT, p)
        stage_residual(nc, K, "wd", p, K.dram["w_down"][0], NF)
    stage_rmsnorm(nc, K, "n3", "norm_final_g", halves(K.xT, K.xT))



META = 16
N_CHUNK = 1 + SEQ // P
LEN = N_CHUNK * P
LEAD = P - META
HEADS = 4
HW = HEADS * P
COL = dict(hq=0, hf=512, hi=1024, hg=1536, gq=2048, gk=2560, gv=3072, gz=3584, beta=4096, pre_ga=4104, pre_gb=5128)
QUART = (META + SEQ) // 4


def stage_meta(nc, K, metaT):
    with ExitStack() as ctx:
        loaded, turned, out = semaphores(nc, K, "meta_loaded", "meta_turned", "meta_out")
        rows = ctx.enter_context(nc.sbuf_tensor("meta_rows", [META, D], FP32))
        with nc.Block(no_gpsimd_drain=True) as block:

            @block.sync
            def _(sync):
                sync.dma_start(rows[:], K.dram["meta_tokens_2"]).then_inc(loaded, 16)

            @block.tensor
            def _(pe):
                pe.wait_ge(loaded, 16)
                for k in range(KD):
                    last = pe.transpose(K.ps[:, 0, k * META:(k + 1) * META], rows[:, k * P:(k + 1) * P],
                                        K.ident[0:META, 0:META])
                last.then_inc(turned, 1)

            @block.scalar
            def _(act):
                act.wait_ge(turned, 1)
                act.activation(metaT[:].rearrange("p k t -> p (k t)"), K.ps[:, 0, 0:KD * META], ACT.Copy).then_inc(out, 1)


def stage_lower_bounds(nc, K, lb):
    with ExitStack() as ctx:
        step, exped = semaphores(nc, K, "lb_step", "lb_exped")
        t = ctx.enter_context(nc.sbuf_tensor("lb_t", [P, 6, HEADS], FP32))
        c = K.col["hg_lb_logits_2"]
        with nc.Block(no_gpsimd_drain=True) as block:

            @block.vector
            def _(dve):
                row = [K.par[:, c + 4 * r:c + 4 * r + 4] for r in range(2)]
                dve.tensor_tensor(t[:, 0, :], row[0], row[1], ALU.max).then_inc(step, 1)
                dve.wait_ge(step, 1)
                dve.tensor_tensor(t[:, 1, :], row[0], t[:, 0, :], ALU.subtract)
                dve.tensor_tensor(t[:, 2, :], row[1], t[:, 0, :], ALU.subtract).then_inc(step, 1)
                dve.wait_ge(exped, 1)
                dve.tensor_tensor(t[:, 5, :], t[:, 3, :], t[:, 4, :], ALU.add).then_inc(step, 1)
                dve.wait_ge(step, 3)
                dve.reciprocal(t[:, 0, :], t[:, 5, :]).then_inc(step, 1)
                dve.wait_ge(step, 4)
                dve.tensor_tensor(lb[:, 0:4], t[:, 3, :], t[:, 0, :], ALU.mult).then_inc(step, 1)
                dve.wait_ge(step, 5)
                dve.tensor_scalar(lb[:, 4:8], lb[:, 0:4], -1.0, 1.0, ALU.mult, ALU.add)

            @block.scalar
            def _(act):
                act.wait_ge(step, 2)
                act.activation(t[:, 3:5, :], t[:, 1:3, :], ACT.Exp).then_inc(exped, 1)


def stage_forget(nc, K, hT, lb):
    with ExitStack() as ctx:
        wl = semaphores(nc, K, "fg_w_in0", "fg_w_in1")
        done = semaphores(nc, K, "fg_done0", "fg_done1")
        free = semaphores(nc, K, "fg_free0", "fg_free1")
        padded, zero_out, forget, keyed, logged, summed, stored = semaphores(
            nc, K, "fg_padded", "fg_zero_out", "fg_forget", "fg_keyed", "fg_logged", "fg_summed", "fg_stored")
        w = ctx.enter_context(nc.sbuf_tensor("fg_w", [P, 2, KD, P], FP32))
        f = ctx.enter_context(nc.sbuf_tensor("fg_f", [P, 2, LEN - LEAD], FP32))
        k_st = ctx.enter_context(nc.sbuf_tensor("fg_k", [P, 2, LEN], FP32))
        b_st = ctx.enter_context(nc.sbuf_tensor("fg_b", [P, 2, LEN], FP32))
        lf = ctx.enter_context(nc.sbuf_tensor("fg_lf", [P, 2, LEN], FP32))
        zero = ctx.enter_context(nc.sbuf_tensor("fg_zero", [P, P], FP32))
        w_v = K.dram["w_in_2"][0].rearrange("(k p) e -> p k e", p=P)
        with nc.Block(no_gpsimd_drain=True) as block:

            @block.sync
            def _(sync):
                with sync.Fori(0, 2) as it:
                    for q in range(2):
                        sync.wait_ge(done[q], it + 1)
                        sync.dma_start(w[:, q, :, :], w_v[:, :, bass.ds(COL["hf"] + q * P + it * (2 * P), P)]
                                       ).then_inc(wl[q], 16)

            @block.tensor
            def _(pe):
                for q in range(2):
                    pe.sem_inc(done[q], 1)
                with pe.Fori(0, 2) as it:
                    for q in range(2):
                        pe.wait_ge(wl[q], 16 * it + 16)
                        pe.wait_ge(free[q], it + 1)
                        project(pe, K.ps, 4 * q, w[:, q], hT, KD, [QUART] * 4, LEAD).then_inc(done[q], 1)

            @block.scalar
            def _(act):
                for q in range(2):
                    act.sem_inc(free[q], 1)
                act.sem_inc(stored, 64)
                act.wait_ge(padded, 1)
                with act.Fori(0, 2) as it:
                    for q in range(2):
                        act.wait_ge(done[q], it + 2)
                        act.activation(f[:, q, :].rearrange("p (b n) -> p b n", b=4),
                                       K.ps[:, 4 * q:4 * q + 4, 0:QUART], ACT.Sigmoid).then_inc(free[q], 1)
                    for q in range(2):
                        act.wait_ge(forget, 2 * it + q + 1)
                        act.activation(lf[:, q, LEAD:], f[:, q, :], ACT.Ln).then_inc(logged, 1)
                    for q in range(2):
                        rows = bass.ds(q * P + it * (2 * P), P)
                        act.wait_ge(keyed, 2 * it + q + 1)
                        act.dma_start(K.scr["k_a"][rows, :], k_st[:, q, :]).then_inc(stored, 16)
                    for q in range(2):
                        rows = bass.ds(q * P + it * (2 * P), P)
                        act.wait_ge(summed, 2 * it + q + 1)
                        act.dma_start(K.scr["b_a"][rows, :], b_st[:, q, :]).then_inc(stored, 16)
                act.wait_ge(stored, 3 * 64)

            @block.vector
            def _(dve):
                with dve.Fori(0, 2) as it:
                    for q in range(2):
                        dve.wait_ge(free[q], it + 2)
                        i = 2 * it + q
                        dve.tensor_scalar(f[:, q, :], f[:, q, :], lb[:, bass.ds(i + 4, 1)], lb[:, bass.ds(i, 1)],
                                          ALU.mult, ALU.add).then_inc(forget, 1)
                        dve.wait_ge(forget, 2 * it + q + 1)
                        dve.wait_ge(stored, 64 * it + 64)
                        dve.tensor_scalar(k_st[:, q, LEAD:], f[:, q, :], -1.0, 1.0, ALU.mult, ALU.add).then_inc(keyed, 1)
                    for q in range(2):
                        dve.wait_ge(logged, 2 * it + q + 1)
                        dve.tensor_tensor_scan(b_st[:, q, :], K.chunk_keep[:], lf[:, q, :], 0.0, ALU.mult,
                                               ALU.add).then_inc(summed, 1)
                    dve.wait_ge(summed, 2 * it + 2)

            @block.gpsimd
            def _(gp):
                gp.memset(zero[:], 0.0)
                gp.memset(k_st[:, :, 0:LEAD], 0.0)
                gp.memset(lf[:, :, 0:LEAD], 0.0).then_inc(padded, 1)
                gp.wait_ge(padded, 1)
                for i in range(HEADS):
                    gp.dma_start(K.scr["q_a"][i * P:(i + 1) * P, 0:P], zero[:]).then_inc(zero_out, 16)
                gp.wait_ge(zero_out, 16 * HEADS)


def stage_by_tokens(nc, K, hT, G, beta):
    with ExitStack() as ctx:
        wl, sl, done, out, stored, gated, step, acted = semaphores(
            nc, K, "bt_w_in", "bt_small_in", "bt_done", "bt_out", "bt_stored", "bt_gated", "bt_step", "bt_acted")
        w = ctx.enter_context(nc.sbuf_tensor("bt_w", [P, KD, HW], FP32))
        wg = ctx.enter_context(nc.sbuf_tensor("bt_wg", [P, KD, 2 * HEADS], FP32))
        st = ctx.enter_context(nc.sbuf_tensor("bt_st", [P, 4, HW], FP32))
        a_log = ctx.enter_context(nc.sbuf_tensor("bt_a_log", [P, HEADS], FP32))
        dt = ctx.enter_context(nc.sbuf_tensor("bt_dt", [P, HEADS], FP32))
        t = ctx.enter_context(nc.sbuf_tensor("bt_t", [P, 6, N_CHUNK, HEADS], FP32))
        w_v = K.dram["w_in_2"][0].rearrange("(k p) e -> p k e", p=P)

        def over_chunks(x):
            return x[:].rearrange("p (a h) -> p a h", a=1).to_broadcast([P, N_CHUNK, HEADS])
        with nc.Block(no_gpsimd_drain=True) as block:

            @block.sync
            def _(sync):
                sync.dma_start(w[:], w_v[:, :, COL["hi"]:COL["hi"] + HW]).then_inc(wl, 16)
                sync.dma_start(wg[:], w_v[:, :, COL["beta"]:COL["beta"] + 2 * HEADS]).then_inc(sl, 16)
                sync.dma_start(a_log[:], K.dram["gd_A_log_2"].to_broadcast([P, HEADS])).then_inc(sl, 16)
                sync.dma_start(dt[:], K.dram["gd_dt_bias_2"].to_broadcast([P, HEADS])).then_inc(sl, 16)

            @block.tensor
            def _(pe):
                pe.wait_ge(wl, 16)
                for c in range(N_CHUNK):
                    if c >= 6:
                        pe.wait_ge(out, c - 5)
                    for k in range(KD):
                        last = pe.matmul(K.ps[:, c % 6, :], hT[:, k, c * P:(c + 1) * P], w[:, k, :],
                                         start=(k == 0), stop=(k == KD - 1))
                    last.then_inc(done, 1)
                pe.wait_ge(sl, 48)
                for c in range(N_CHUNK):
                    for k in range(KD):
                        last = pe.matmul(K.ps[:, 7, 8 * c:8 * c + 8], hT[:, k, c * P:(c + 1) * P], wg[:, k, :],
                                         start=(k == 0), stop=(k == KD - 1))
                last.then_inc(gated, 1)
                pe.wait_ge(step, 5)
                pe.matmul(K.ps[:, 6, 0:N_CHUNK * HEADS], K.upper[:], t[:, 5, :, :].rearrange("p c h -> p (c h)"),
                          start=True, stop=True).then_inc(gated, 1)

            @block.scalar
            def _(act):
                for c in range(N_CHUNK):
                    act.wait_ge(done, c + 1)
                    if c >= 4:
                        act.wait_ge(stored, 16 * (c - 3))
                    act.activation(st[:, c % 4, :], K.ps[:, c % 6, :], ACT.Copy).then_inc(out, 1)
                act.wait_ge(gated, 1)
                view = K.ps[:, 7, 0:8 * N_CHUNK].rearrange("p (c j) -> p c j", j=8)
                act.wait_ge(step, 1)
                act.activation(beta[:], view[:, :, 0:HEADS], ACT.Sigmoid).then_inc(acted, 1)
                act.wait_ge(step, 2)
                act.activation(t[:, 2, :, :], t[:, 1, :, :], ACT.Exp).then_inc(acted, 1)
                act.activation(a_log[:], a_log[:], ACT.Exp).then_inc(acted, 1)
                act.wait_ge(acted, 3)
                act.activation(t[:, 3, :, :], t[:, 2, :, :], ACT.Ln, bias=K.ones[:, 0:1]).then_inc(acted, 1)
                act.wait_ge(gated, 2)
                act.activation(G[:].rearrange("p c h -> p (c h)"), K.ps[:, 6, 0:N_CHUNK * HEADS], ACT.Copy).then_inc(acted, 1)

            @block.vector
            def _(dve):
                dve.wait_ge(gated, 1)
                view = K.ps[:, 7, 0:8 * N_CHUNK].rearrange("p (c j) -> p c j", j=8)
                dve.tensor_tensor(t[:, 0, :, :], view[:, :, HEADS:], over_chunks(dt), ALU.add).then_inc(step, 1)
                dve.wait_ge(step, 1)
                dve.scalar_tensor_tensor(out=t[:, 1, :, :], in0=t[:, 0, :, :], scalar=-1.0, in1=t[:, 0, :, :],
                                         op0=ALU.mult, op1=ALU.min).then_inc(step, 1)
                dve.wait_ge(acted, 4)
                dve.scalar_tensor_tensor(out=t[:, 4, :, :], in0=t[:, 0, :, :], scalar=0.0, in1=t[:, 3, :, :],
                                         op0=ALU.max, op1=ALU.add).then_inc(step, 1)
                dve.wait_ge(step, 3)
                dve.scalar_tensor_tensor(out=t[:, 5, :, :], in0=t[:, 4, :, :], scalar=-1.0, in1=over_chunks(a_log),
                                         op0=ALU.mult, op1=ALU.mult).then_inc(step, 2)

            @block.gpsimd
            def _(gp):
                for c in range(N_CHUNK):
                    gp.wait_ge(out, c + 1)
                    gp.dma_start(K.scr["v_a"][c * P:(c + 1) * P, :], st[:, c % 4, :]).then_inc(stored, 16)
                    gp.wait_ge(stored, 16 * (c + 1))


def stage_conv_qkv(nc, K, hT):
    TAPS = 4
    N = META + SEQ
    tiles = [(name, i) for name in ("gq", "gk", "gv") for i in range(HEADS)]
    scale = {"gq": P ** -0.5, "gk": 1.0}
    with ExitStack() as ctx:
        wl, done, copied, conved, silued, squared, norm_done, rooted, inverted, ready, ready_v, stored, step, padded = semaphores(
            nc, K, "cv_w_in", "cv_done", "cv_copied", "cv_conved", "cv_silued", "cv_squared", "cv_norm_done",
            "cv_rooted", "cv_inverted", "cv_ready", "cv_ready_v", "cv_stored", "cv_step", "cv_padded")
        w = ctx.enter_context(nc.sbuf_tensor("cv_w", [P, 2, KD, P], FP32))
        cin = ctx.enter_context(nc.sbuf_tensor("cv_in", [P, 2, N + TAPS - 1], FP32))
        cv = ctx.enter_context(nc.sbuf_tensor("cv_cv", [P, 2, N], FP32))
        sq = ctx.enter_context(nc.sbuf_tensor("cv_sq", [P, 2, N], FP32))
        inv = ctx.enter_context(nc.sbuf_tensor("cv_inv", [P, N], FP32))
        st = ctx.enter_context(nc.sbuf_tensor("cv_st", [P, 2, LEN], FP32))
        w_v = K.dram["w_in_2"][0].rearrange("(k p) e -> p k e", p=P)
        n_norm = 2 * HEADS

        def banks(x, q):
            return x[:, 4 * q:4 * q + 4, 0:QUART]

        def quarters(x):
            return x.rearrange("p (b n) -> p b n", b=4)
        with nc.Block(no_gpsimd_drain=True) as block:

            @block.sync
            def _(sync):
                for n, (name, i) in enumerate(tiles):
                    if n >= 2:
                        sync.wait_ge(done, n - 1)
                    at = COL[name] + i * P
                    sync.dma_start(w[:, n % 2, :, :], w_v[:, :, at:at + P]).then_inc(wl, 16)
                    sync.wait_ge(wl, 16 * (n + 1))

            @block.tensor
            def _(pe):
                for n in range(len(tiles) + 1):
                    if n < len(tiles):
                        pe.wait_ge(wl, 16 * (n + 1))
                        if n >= 2:
                            if n - 2 < n_norm:
                                pe.wait_ge(rooted, n - 1)
                            else:
                                pe.wait_ge(copied, n - 1)
                        project(pe, K.ps, 4 * (n % 2), w[:, n % 2], hT, KD, [QUART] * 4, LEAD).then_inc(done, 1)
                    m = n - 1
                    if 0 <= m < n_norm:
                        pe.wait_ge(squared, m + 1)
                        for b in range(4):
                            last = pe.matmul(K.ps[:, 4 * (m % 2) + b, 0:QUART], K.ones[:],
                                             sq[:, m % 2, b * QUART:(b + 1) * QUART], start=True, stop=True)
                        last.then_inc(norm_done, 1)

            @block.scalar
            def _(act):
                act.wait_ge(padded, 1)
                for n in range(len(tiles) + 1):
                    if n < len(tiles):
                        act.wait_ge(done, n + 1)
                        if n >= 2:
                            act.wait_ge(conved, n - 1)
                        act.activation(quarters(cin[:, n % 2, TAPS - 1:]), banks(K.ps, n % 2), ACT.Copy).then_inc(copied, 1)
                    m = n - 1
                    if 0 <= m < n_norm:
                        act.wait_ge(norm_done, m + 1)
                        act.activation(quarters(sq[:, m % 2, :]), banks(K.ps, m % 2), ACT.Sqrt,
                                       bias=K.eps_rms[:, 0:1]).then_inc(rooted, 1)
                    if n < len(tiles):
                        act.wait_ge(conved, n + 1)
                        if n < n_norm:
                            act.activation(cv[:, n % 2, :], cv[:, n % 2, :], ACT.Silu).then_inc(silued, 1)
                            act.wait_ge(silued, n + 1)
                            if n >= 2:
                                act.wait_ge(inverted, n - 1)
                            act.activation(sq[:, n % 2, :], cv[:, n % 2, :], ACT.Square).then_inc(squared, 1)
                        else:
                            act.wait_ge(stored, 16 * (n - 1))
                            act.activation(st[:, n % 2, LEAD:], cv[:, n % 2, :], ACT.Silu).then_inc(ready_v, 1)

            @block.vector
            def _(dve):
                for n in range(len(tiles) + 1):
                    if n < len(tiles):
                        name, i = tiles[n]
                        c = 4 * ("gq", "gk", "gv").index(name) + i
                        dve.wait_ge(copied, n + 1)
                        if n >= 2:
                            if n - 2 < n_norm:
                                dve.wait_ge(ready, n - 1)
                            else:
                                dve.wait_ge(ready_v, n - 1 - n_norm)
                        for k in range(TAPS):
                            src = cin[:, n % 2, k:k + N]
                            tap = param(K, "gd_conv_w_2", 12 * k + c)
                            if k == 0:
                                ins = dve.tensor_scalar(cv[:, n % 2, :], src, tap, None, ALU.mult)
                            else:
                                ins = dve.scalar_tensor_tensor(out=cv[:, n % 2, :], in0=src, scalar=tap,
                                                               in1=cv[:, n % 2, :], op0=ALU.mult, op1=ALU.add)
                            if k < TAPS - 1:
                                ins.then_inc(step, 1)
                                dve.wait_ge(step, (TAPS - 1) * n + k + 1)
                            else:
                                ins.then_inc(conved, 1)
                    m = n - 1
                    if 0 <= m < n_norm:
                        dve.wait_ge(rooted, m + 1)
                        dve.reciprocal(inv[:], sq[:, m % 2, :]).then_inc(inverted, 1)
                        dve.wait_ge(inverted, m + 1)
                        if m >= 2:
                            dve.wait_ge(stored, 16 * (m - 1))
                        dve.scalar_tensor_tensor(out=st[:, m % 2, LEAD:], in0=cv[:, m % 2, :], scalar=scale[tiles[m][0]],
                                                 in1=inv[:], op0=ALU.mult, op1=ALU.mult).then_inc(ready, 1)

            @block.gpsimd
            def _(gp):
                gp.memset(cin[:, :, 0:TAPS - 1], 0.0)
                gp.memset(st[:, :, 0:LEAD], 0.0).then_inc(padded, 1)
                gp.wait_ge(padded, 1)
                for n, (name, i) in enumerate(tiles):
                    if n < n_norm:
                        gp.wait_ge(ready, n + 1)
                    else:
                        gp.wait_ge(ready_v, n + 1 - n_norm)
                    gp.dma_start(K.scr[name][i * P:(i + 1) * P, :], st[:, n % 2, :]).then_inc(stored, 16)
                    gp.wait_ge(stored, 16 * (n + 1))


def stage_gates(nc, K, hT):
    groups = [("hq", 4, ACT.Silu, K.scr["q_a"][:, P:]), ("hg", 4, ACT.Silu, K.scr["gate"][0:HW, :]),
              ("gz", 4, ACT.Silu, K.scr["gate"][HW:, :]), ("pre_ga", 8, ACT.Sigmoid, K.scr["merge_a"]),
              ("pre_gb", 8, ACT.Sigmoid, K.scr["merge_b"])]
    with ExitStack() as ctx:
        wl = semaphores(nc, K, *[f"ga_w_in{q}" for q in range(4)])
        done = semaphores(nc, K, *[f"ga_done{q}" for q in range(4)])
        free = semaphores(nc, K, *[f"ga_free{q}" for q in range(4)])
        stored = semaphores(nc, K, *[f"ga_stored{q}" for q in range(4)])
        w = ctx.enter_context(nc.sbuf_tensor("ga_w", [P, 4, KD, P], FP32))
        st = ctx.enter_context(nc.sbuf_tensor("ga_st", [P, 4, SEQ], FP32))
        w_v = K.dram["w_in_2"][0].rearrange("(k p) e -> p k e", p=P)

        def turns(eng, body):
            base = 0
            for g in groups:
                if g[1] == 4:
                    body(g, 0, base)
                else:
                    with eng.Fori(0, g[1] // 4) as it:
                        body(g, it, it + base)
                base += g[1] // 4
        total = sum(g[1] // 4 for g in groups)
        with nc.Block(no_gpsimd_drain=True) as block:

            @block.sync
            def _(sync):
                def body(g, it, n):
                    for q in range(4):
                        sync.wait_ge(done[q], n + 1)
                        sync.dma_start(w[:, q, :, :], w_v[:, :, bass.ds(it * (4 * P) + (COL[g[0]] + q * P), P)]
                                       ).then_inc(wl[q], 16)
                turns(sync, body)

            @block.tensor
            def _(pe):
                for q in range(4):
                    pe.sem_inc(done[q], 1)

                def body(g, it, n):
                    for q in range(4):
                        pe.wait_ge(wl[q], n * 16 + 16)
                        pe.wait_ge(free[q], n + 1)
                        project(pe, K.ps, 2 * q, w[:, q], hT, KD, [HALF, HALF], P).then_inc(done[q], 1)
                turns(pe, body)

            @block.scalar
            def _(act):
                for q in range(4):
                    act.sem_inc(free[q], 1)
                    act.sem_inc(stored[q], 16)

                def body(g, it, n):
                    for q in range(4):
                        act.wait_ge(done[q], n + 2)
                        act.wait_ge(stored[q], n * 16 + 16)
                        act.activation(st[:, q, :], pair(K.ps, q), g[2]).then_inc(free[q], 1)
                        act.wait_ge(free[q], n + 2)
                        act.dma_start(g[3][bass.ds(it * (4 * P) + q * P, P), :], st[:, q, :]).then_inc(stored[q], 16)
                turns(act, body)
                for q in range(4):
                    act.wait_ge(stored[q], 16 * (total + 1))


def second_projections(nc, K, G, beta):
    with ExitStack() as ctx:
        metaT = ctx.enter_context(nc.sbuf_tensor("metaT", [P, KD, META], FP32))
        lb = ctx.enter_context(nc.sbuf_tensor("lb", [P, 2 * HEADS], FP32))
        hT = ctx.enter_context(nc.sbuf_tensor("hT2", [P, KD, LEN], FP32))
        zeroed, = semaphores(nc, K, "lead_zeroed")
        stage_meta(nc, K, metaT)
        with nc.Block(no_gpsimd_drain=True) as block:

            @block.gpsimd
            def _(gp):
                gp.memset(hT[:, :, 0:LEAD], 0.0).then_inc(zeroed, 1)
        stage_rmsnorm(nc, K, "n4", "norm_mix_g_2", [(metaT, 0, hT, LEAD, META), (K.xT, 0, hT, P, HALF),
                                                    (K.xT, HALF, hT, P + HALF, HALF)])
        stage_lower_bounds(nc, K, lb)
        stage_forget(nc, K, hT, lb)
        stage_by_tokens(nc, K, hT, G, beta)
        stage_conv_qkv(nc, K, hT)
        stage_gates(nc, K, hT)


def scratch(nc):
    shapes = dict(q_a=(HW, LEN), k_a=(HW, LEN), b_a=(HW, LEN), v_a=(LEN, HW), gq=(HW, LEN), gk=(HW, LEN), gv=(HW, LEN),
                  gate=(2 * HW, SEQ), merge_a=(D, SEQ), merge_b=(D, SEQ))
    scr = {n: nc.dram_tensor(f"scr_{n}", s, FP32, kind="Internal").ap() for n, s in shapes.items()}
    scr["h2"] = nc.dram_tensor("scr_h2", (SEQ, D), FP32, kind="Internal").ap()
    scr["y"] = nc.dram_tensor("scr_y", (N_BLOCK * P, D), FP32, kind="Internal").ap()
    scr["row_table"] = nc.dram_tensor("scr_row_table", (N_BLOCK * P, 1), I32, kind="Internal").ap()
    return scr



LEVELS = 7

EVENTS = dict(
    in_g=48, in_a=48, in_v=16,
    bc_ready=1, kq_ready=7, m_ready=7, added=7, qeb_ready=1, kdt_ready=1,
    eg_ready=1, rt_exp=1, ege_ready=1, eb_ready=1, e_ready=7, edb_ready=1, kd_ready=1, kda_ready=1,
    pm_ready=6, rs_ready=1, us_ready=1, og_out=1, oa_out=1,
    kb_ready=1, rt_ready=1, vb_ready=1, nk_ready=1, qe_ready=1, rt_masked=1, lt_ready=1, at_ready=1,
    d_ready=7, dbe_ready=1, masked=8, xy=7, sg_ready=1, sa_ready=1,
    bcast_done=1, kk_done=1, kq_done=1, lev_done=8, m1t_done=1, p_done=6, dxy_done=6, kdat_done=1,
    r_done=1, u_done=1, o_done=1, dsg_done=1, oa_done=1, dsa_done=1)
MAKER = dict(sync="in_g in_a in_v", gpsimd="bc_ready kq_ready m_ready added qeb_ready kdt_ready",
             scalar="eg_ready rt_exp ege_ready eb_ready e_ready edb_ready kd_ready kda_ready pm_ready rs_ready us_ready og_out oa_out",
             vector="kb_ready rt_ready vb_ready nk_ready qe_ready rt_masked lt_ready at_ready d_ready dbe_ready masked xy sg_ready sa_ready",
             tensor="bcast_done kk_done kq_done lev_done m1t_done p_done dxy_done kdat_done r_done u_done o_done dsg_done oa_done dsa_done")


def stage_recurrences(nc, K, G, beta, oT):
    C4 = [P, HEADS, P]
    with ExitStack() as ctx:
        ev = {n: semaphores(nc, K, f"rc_{n}")[0] for n in EVENTS}

        def buf(name, n=0):
            shape = [P, n, HEADS, P] if n else C4
            return ctx.enter_context(nc.sbuf_tensor(f"rc_{name}", shape, FP32))

        q_a, k_a, b_a, v_a, q_g, k_g, v_g = [buf(n) for n in ("q_a", "k_a", "b_a", "v_a", "q_g", "k_g", "v_g")]
        Gb, Bb, eG, kb, nkbe, vb, qe = [buf(n) for n in ("Gb", "Bb", "eG", "kb", "nkbe", "vb", "qe")]
        rT, LT, aT, kd, Rs, us, Pm, X, Y = [buf(n) for n in ("rT", "LT", "aT", "kd", "Rs", "us", "Pm", "X", "Y")]
        M = buf("M", LEVELS)
        KQ = buf("KQ", LEVELS)
        Dl = buf("D", 2)
        El = buf("E", 2)
        edb, eb, qeb, kdT, kda, A = [buf(n) for n in ("edb", "eb", "qeb", "kdT", "kda", "A")]
        tmp = buf("tmp", 2)
        Sa, Sg = buf("Sa"), buf("Sg")
        ge = ctx.enter_context(nc.sbuf_tensor("rc_ge", [P, 2, HEADS], FP32))
        s_zero, = semaphores(nc, K, "rc_state_zero")

        def bank(n):
            return K.ps[:, n, :].rearrange("p (h t) -> p h t", h=HEADS)

        def all_heads(m):
            return m.rearrange("p (a t) -> p a t", a=1).to_broadcast(C4)

        def column(x, c):
            return x[:, bass.ds(c, 1), :].rearrange("p a (h b) -> p (a h) b", b=1).to_broadcast(C4)

        def halves_of(x, lev):
            m = 1 << lev
            v = x.rearrange("p h t -> p (h t)").rearrange("p (b s i) -> p b s i", s=2, i=m // 2)
            return v[:, :, 0, :], v[:, :, 1, :]

        def middle(x, lev):
            m = 1 << lev
            v = x.rearrange("p h t -> p (h t)").rearrange("p (b i) -> p b i", i=m)[:, :, m // 2 - 1:m // 2]
            return v.to_broadcast([P, HEADS * P // m, m // 2])

        def start(eng, kind):
            for n in MAKER[kind].split():
                eng.sem_inc(ev[n], EVENTS[n])

        def wait(eng, c, name, k=None):
            per = EVENTS[name]
            eng.wait_ge(ev[name], c * per + per + (per if k is None else k))

        def wait_before(eng, c, *names):
            for name in names:
                eng.wait_ge(ev[name], c * EVENTS[name] + EVENTS[name])

        LAST = ("dsa_done", "sa_ready", "oa_out", "kdt_ready", "qeb_ready", "added")

        def over_chunks(eng, kind, body):
            start(eng, kind)
            with eng.Fori(0, N_CHUNK) as c:
                if kind != "sync":
                    wait_before(eng, c, *LAST)
                body(c)

        with nc.Block(no_gpsimd_drain=True) as block:

            @block.sync
            def _(sync):
                def by_channels(name, c):
                    return K.scr[name].rearrange("(h p) t -> p h t", p=P)[:, :, bass.ds(c * P, P)]

                def body(c):
                    wait_before(sync, c, "kq_done", "kb_ready", "vb_ready", "qe_ready")
                    for x, n in ((q_g, "gq"), (k_g, "gk"), (v_g, "gv")):
                        sync.dma_start(x[:], by_channels(n, c)).then_inc(ev["in_g"], 16)
                    wait_before(sync, c, "lev_done", "kq_ready", "dbe_ready", "d_ready", "qeb_ready", "kdt_ready", "eb_ready")
                    for x, n in ((q_a, "q_a"), (k_a, "k_a"), (b_a, "b_a")):
                        sync.dma_start(x[:], by_channels(n, c)).then_inc(ev["in_a"], 16)
                    wait_before(sync, c, "dsa_done")
                    sync.dma_start(v_a[:].rearrange("p h v -> p (h v)"), K.scr["v_a"][bass.ds(c * P, P), :]
                                   ).then_inc(ev["in_v"], 16)
                over_chunks(sync, "sync", body)

            @block.gpsimd
            def _(gp):
                gp.memset(Sa[:], 0.0)
                gp.memset(Sg[:], 0.0).then_inc(s_zero, 1)

                def body(c):
                    gp.tensor_copy(Gb[:], column(G, c))
                    gp.tensor_copy(Bb[:], column(beta, c)).then_inc(ev["bc_ready"], 1)

                    def kq(lev):
                        wait(gp, c, "e_ready", lev)
                        if lev == 1:
                            wait(gp, c, "in_a")
                        e = halves_of(El[:, lev % 2], lev)
                        for half, src in ((0, k_a), (1, q_a)):
                            ins = gp.tensor_tensor(halves_of(KQ[:, lev - 1], lev)[half], halves_of(src[:], lev)[half],
                                                   e[half], ALU.mult)
                        ins.then_inc(ev["kq_ready"], 1)

                    def m_level(lev):
                        if lev == 1:
                            wait(gp, c, "lt_ready")
                        gp.tensor_tensor(M[:, lev - 1], LT[:], all_heads(K.level[:, lev, :]), ALU.mult
                                         ).then_inc(ev["m_ready"], 1)

                    def add(lev):
                        wait(gp, c, "masked", lev + 1)
                        if lev > 1:
                            wait(gp, c, "added", lev - 1)
                        gp.tensor_tensor(A[:], A[:], tmp[:, lev % 2], ALU.add).then_inc(ev["added"], 1)

                    kq(1)
                    kq(2)
                    m_level(1)
                    m_level(2)
                    for lev in range(3, LEVELS + 1):
                        kq(lev)
                        add(lev - 2)
                        m_level(lev)
                    wait(gp, c, "eb_ready")
                    gp.tensor_tensor(qeb[:], q_a[:], eb[:], ALU.mult).then_inc(ev["qeb_ready"], 1)
                    wait(gp, c, "edb_ready")
                    gp.tensor_tensor(kdT[:], k_a[:], edb[:], ALU.mult).then_inc(ev["kdt_ready"], 1)
                    add(LEVELS - 1)
                    add(LEVELS)
                over_chunks(gp, "gpsimd", body)

            @block.scalar
            def _(act):
                def body(c):
                    def exp_level(lev):
                        wait(act, c, "d_ready", lev)
                        if lev > 2:
                            wait(act, c, "kq_ready", lev - 2)
                        act.activation(El[:, lev % 2], Dl[:, lev % 2], ACT.Exp).then_inc(ev["e_ready"], 1)

                    wait(act, c, "bcast_done")
                    act.activation(eG[:], bank(0), ACT.Exp).then_inc(ev["eg_ready"], 1)
                    wait(act, c, "rt_ready")
                    act.activation(rT[:], rT[:], ACT.Exp).then_inc(ev["rt_exp"], 1)
                    act.activation(ge[:, 1, :], ge[:, 0, :], ACT.Exp).then_inc(ev["ege_ready"], 1)
                    exp_level(1)
                    exp_level(2)
                    wait(act, c, "kq_done")
                    wait(act, c, "ege_ready")
                    for h in range(HEADS):
                        ins = act.activation(kd[:, h, :], bank(4)[:, h, :], ACT.Copy, scale=ge[:, 1, h:h + 1])
                    ins.then_inc(ev["kd_ready"], 1)
                    wait(act, c, "in_a")
                    act.activation(eb[:], b_a[:], ACT.Exp).then_inc(ev["eb_ready"], 1)
                    exp_level(3)
                    wait(act, c, "r_done")
                    act.activation(Rs[:], bank(2), ACT.Copy).then_inc(ev["rs_ready"], 1)
                    for lev in range(2, LEVELS + 1):
                        wait(act, c, "p_done", lev - 1)
                        if lev > 2:
                            wait(act, c, "dxy_done", lev - 2)
                        act.activation(Pm[:], bank(5), ACT.Copy).then_inc(ev["pm_ready"], 1)
                        if lev + 2 <= LEVELS:
                            exp_level(lev + 2)
                        if lev == 5:
                            wait(act, c, "dbe_ready")
                            act.activation(edb[:], edb[:], ACT.Exp, scale=-1.0).then_inc(ev["edb_ready"], 1)
                    wait(act, c, "kdat_done")
                    act.activation(kda[:], bank(0), ACT.Copy).then_inc(ev["kda_ready"], 1)
                    wait(act, c, "u_done")
                    act.activation(us[:], bank(3), ACT.Copy).then_inc(ev["us_ready"], 1)
                    wait(act, c, "o_done")
                    act.activation(oT[:, HEADS:, bass.ds(c * P, P)], bank(4), ACT.Copy).then_inc(ev["og_out"], 1)
                    wait(act, c, "oa_done")
                    act.activation(oT[:, 0:HEADS, bass.ds(c * P, P)], bank(1), ACT.Copy).then_inc(ev["oa_out"], 1)
                over_chunks(act, "scalar", body)

            @block.vector
            def _(dve):
                def body(c):
                    def exponents(lev):
                        if lev == 1:
                            wait(dve, c, "in_a")
                        if lev > 2:
                            wait(dve, c, "e_ready", lev - 2)
                        left, right = halves_of(Dl[:, lev % 2], lev)
                        b_left, b_right = halves_of(b_a[:], lev)
                        dve.tensor_tensor(left, middle(b_a[:], lev), b_left, ALU.subtract)
                        dve.tensor_tensor(right, b_right, middle(b_a[:], lev), ALU.subtract).then_inc(ev["d_ready"], 1)

                    def mask(lev):
                        wait(dve, c, "lev_done", lev + 1)
                        if lev > 2:
                            wait(dve, c, "added", lev - 2)
                        dst = A[:] if lev == 0 else tmp[:, lev % 2]
                        dve.tensor_tensor(dst, bank(lev % 2), all_heads(K.level[:, lev, :]), ALU.mult
                                          ).then_inc(ev["masked"], 1)

                    wait(dve, c, "eg_ready")
                    wait(dve, c, "in_g")
                    dve.tensor_tensor(kb[:], k_g[:], bank(1), ALU.mult).then_inc(ev["kb_ready"], 1)
                    for h in range(HEADS):
                        dve.tensor_scalar(rT[:, h, :], bank(0)[:, h, :],
                                          G[:, bass.ds(c, 1), h:h + 1].rearrange("p a b -> p (a b)"), 0.0,
                                          ALU.subtract, ALU.min)
                    dve.tensor_tensor(ge[:, 0, :], K.ps[:, 0, P - 1::P], G[:, bass.ds(c, 1), :].rearrange("p a h -> p (a h)"),
                                      ALU.subtract).then_inc(ev["rt_ready"], 1)
                    dve.tensor_tensor(vb[:], v_g[:], bank(1), ALU.mult).then_inc(ev["vb_ready"], 1)
                    wait(dve, c, "kb_ready")
                    dve.scalar_tensor_tensor(out=nkbe[:], in0=kb[:], scalar=-1.0, in1=eG[:], op0=ALU.mult,
                                             op1=ALU.mult).then_inc(ev["nk_ready"], 1)
                    dve.tensor_tensor(qe[:], q_g[:], eG[:], ALU.mult).then_inc(ev["qe_ready"], 1)
                    exponents(1)
                    exponents(2)
                    wait(dve, c, "rt_exp")
                    dve.tensor_tensor(rT[:], rT[:], all_heads(K.upper[:]), ALU.mult).then_inc(ev["rt_masked"], 1)
                    wait(dve, c, "kk_done")
                    wait(dve, c, "rt_masked")
                    dve.tensor_tensor(LT[:], bank(2), rT[:], ALU.mult).then_inc(ev["lt_ready"], 1)
                    wait(dve, c, "kq_done")
                    dve.tensor_tensor(aT[:], bank(3), rT[:], ALU.mult).then_inc(ev["at_ready"], 1)
                    mask(0)
                    mask(1)
                    exponents(3)
                    wait(dve, c, "m_ready", 1)
                    wait(dve, c, "m1t_done")
                    dve.tensor_tensor(Y[:], all_heads(K.ident[:]), M[:, 0], ALU.subtract)
                    dve.tensor_tensor(X[:], all_heads(K.ident[:]), bank(5), ALU.subtract).then_inc(ev["xy"], 1)
                    for lev in range(2, LEVELS + 1):
                        mask(lev)
                        if lev + 2 <= LEVELS:
                            exponents(lev + 2)
                        if lev == 4:
                            for h in range(HEADS):
                                ins = dve.tensor_scalar(edb[:, h, :], b_a[:, h, :], b_a[:, h, P - 1:P], None, ALU.subtract)
                            ins.then_inc(ev["dbe_ready"], 1)
                        wait(dve, c, "dxy_done", lev - 1)
                        wait(dve, c, "xy", lev - 1)
                        if lev < LEVELS:
                            dve.tensor_tensor(X[:], X[:], bank(6), ALU.subtract)
                        dve.tensor_tensor(Y[:], Y[:], bank(7), ALU.subtract).then_inc(ev["xy"], 1)
                    for name, S, e, b in (("g", Sg, eG, 5), ("a", Sa, eb, 0)):
                        wait(dve, c, f"ds{name}_done")
                        for h in range(HEADS):
                            ins = dve.scalar_tensor_tensor(out=S[:, h, :], in0=S[:, h, :], scalar=e[:, h, P - 1:P],
                                                           in1=bank(b)[:, h, :], op0=ALU.mult, op1=ALU.add)
                        ins.then_inc(ev[f"s{name}_ready"], 1)
                over_chunks(dve, "vector", body)

            @block.tensor
            def _(pe):
                ident = K.ident[:]

                def heads(b, *terms):
                    for h in range(HEADS):
                        for n, (lhsT, rhs) in enumerate(terms):
                            r = ident if rhs is None else rhs[:, h, :]
                            last = pe.matmul(bank(b)[:, h, :], lhsT[:, h, :], r, start=(n == 0), stop=(n == len(terms) - 1))
                    return last

                def turn(b, x):
                    for h in range(HEADS):
                        last = pe.transpose(bank(b)[:, h, :], x[:, h, :], ident)
                    return last

                def body(c):
                    def level(lev):
                        if lev == 0:
                            wait(pe, c, "in_a")
                            wait(pe, c, "rt_ready")
                            heads(0, (k_a, q_a)).then_inc(ev["lev_done"], 1)
                            return
                        if lev == 1:
                            wait(pe, c, "vb_ready")
                        else:
                            wait(pe, c, "masked", lev - 1)
                        wait(pe, c, "kq_ready", lev)
                        x = KQ[:, lev - 1]
                        heads(lev % 2, (x, x)).then_inc(ev["lev_done"], 1)

                    wait(pe, c, "bc_ready")
                    heads(0, (Gb, None))
                    heads(1, (Bb, None)).then_inc(ev["bcast_done"], 1)
                    wait(pe, c, "in_g")
                    wait(pe, c, "kb_ready")
                    heads(2, (k_g, kb)).then_inc(ev["kk_done"], 1)
                    heads(3, (k_g, q_g))
                    turn(4, k_g).then_inc(ev["kq_done"], 1)
                    level(0)
                    level(1)
                    wait(pe, c, "m_ready", 1)
                    turn(5, M[:, 0]).then_inc(ev["m1t_done"], 1)
                    wait(pe, c, "nk_ready")
                    wait(pe, c, "lt_ready")
                    heads(2, (vb, None), (nkbe, Sg)).then_inc(ev["r_done"], 1)
                    for lev in range(2, LEVELS + 1):
                        wait(pe, c, "xy", lev - 1)
                        wait(pe, c, "m_ready", lev)
                        heads(5, (M[:, lev - 1], X)).then_inc(ev["p_done"], 1)
                        level(lev)
                        wait(pe, c, "pm_ready", lev - 1)
                        if lev < LEVELS:
                            heads(6, (Y, Pm))
                        heads(7, (Pm, Y)).then_inc(ev["dxy_done"], 1)
                    wait(pe, c, "kdt_ready")
                    wait(pe, c, "masked", LEVELS)
                    turn(0, kdT).then_inc(ev["kdat_done"], 1)
                    wait(pe, c, "xy")
                    wait(pe, c, "rs_ready")
                    wait(pe, c, "at_ready")
                    heads(3, (Y, Rs)).then_inc(ev["u_done"], 1)
                    wait(pe, c, "qeb_ready")
                    wait(pe, c, "added")
                    wait(pe, c, "masked")
                    wait(pe, c, "in_v")
                    heads(1, (Sa, qeb), (v_a, A)).then_inc(ev["oa_done"], 1)
                    wait(pe, c, "us_ready")
                    wait(pe, c, "qe_ready")
                    wait(pe, c, "kd_ready")
                    heads(4, (Sg, qe), (us, aT)).then_inc(ev["o_done"], 1)
                    heads(5, (kd, us)).then_inc(ev["dsg_done"], 1)
                    wait(pe, c, "kda_ready")
                    heads(0, (kda, v_a)).then_inc(ev["dsa_done"], 1)
                pe.wait_ge(s_zero, 1)
                over_chunks(pe, "tensor", body)


def stage_head_norm(nc, K, oT):
    n_tiles = 2 * HEADS
    with ExitStack() as ctx:
        squared, summed, rooted, inverted, scaled, gated = semaphores(
            nc, K, "hn_squared", "hn_summed", "hn_rooted", "hn_inverted", "hn_scaled", "hn_gated")
        gate_in = semaphores(nc, K, *[f"hn_gate_in{i}" for i in range(n_tiles)])
        gate = ctx.enter_context(nc.sbuf_tensor("hn_gate", [P, n_tiles, SEQ], FP32))
        sq = ctx.enter_context(nc.sbuf_tensor("hn_sq", [P, 2, HALF], FP32))
        root = ctx.enter_context(nc.sbuf_tensor("hn_root", [P, 2, HALF], FP32))
        inv = ctx.enter_context(nc.sbuf_tensor("hn_inv", [P, 2, HALF], FP32))
        units = [(i, P + h * HALF) for i in range(n_tiles) for h in range(2)]
        with nc.Block(no_gpsimd_drain=True) as block:

            @block.sync
            def _(sync):
                for i in range(n_tiles):
                    sync.dma_start(gate[:, i, :], K.scr["gate"][i * P:(i + 1) * P, :]).then_inc(gate_in[i], 16)

            @block.scalar
            def _(act):
                for n in range(len(units) + 1):
                    if n < len(units):
                        i, at = units[n]
                        if n >= 2:
                            act.wait_ge(summed, n - 1)
                        act.activation(sq[:, n % 2, :], oT[:, i, at:at + HALF], ACT.Square).then_inc(squared, 1)
                    if n >= 1:
                        m = n - 1
                        act.wait_ge(summed, m + 1)
                        if m >= 2:
                            act.wait_ge(inverted, m - 1)
                        act.activation(root[:, m % 2, :], K.ps[:, m % 8, :], ACT.Sqrt, bias=K.eps_rms[:, 0:1],
                                       scale=1.0 / P).then_inc(rooted, 1)

            @block.tensor
            def _(pe):
                for n in range(len(units)):
                    pe.wait_ge(squared, n + 1)
                    if n >= 8:
                        pe.wait_ge(rooted, n - 7)
                    pe.matmul(K.ps[:, n % 8, :], K.ones[:], sq[:, n % 2, :], start=True, stop=True).then_inc(summed, 1)

            @block.vector
            def _(dve):
                for n, (i, at) in enumerate(units):
                    dve.wait_ge(rooted, n + 1)
                    if n >= 2:
                        dve.wait_ge(scaled, n - 1)
                    dve.reciprocal(inv[:, n % 2, :], root[:, n % 2, :]).then_inc(inverted, 1)
                    dve.wait_ge(inverted, n + 1)
                    dve.scalar_tensor_tensor(out=oT[:, i, at:at + HALF], in0=oT[:, i, at:at + HALF],
                                             scalar=param(K, "hg_norm_g_2" if i < HEADS else "gd_norm_g_2"),
                                             in1=inv[:, n % 2, :], op0=ALU.mult, op1=ALU.mult).then_inc(scaled, 1)

            @block.gpsimd
            def _(gp):
                for n, (i, at) in enumerate(units):
                    gp.wait_ge(gate_in[i], 16)
                    gp.wait_ge(scaled, n + 1)
                    gp.tensor_tensor(oT[:, i, at:at + HALF], oT[:, i, at:at + HALF], gate[:, i, at - P:at - P + HALF],
                                     ALU.mult).then_inc(gated, 1)
                gp.wait_ge(gated, len(units))


def stage_merge(nc, K, oT, mT):
    with ExitStack() as ctx:
        wl = semaphores(nc, K, *[f"mg_w_in{q}" for q in range(4)])
        gl = semaphores(nc, K, *[f"mg_gate_in{q}" for q in range(4)])
        done = semaphores(nc, K, *[f"mg_done{q}" for q in range(4)])
        free = semaphores(nc, K, *[f"mg_free{q}" for q in range(4)])
        merged, = semaphores(nc, K, "mg_merged")
        w = ctx.enter_context(nc.sbuf_tensor("mg_w", [P, 4, HEADS, P], FP32))
        g = ctx.enter_context(nc.sbuf_tensor("mg_g", [P, 4, SEQ], FP32))
        w_v = [K.dram[n][0].rearrange("(k p) e -> p k e", p=P) for n in ("hg_up_2", "gd_up_2")]
        g_v = [K.scr[n] for n in ("merge_a", "merge_b")]
        with nc.Block(no_gpsimd_drain=True) as block:

            @block.sync
            def _(sync):
                with sync.Fori(0, KD // 2) as it:
                    for q in range(4):
                        cols = bass.ds(q // 2 * P + it * (2 * P), P)
                        sync.wait_ge(done[q], it + 1)
                        sync.dma_start(w[:, q, :, :], w_v[q % 2][:, :, cols]).then_inc(wl[q], 16)
                        sync.wait_ge(merged, 2 * it + q // 2 + 1)
                        sync.dma_start(g[:, q, :], g_v[q % 2][cols, :]).then_inc(gl[q], 16)

            @block.tensor
            def _(pe):
                for q in range(4):
                    pe.sem_inc(done[q], 1)
                with pe.Fori(0, KD // 2) as it:
                    for q in range(4):
                        pe.wait_ge(wl[q], 16 * it + 16)
                        pe.wait_ge(free[q], it + 1)
                        side = q % 2
                        project(pe, K.ps, 2 * q, w[:, q], oT[:, side * HEADS:(side + 1) * HEADS, :], HEADS,
                                [HALF, HALF], P).then_inc(done[q], 1)

            @block.vector
            def _(dve):
                for q in range(4):
                    dve.sem_inc(free[q], 1)
                with dve.Fori(0, KD // 2) as it:
                    for q in range(4):
                        dve.wait_ge(done[q], it + 2)
                        dve.wait_ge(gl[q], 16 * it + 16)
                        dve.tensor_tensor(g[:, q, :], pair(K.ps, q), g[:, q, :], ALU.mult).then_inc(free[q], 1)
                    dve.wait_ge(free[3], it + 2)

            @block.gpsimd
            def _(gp):
                gp.sem_inc(merged, 2)
                with gp.Fori(0, KD // 2) as it:
                    for v in range(2):
                        gp.wait_ge(free[2 * v], it + 2)
                        gp.wait_ge(free[2 * v + 1], it + 2)
                        gp.tensor_tensor(mT[:, bass.ds(2 * it + v, 1), :], g[:, 2 * v, :].rearrange("p (a n) -> p a n", a=1),
                                         g[:, 2 * v + 1, :].rearrange("p (a n) -> p a n", a=1), ALU.add).then_inc(merged, 1)
                gp.wait_ge(merged, 2 + KD)



N_TILE = SEQ // P
N_GROUP = 4
N_EXPERT = 32
PER_GROUP = N_EXPERT // N_GROUP
N_LOGIT = N_GROUP + N_EXPERT
FE = 512
KE = FE // P
N_BLOCK = (2 * SEQ + N_EXPERT * (P - 1)) // P
N_BLOCK += N_BLOCK % 2
FAR = 1e30


def stage_to_tokens(nc, K, xt, L):
    with ExitStack() as ctx:
        turned, out, squared, inv_r, inv_i, normed, stored, in_, wscaled, logits, added = semaphores(
            nc, K, "tk_turned", "tk_out", "tk_squared", "tk_rooted", "tk_inverted", "tk_normed", "tk_stored", "tk_in",
            "tk_w_scaled", "tk_logits", "tk_added")
        gain = ctx.enter_context(nc.sbuf_tensor("tk_gain", [P, D], FP32))
        rw = ctx.enter_context(nc.sbuf_tensor("tk_rw", [P, KD, N_LOGIT], FP32))
        rb = ctx.enter_context(nc.sbuf_tensor("tk_rb", [P, N_LOGIT], FP32))
        junk = ctx.enter_context(nc.sbuf_tensor("tk_junk", [P, D], FP32))
        h = ctx.enter_context(nc.sbuf_tensor("tk_h", [P, 2, D], FP32))
        ss = ctx.enter_context(nc.sbuf_tensor("tk_ss", [P, 3, N_TILE], FP32))
        with nc.Block(no_gpsimd_drain=True) as block:

            @block.sync
            def _(sync):
                sync.dma_start(gain[:], K.dram["norm_ffn_g_2"].to_broadcast([P, D])).then_inc(in_, 16)
                sync.dma_start(rw[:, :, 0:N_GROUP], K.dram["router_group_w_2"][0].rearrange("(k p) e -> p k e", p=P)).then_inc(in_, 16)
                sync.dma_start(rw[:, :, N_GROUP:], K.dram["router_expert_w_2"][0].rearrange("(k p) e -> p k e", p=P)).then_inc(in_, 16)
                sync.dma_start(rb[:, 0:N_GROUP], K.dram["router_group_b_2"].to_broadcast([P, N_GROUP])).then_inc(in_, 16)
                sync.dma_start(rb[:, N_GROUP:], K.dram["router_expert_b_2"].to_broadcast([P, N_EXPERT])).then_inc(in_, 16)
                for t in range(N_TILE):
                    sync.wait_ge(normed, t + 1)
                    sync.dma_start(K.scr["h2"][t * P:(t + 1) * P, :], h[:, t % 2, :]).then_inc(stored, 16)
                    sync.wait_ge(stored, 16 * (t + 1))

            @block.tensor
            def _(pe):
                for n in range(2 * N_TILE):
                    t, g = n // 2, n % 2
                    if n >= 6:
                        pe.wait_ge(out, n - 5)
                    for k in range(4):
                        last = pe.transpose(K.ps[:, n % 6, k * P:(k + 1) * P], K.xT[:, 4 * g + k, t * P:(t + 1) * P], K.ident[:])
                    last.then_inc(turned, 1)
                pe.wait_ge(wscaled, 1)
                for t in range(N_TILE):
                    for k in range(KD):
                        last = pe.matmul(K.ps[:, 7, t * N_LOGIT:(t + 1) * N_LOGIT], K.xT[:, k, t * P:(t + 1) * P], rw[:, k, :],
                                         start=(k == 0), stop=(k == KD - 1))
                last.then_inc(logits, 1)

            @block.scalar
            def _(act):
                for n in range(2 * N_TILE):
                    t, g = n // 2, n % 2
                    act.wait_ge(turned, n + 1)
                    act.activation(xt[:, t, g * HALF:(g + 1) * HALF], K.ps[:, n % 6, :], ACT.Copy).then_inc(out, 1)
                for t in range(N_TILE):
                    act.wait_ge(out, 2 * (t + 1))
                    if t:
                        act.wait_ge(squared, t)
                    act.activation(junk[:], xt[:, t, :], ACT.Square, accum_out=ss[:, 0, t:t + 1]).then_inc(squared, 1)
                act.wait_ge(squared, N_TILE)
                act.activation(ss[:, 1, :], ss[:, 0, :], ACT.Sqrt, bias=K.eps_rms[:, 0:1], scale=1.0 / D).then_inc(inv_r, 1)

            @block.vector
            def _(dve):
                dve.wait_ge(in_, 16 * 5)
                for k in range(KD):
                    ins = dve.tensor_scalar(rw[:, k, :], rw[:, k, :], param(K, "norm_ffn_g_2", k), None, ALU.mult)
                ins.then_inc(wscaled, 1)
                dve.wait_ge(inv_r, 1)
                dve.reciprocal(ss[:, 2, :], ss[:, 1, :]).then_inc(inv_i, 1)
                dve.wait_ge(inv_i, 1)
                for t in range(N_TILE):
                    if t >= 2:
                        dve.wait_ge(stored, 16 * (t - 1))
                    dve.scalar_tensor_tensor(out=h[:, t % 2, :], in0=xt[:, t, :], scalar=ss[:, 2, t:t + 1], in1=gain[:],
                                             op0=ALU.mult, op1=ALU.mult).then_inc(normed, 1)
                dve.wait_ge(logits, 1)
                for t in range(N_TILE):
                    dve.scalar_tensor_tensor(out=L[:, t, :], in0=K.ps[:, 7, t * N_LOGIT:(t + 1) * N_LOGIT],
                                             scalar=ss[:, 2, t:t + 1], in1=rb[:], op0=ALU.mult, op1=ALU.add).then_inc(added, 1)
                dve.wait_ge(added, N_TILE)


def stage_route(nc, K, L, dest, weight, row_ids, experts):
    with ExitStack() as ctx:
        step, exped, ranked, filled, tok_made, scattered, tab_in, tab_f, turned = semaphores(
            nc, K, "rt_step", "rt_exped", "rt_ranked", "rt_filled", "rt_tok_made", "rt_scattered", "rt_tab_in", "rt_tab_f",
            "rt_turned")

        def sb(name, *shape, dt=FP32):
            return ctx.enter_context(nc.sbuf_tensor(f"rt_{name}", [P, *shape], dt))
        T, E, NG = N_TILE, N_EXPERT, N_GROUP
        gm, pg, s1, s2 = sb("gm", T), sb("pg", T), sb("s1", T), sb("s2", T)
        g4, g5, oh4 = sb("g4", T, NG), sb("g5", T, NG), sb("oh4", T, NG)
        Em, e1, e2 = sb("Em", T, E), sb("e1", T, E), sb("e2", T, E)
        oh = sb("oh", 2, T, E)
        both = sb("both", T, E)
        m = sb("m", 2, T)
        first = sb("first", E, dt=I32)
        firstf = sb("firstf", E)
        strict = sb("strict", P)
        tot, base = sb("tot", T, E), sb("base", T + 1, E)
        thr, thrf = sb("thr", T, dt=I32), sb("thrf", T)
        cmp = sb("cmp", E, T)
        nblk, cend, pstart = sb("nblk", E), sb("cend", E), sb("pstart", E)
        blk, blkf = sb("blk", N_BLOCK, dt=I32), sb("blkf", N_BLOCK)
        bcmp, bexp = sb("bcmp", N_BLOCK, E), sb("bexp", N_BLOCK)
        slot, pick = sb("slot", T, E), sb("pick", T, E)
        destf = sb("destf", T, 2)
        tok = sb("tok", T, dt=I32)
        zero = sb("zero", N_BLOCK, dt=I32)
        tab = ctx.enter_context(nc.sbuf_tensor("rt_tab", [N_BLOCK, P], I32))
        tabf = ctx.enter_context(nc.sbuf_tensor("rt_tabf", [N_BLOCK, P], FP32))

        def last_dim(x, shape):
            n = len(x.shape)
            v = x.rearrange("p (t a) -> p t a", a=1) if n == 2 else x.rearrange("p t (g a) -> p t g a", a=1)
            return v.to_broadcast(shape)

        def mid_dim(x, shape):
            return x.rearrange("p (a n) -> p a n", a=1).to_broadcast(shape)
        with nc.Block(no_gpsimd_drain=True) as block:

            @block.gpsimd
            def _(gp):
                gp.memset(zero[:], 0).then_inc(tok_made, 1)
                gp.wait_ge(tok_made, 1)
                gp.dma_start(K.scr["row_table"].rearrange("(p j) a -> p (j a)", p=P), zero[:]).then_inc(filled, 16)
                gp.iota(tok[:], pattern=[[P, T]], base=0, channel_multiplier=1)
                gp.iota(first[:], pattern=[[-1, E]], base=E, channel_multiplier=0)
                gp.iota(thr[:], pattern=[[P, T]], base=0, channel_multiplier=0)
                gp.iota(blk[:], pattern=[[1, N_BLOCK]], base=0, channel_multiplier=0)
                gp.memset(base[:, 0, :], 0.0)
                gp.tensor_tensor(strict[:], K.upper[:], K.ident[:], ALU.subtract).then_inc(tok_made, 1)
                gp.wait_ge(filled, 16)
                gp.wait_ge(ranked, 1)
                for c in range(2):
                    for t in range(T):
                        gp.indirect_dma_start(out=K.scr["row_table"], out_offset=bass.IndirectOffsetOnAxis(ap=dest[:, c, t:t + 1], axis=0),
                                              in_=tok[:, t:t + 1], in_offset=None).then_inc(scattered, 16)
                gp.wait_ge(scattered, 16 * 2 * T)
                gp.dma_start(tab[:], K.scr["row_table"].rearrange("(j p) a -> j (p a)", p=P)).then_inc(tab_in, 16)
                gp.wait_ge(tab_in, 16)

            @block.scalar
            def _(act):
                act.wait_ge(exped, 1)
                act.activation(g5[:], g4[:], ACT.Exp).then_inc(exped, 1)
                act.wait_ge(exped, 3)
                act.activation(s2[:], s1[:], ACT.Exp).then_inc(exped, 1)

            @block.tensor
            def _(pe):
                pe.wait_ge(tok_made, 2)
                pe.wait_ge(turned, 1)
                flat = both[:].rearrange("p t e -> p (t e)")
                pe.matmul(K.ps[:, 0, 0:T * E], strict[:], flat, start=True, stop=True)
                pe.matmul(K.ps[:, 1, 0:T * E], K.ones[:], flat, start=True, stop=True).then_inc(turned, 1)
                pe.wait_ge(tab_f, 1)
                pe.transpose(K.ps[:, 2, 0:N_BLOCK], tabf[:], K.ident[0:N_BLOCK, 0:N_BLOCK]).then_inc(turned, 1)

            @block.vector
            def _(dve):
                n = [0]

                def link(ins):
                    n[0] += 1
                    ins.then_inc(step, 1)
                    dve.wait_ge(step, n[0])

                Lg = L[:, :, 0:NG]
                Le = L[:, :, NG:]
                dve.wait_ge(tok_made, 2)
                link(dve.tensor_copy(firstf[:], first[:]))
                link(dve.tensor_copy(thrf[:], thr[:]))
                link(dve.tensor_copy(blkf[:], blk[:]))
                link(dve.tensor_reduce(gm[:], Lg, AX.X, ALU.max))
                dve.tensor_tensor(g4[:], Lg, last_dim(gm[:], [P, T, NG]), ALU.subtract).then_inc(exped, 1)
                dve.wait_ge(exped, 2)
                link(dve.tensor_reduce(pg[:], g5[:], AX.X, ALU.add))
                link(dve.reciprocal(pg[:], pg[:]))

                def first_largest(out, x, top, width, tie):
                    shape = [P, T, width]
                    link(dve.tensor_tensor(out, x, last_dim(top, shape), ALU.is_equal))
                    link(dve.tensor_tensor(tie, out, mid_dim(firstf[:, 0:width], shape), ALU.mult))
                    link(dve.tensor_reduce(s1[:], tie, AX.X, ALU.max))
                    link(dve.tensor_tensor(out, tie, last_dim(s1[:], shape), ALU.is_equal))

                first_largest(oh4[:], Lg, gm[:], NG, g4[:])
                link(dve.tensor_scalar(g4[:], oh4[:], -1.0, FAR, ALU.add, ALU.mult))
                view = [P, T, NG, PER_GROUP]
                link(dve.tensor_tensor(Em[:].rearrange("p t (g e) -> p t g e", g=NG), Le.rearrange("p t (g e) -> p t g e", g=NG),
                                       last_dim(g4[:], view), ALU.add))
                link(dve.tensor_reduce(m[:, 0, :], Em[:], AX.X, ALU.max))
                first_largest(oh[:, 0], Em[:], m[:, 0, :], E, e1[:])
                link(dve.scalar_tensor_tensor(out=e2[:], in0=oh[:, 0], scalar=-3.0 * FAR, in1=Em[:], op0=ALU.mult, op1=ALU.add))
                link(dve.tensor_reduce(m[:, 1, :], e2[:], AX.X, ALU.max))
                first_largest(oh[:, 1], e2[:], m[:, 1, :], E, e1[:])
                dve.tensor_tensor(both[:], oh[:, 0], oh[:, 1], ALU.add).then_inc(turned, 1)
                dve.tensor_tensor(s1[:], m[:, 1, :], m[:, 0, :], ALU.subtract).then_inc(exped, 1)
                dve.wait_ge(exped, 4)
                link(dve.tensor_scalar(gm[:], s2[:], 1.0, None, ALU.add))
                link(dve.reciprocal(s1[:], gm[:]))
                link(dve.tensor_tensor(weight[:, 0, :], pg[:], s1[:], ALU.mult))
                link(dve.tensor_tensor(weight[:, 1, :], weight[:, 0, :], s2[:], ALU.mult))
                dve.wait_ge(turned, 2)
                link(dve.tensor_copy(tot[:], K.ps[:, 1, 0:T * E].rearrange("p (t e) -> p t e", e=E)))
                for t in range(T):
                    link(dve.tensor_tensor(base[:, t + 1, :], base[:, t, :], tot[:, t, :], ALU.add))
                link(dve.tensor_tensor(cmp[:], last_dim(base[:, T, :], [P, E, T]), mid_dim(thrf[:], [P, E, T]), ALU.is_gt))
                link(dve.tensor_reduce(nblk[:], cmp[:], AX.X, ALU.add))
                link(dve.tensor_tensor_scan(cend[:], K.ones[:, 0:E], nblk[:], 0.0, ALU.mult, ALU.add))
                link(dve.tensor_tensor(pstart[:], cend[:], nblk[:], ALU.subtract))
                link(dve.tensor_scalar(pstart[:], pstart[:], float(P), None, ALU.mult))
                link(dve.tensor_tensor(slot[:], K.ps[:, 0, 0:T * E].rearrange("p (t e) -> p t e", e=E), base[:, 0:T, :], ALU.add))
                link(dve.tensor_tensor(slot[:], slot[:], mid_dim(pstart[:], [P, T, E]), ALU.add))
                for c in range(2):
                    link(dve.tensor_tensor(pick[:], slot[:], oh[:, c], ALU.mult))
                    link(dve.tensor_reduce(destf[:, :, c], pick[:], AX.X, ALU.add))
                    link(dve.tensor_copy(dest[:, c, :], destf[:, :, c]))
                dve.sem_inc(ranked, 1)
                shape = [P, N_BLOCK, E]
                link(dve.tensor_tensor(bcmp[:], mid_dim(cend[:], shape), last_dim(blkf[:], shape), ALU.is_le))
                link(dve.tensor_reduce(bexp[:], bcmp[:], AX.X, ALU.add))
                link(dve.tensor_scalar(bexp[:], bexp[:], float(E - 1), None, ALU.min))
                link(dve.tensor_copy(experts[:, 0:N_BLOCK], bexp[0:1, :]))
                even = blkf[0:1, 0::2]
                link(dve.tensor_tensor(bexp[0:1, 0::2], even, cend[0:1, E - 1:E].to_broadcast([1, N_BLOCK // 2]), ALU.is_lt))
                link(dve.tensor_reduce(nblk[0:1, 0:1], bexp[0:1, 0::2], AX.X, ALU.add))
                link(dve.tensor_copy(experts[:, N_BLOCK:], nblk[0:1, 0:1]))
                dve.wait_ge(tab_in, 16)
                dve.tensor_copy(tabf[:], tab[:]).then_inc(tab_f, 1)
                dve.wait_ge(turned, 3)
                link(dve.tensor_copy(row_ids[:], K.ps[:, 2, 0:N_BLOCK]))


def stage_experts(nc, K, row_ids, experts):
    with ExitStack() as ctx:
        def two(name):
            return semaphores(nc, K, f"ex_{name}0", f"ex_{name}1")
        wg_in, wu_in, wd_in, gathered, stored = two("wg_in"), two("wu_in"), two("wd_in"), two("gathered"), two("stored")
        x_turned, x_out, gu_done, silued, acted, a_turned, a_out, y_done, y_out = semaphores(
            nc, K, *[f"ex_{n}" for n in ("x_turned", "x_out", "gu_done", "silued", "acted", "a_turned", "a_out", "y_done", "y_out")])
        x_out_b, y_out_b, all_stored = semaphores(nc, K, "ex_x_out_b", "ex_y_out_b", "ex_all_stored")
        wg = ctx.enter_context(nc.sbuf_tensor("ex_wg", [P, 2, KD, FE], FP32))
        wu = ctx.enter_context(nc.sbuf_tensor("ex_wu", [P, 2, KD, FE], FP32))
        wd = ctx.enter_context(nc.sbuf_tensor("ex_wd", [P, 2, KE, D], FP32))
        xg = ctx.enter_context(nc.sbuf_tensor("ex_xg", [P, 2, D], FP32))
        XT = ctx.enter_context(nc.sbuf_tensor("ex_XT", [P, 2, KD, P], FP32))
        sg = ctx.enter_context(nc.sbuf_tensor("ex_sg", [P, FE], FP32))
        ac = ctx.enter_context(nc.sbuf_tensor("ex_ac", [P, FE], FP32))
        AT = ctx.enter_context(nc.sbuf_tensor("ex_AT", [P, KE, P], FP32))
        yo = ctx.enter_context(nc.sbuf_tensor("ex_yo", [P, 2, D], FP32))
        g_v = K.dram["w_gate_2"][0].rearrange("e (p k) f -> p e (k f)", k=KD)
        u_v = K.dram["w_up_2"][0].rearrange("e (p k) f -> p e (k f)", k=KD)
        d_v = K.dram["w_down_2"][0].rearrange("e (p k) f -> p e (k f)", k=KE)

        def pairs(eng, body):
            used = eng.value_load(experts[0:1, N_BLOCK:N_BLOCK + 1], min_val=1, max_val=N_BLOCK // 2)
            with eng.Fori(0, N_BLOCK // 2) as it:
                with eng.If(it < used):
                    body(it)
            return used

        with nc.Block(no_gpsimd_drain=True) as block:

            @block.sync
            def _(sync):
                def body(it):
                    for q in range(2):
                        e = sync.value_load(experts[0:1, bass.ds(2 * it + q, 1)], min_val=0, max_val=N_EXPERT - 1)
                        sync.wait_ge(gu_done, 2 * it + q + 1)
                        sync.dma_start(wg[:, q, :, :].rearrange("p (a k) f -> p a (k f)", a=1), g_v[:, bass.ds(e, 1), :]).then_inc(wg_in[q], 16)
                        sync.dma_start(wu[:, q, :, :].rearrange("p (a k) f -> p a (k f)", a=1), u_v[:, bass.ds(e, 1), :]).then_inc(wu_in[q], 16)
                        sync.wait_ge(y_done, 2 * it + q + 1)
                        sync.dma_start(wd[:, q, :, :].rearrange("p (a k) f -> p a (k f)", a=1), d_v[:, bass.ds(e, 1), :]).then_inc(wd_in[q], 16)
                pairs(sync, body)

            @block.gpsimd
            def _(gp):
                used = gp.value_load(experts[0:1, N_BLOCK:N_BLOCK + 1], min_val=1, max_val=N_BLOCK // 2)
                for it in range(N_BLOCK // 2):
                    with gp.If(used > it):
                        for q in range(2):
                            b = 2 * it + q
                            if b >= 2:
                                gp.wait_ge(x_turned, b - 1)
                            gp.indirect_dma_start(out=xg[:, q, :], out_offset=None, in_=K.scr["h2"],
                                                  in_offset=bass.IndirectOffsetOnAxis(ap=row_ids[:, b:b + 1], axis=0)
                                                  ).then_inc(gathered[q], 16)

            @block.tensor
            def _(pe):
                pe.sem_inc(gu_done, 2)
                pe.sem_inc(y_done, 2)

                def turn_x(b, it, q):
                    pe.wait_ge(gathered[q], 16 * it + 16)
                    pe.wait_ge(x_out, b + 1)
                    pe.wait_ge(x_out_b, b + 1)
                    for k in range(KD):
                        last = pe.transpose(K.ps[:, k // 4, (k % 4) * P:(k % 4 + 1) * P], xg[:, q, k::KD], K.ident[:])
                    last.then_inc(x_turned, 1)

                def body(it):
                    turn_x(2 * it, it, 0)
                    for q in range(2):
                        b = 2 * it + q
                        pe.wait_ge(x_out, b + 2)
                        pe.wait_ge(x_out_b, b + 2)
                        for w, loaded, bank in ((wg, wg_in, 2), (wu, wu_in, 3)):
                            pe.wait_ge(loaded[q], 16 * it + 16)
                            pe.wait_ge(acted, b + 1)
                            for k in range(KD):
                                last = pe.matmul(K.ps[:, bank, :], XT[:, q, k, :], w[:, q, k, :], start=(k == 0), stop=(k == KD - 1))
                        last.then_inc(gu_done, 1)
                        if q == 0:
                            turn_x(b + 1, it, 1)
                        pe.wait_ge(acted, b + 2)
                        pe.wait_ge(a_out, b + 1)
                        for k in range(KE):
                            last = pe.transpose(K.ps[:, 4, k * P:(k + 1) * P], ac[:, k::KE], K.ident[:])
                        last.then_inc(a_turned, 1)
                        pe.wait_ge(a_out, b + 2)
                        pe.wait_ge(wd_in[q], 16 * it + 16)
                        pe.wait_ge(y_out, b + 1)
                        pe.wait_ge(y_out_b, b + 1)
                        for n in range(2):
                            for k in range(KE):
                                last = pe.matmul(K.ps[:, 5 + n, :], AT[:, k, :], wd[:, q, k, n * HALF:(n + 1) * HALF],
                                                 start=(k == 0), stop=(k == KE - 1))
                        last.then_inc(y_done, 1)
                pairs(pe, body)

            @block.scalar
            def _(act):
                act.sem_inc(x_out, 1)
                act.sem_inc(silued, 1)
                act.sem_inc(y_out, 1)
                act.sem_inc(stored[0], 16)
                act.sem_inc(stored[1], 16)

                def x_half(b, q):
                    act.wait_ge(x_turned, b + 1)
                    act.wait_ge(gu_done, b + 1)
                    act.activation(XT[:, q, 0:4, :].rearrange("p k t -> p (k t)"), K.ps[:, 0, :], ACT.Copy).then_inc(x_out, 1)

                def body(it):
                    x_half(2 * it, 0)
                    for q in range(2):
                        b = 2 * it + q
                        act.wait_ge(gu_done, b + 3)
                        act.wait_ge(acted, b + 1)
                        act.activation(sg[:], K.ps[:, 2, :], ACT.Silu).then_inc(silued, 1)
                        if q == 0:
                            x_half(b + 1, 1)
                        act.wait_ge(y_done, b + 3)
                        act.wait_ge(stored[q], 16 * it + 16)
                        act.activation(yo[:, q, 0:HALF], K.ps[:, 5, :], ACT.Copy).then_inc(y_out, 1)
                        act.wait_ge(y_out, b + 2)
                        act.wait_ge(y_out_b, b + 2)
                        act.dma_start(K.scr["y"][bass.ds(b * P, P), :], yo[:, q, :]).then_inc(stored[q], 16)
                used = pairs(act, body)
                for q in range(2):
                    act.wait_ge(stored[q], used * 16 + 16)
                    act.sem_inc(all_stored, 1)

            @block.vector
            def _(dve):
                dve.sem_inc(x_out_b, 1)
                dve.sem_inc(acted, 1)
                dve.sem_inc(a_out, 1)
                dve.sem_inc(y_out_b, 1)

                def x_half(b, q):
                    dve.wait_ge(x_turned, b + 1)
                    dve.wait_ge(gu_done, b + 1)
                    dve.tensor_copy(XT[:, q, 4:8, :].rearrange("p k t -> p (k t)"), K.ps[:, 1, :]).then_inc(x_out_b, 1)

                def body(it):
                    x_half(2 * it, 0)
                    for q in range(2):
                        b = 2 * it + q
                        dve.wait_ge(silued, b + 2)
                        dve.wait_ge(a_out, b + 1)
                        dve.tensor_tensor(ac[:], K.ps[:, 3, :], sg[:], ALU.mult).then_inc(acted, 1)
                        if q == 0:
                            x_half(b + 1, 1)
                        dve.wait_ge(a_turned, b + 1)
                        dve.wait_ge(y_done, b + 2)
                        dve.tensor_copy(AT[:].rearrange("p k t -> p (k t)"), K.ps[:, 4, :]).then_inc(a_out, 1)
                        dve.wait_ge(y_done, b + 3)
                        dve.wait_ge(stored[q], 16 * it + 16)
                        dve.tensor_copy(yo[:, q, HALF:], K.ps[:, 6, :]).then_inc(y_out_b, 1)
                pairs(dve, body)


def stage_combine(nc, K, xt, dest, weight, out):
    with ExitStack() as ctx:
        g_in = semaphores(nc, K, *[f"cb_gathered{t}" for t in range(N_TILE)])
        gain_in, mixed, squared, rooted, inverted, scaled, stored = semaphores(
            nc, K, "cb_gain_in", "cb_mixed", "cb_squared", "cb_rooted", "cb_inverted", "cb_scaled", "cb_stored")
        gain = ctx.enter_context(nc.sbuf_tensor("cb_gain", [P, D], FP32))
        y = ctx.enter_context(nc.sbuf_tensor("cb_y", [P, N_TILE, 2, D], FP32))
        junk = ctx.enter_context(nc.sbuf_tensor("cb_junk", [P, D], FP32))
        ss = ctx.enter_context(nc.sbuf_tensor("cb_ss", [P, 3, N_TILE], FP32))
        with nc.Block(no_gpsimd_drain=True) as block:

            @block.gpsimd
            def _(gp):
                for t in range(N_TILE):
                    for c in range(2):
                        gp.indirect_dma_start(out=y[:, t, c, :], out_offset=None, in_=K.scr["y"],
                                              in_offset=bass.IndirectOffsetOnAxis(ap=dest[:, c, t:t + 1], axis=0)
                                              ).then_inc(g_in[t], 16)

            @block.sync
            def _(sync):
                sync.dma_start(gain[:], K.dram["final_norm_g_2"].rearrange("(a n) -> a n", a=1).to_broadcast([P, D])).then_inc(gain_in, 16)
                for t in range(N_TILE):
                    sync.wait_ge(scaled, t + 1)
                    sync.dma_start(out[t * P:(t + 1) * P, :], xt[:, t, :]).then_inc(stored, 16)
                sync.wait_ge(stored, 16 * N_TILE)

            @block.vector
            def _(dve):
                for t in range(N_TILE):
                    dve.wait_ge(g_in[t], 32)
                    for c in range(2):
                        dve.scalar_tensor_tensor(out=xt[:, t, :], in0=y[:, t, c, :], scalar=weight[:, c, t:t + 1],
                                                 in1=xt[:, t, :], op0=ALU.mult, op1=ALU.add).then_inc(mixed, 1)
                        dve.wait_ge(mixed, 2 * t + c + 1)
                dve.wait_ge(gain_in, 16)
                for t in range(N_TILE):
                    dve.wait_ge(rooted, t + 1)
                    dve.reciprocal(ss[:, 2, t:t + 1], ss[:, 1, t:t + 1]).then_inc(inverted, 1)
                    dve.wait_ge(inverted, t + 1)
                    dve.scalar_tensor_tensor(out=xt[:, t, :], in0=xt[:, t, :], scalar=ss[:, 2, t:t + 1], in1=gain[:],
                                             op0=ALU.mult, op1=ALU.mult).then_inc(scaled, 1)

            @block.scalar
            def _(act):
                for t in range(N_TILE):
                    act.wait_ge(mixed, 2 * (t + 1))
                    if t:
                        act.wait_ge(squared, t)
                    act.activation(junk[:], xt[:, t, :], ACT.Square, accum_out=ss[:, 0, t:t + 1]).then_inc(squared, 1)
                    act.wait_ge(squared, t + 1)
                    act.activation(ss[:, 1, t:t + 1], ss[:, 0, t:t + 1], ACT.Sqrt, bias=K.eps_rms[:, 0:1],
                                   scale=1.0 / D).then_inc(rooted, 1)


def second_mixer(nc, K):
    with ExitStack() as ctx:
        oT = ctx.enter_context(nc.sbuf_tensor("oT", [P, 2 * HEADS, LEN], FP32))
        with ExitStack() as inner:
            G = inner.enter_context(nc.sbuf_tensor("G", [P, N_CHUNK, HEADS], FP32))
            beta = inner.enter_context(nc.sbuf_tensor("beta", [P, N_CHUNK, HEADS], FP32))
            second_projections(nc, K, G, beta)
            stage_recurrences(nc, K, G, beta, oT)
        stage_head_norm(nc, K, oT)
        mT = ctx.enter_context(nc.sbuf_tensor("mT", [P, KD, SEQ], FP32))
        stage_merge(nc, K, oT, mT)
        stage_residual(nc, K, "wo2", mT, K.dram["w_out_2"][0], KD)


def second_moe(nc, K, out):
    with ExitStack() as ctx:
        xt = ctx.enter_context(nc.sbuf_tensor("xt", [P, N_TILE, D], FP32))
        dest = ctx.enter_context(nc.sbuf_tensor("dest", [P, 2, N_TILE], I32))
        weight = ctx.enter_context(nc.sbuf_tensor("weight", [P, 2, N_TILE], FP32))
        row_ids = ctx.enter_context(nc.sbuf_tensor("row_ids", [P, N_BLOCK], I32))
        experts = ctx.enter_context(nc.sbuf_tensor("experts", [1, N_BLOCK + 1], I32))
        with ExitStack() as inner:
            L = inner.enter_context(nc.sbuf_tensor("logits", [P, N_TILE, N_LOGIT], FP32))
            stage_to_tokens(nc, K, xt, L)
            stage_route(nc, K, L, dest, weight, row_ids, experts)
        stage_experts(nc, K, row_ids, experts)
        stage_combine(nc, K, xt, dest, weight, out)


def program(nc, dram, out):
    K = Pack()
    K.dram = dram
    with ExitStack() as ctx:
        common(nc, ctx, K)
        K.scr = scratch(nc)
        stage_constants(nc, K)
        first_block(nc, K)
        retire_semaphores(nc, K)
        second_mixer(nc, K)
        retire_semaphores(nc, K)
        second_moe(nc, K, out)


_INS = ["x", "norm_mix_g", "w_in", "conv_a_w", "conv_b_w", "conv_b_b", "ln_b_g", "ln_b_b", "w_out", "norm_ffn_g",
        "w_gate", "w_up", "conv_ffn_w", "w_down", "norm_final_g", "meta_tokens_2", "hg_lb_logits_2", "norm_mix_g_2",
        "w_in_2", "gd_conv_w_2", "gd_A_log_2", "gd_dt_bias_2", "hg_norm_g_2", "gd_norm_g_2", "hg_up_2", "gd_up_2",
        "w_out_2", "norm_ffn_g_2", "router_group_w_2", "router_group_b_2", "router_expert_w_2", "router_expert_b_2",
        "w_gate_2", "w_up_2", "w_down_2", "final_norm_g_2"]


def kernel(**inputs):
    import concourse.bacc as _bacc
    from concourse.bass_utils import run_bass_kernel_spmd as _run

    nc = _bacc.Bacc("TRN2", target_bir_lowering=False, num_devices=1)
    arrays, dram = {}, {}
    for name in _INS:
        a = np.ascontiguousarray(inputs[name])
        arrays[f"in_{name}_dram"] = a
        dram[name] = nc.dram_tensor(f"in_{name}_dram", a.shape, mybir.dt.from_np(a.dtype), kind="ExternalInput").ap()
    out = nc.dram_tensor("out_0_dram", (1, SEQ, D), FP32, kind="ExternalOutput").ap()
    program(nc, dram, out[0])
    r = _run(nc, [arrays], core_ids=[0])
    return r.results[0]["out_0_dram"]
```

```python
import numpy as np
import concourse.bass as bass
from concourse import mybir
from contextlib import ExitStack

FP32 = mybir.dt.float32
FP32R = mybir.dt.float32r
I32 = mybir.dt.int32
ALU = mybir.AluOpType
ACT = mybir.ActivationFunctionType
AX = mybir.AxisListType

P = 128
D = 1024
KD = D // P
SEQ = 1024
HALF = 512
DFF = 2816
NF = DFF // P
EPS_RMS = 1e-6
EPS_LN = 1e-5


class Pack:
    pass


def semaphores(nc, K, *names):
    got = [nc.alloc_semaphore(name=n) for n in names]
    K.sems.extend(got)
    return got


def retire_semaphores(nc, K):
    nc.clear_and_free_semaphores(K.sems)
    nc.all_engine_barrier()
    K.sems = []


def pair(ps, slot):
    return ps[:, 2 * slot:2 * slot + 2, :].rearrange("p b n -> p (b n)")


class Halves:

    def __init__(self, nc, ctx, name, shape):
        self.hi = ctx.enter_context(nc.sbuf_tensor(f"{name}_hi", shape, FP32R))
        self.lo = ctx.enter_context(nc.sbuf_tensor(f"{name}_lo", shape, FP32R))


class Weights:

    def __init__(self, nc, K, ctx, tag, slots, nk, cols=P):
        self.nk = nk
        self.raw = ctx.enter_context(nc.sbuf_tensor(f"{tag}_w", [P, slots, nk, cols], FP32))
        self.part = Halves(nc, ctx, f"{tag}_w", [P, slots, nk, cols])
        self.loaded = semaphores(nc, K, *[f"{tag}_w_in{q}" for q in range(slots)])
        self.rounded = semaphores(nc, K, *[f"{tag}_w_rounded{q}" for q in range(slots)])
        self.split = semaphores(nc, K, *[f"{tag}_w_split{q}" for q in range(slots)])
        self.done = semaphores(nc, K, *[f"{tag}_done{q}" for q in range(slots)])

    def start(self, sync):
        for q in range(len(self.split)):
            sync.sem_inc(self.split[q], 1)
            sync.sem_inc(self.done[q], 1)

    def load(self, sync, q, n, src):
        sync.wait_ge(self.split[q], n + 1)
        sync.dma_start(self.raw[:, q], src).then_inc(self.loaded[q], 16)

    def round(self, act, q, n):
        act.wait_ge(self.loaded[q], n * 16 + 16)
        act.wait_ge(self.done[q], n + 1)
        act.activation(self.part.hi[:, q], self.raw[:, q], ACT.Copy).then_inc(self.rounded[q], 1)

    def rest(self, gp, q, n):
        gp.wait_ge(self.rounded[q], n + 1)
        gp.tensor_tensor(self.part.lo[:, q], self.raw[:, q], self.part.hi[:, q], ALU.subtract).then_inc(self.split[q], 1)


def three_products(pe, out, w_hi, w_lo, x_hi, x_lo, start, stop):
    pe.matmul(out, w_hi, x_hi, start=start, stop=False)
    pe.matmul(out, w_hi, x_lo, start=False, stop=False)
    return pe.matmul(out, w_lo, x_hi, start=False, stop=stop)


def project(pe, ps, bank0, W, q, n, src, groups, lo=0, ready=None):
    pe.wait_ge(W.split[q], n + 2)
    for g, cols in enumerate(groups):
        at = lo + sum(groups[:g])
        for k in range(W.nk):
            if ready is not None:
                pe.wait_ge(ready, g * W.nk + k + 1)
            last = three_products(pe, ps[:, bank0 + g, 0:cols], W.part.hi[:, q, k, :], W.part.lo[:, q, k, :],
                                  src.hi[:, k, at:at + cols], src.lo[:, k, at:at + cols], k == 0, k == W.nk - 1)
    last.then_inc(W.done[q], 1)



PARAM_ROWS = [
    [("conv_b_w", 124), ("conv_b_b", 4)],
    [("conv_ffn_w", 66), ("conv_a_w", 12), ("norm_mix_g", 8), ("norm_ffn_g", 8), ("norm_final_g", 8),
     ("norm_mix_g_2", 8), ("ln_b_g", 4), ("ln_b_b", 4), ("hg_norm_g_2", 1), ("gd_norm_g_2", 1),
     ("hg_lb_logits_2", 8)],
    [("gd_conv_w_2", 48), ("norm_ffn_g_2", 8)],
]


def stage_constants(nc, K):
    with ExitStack() as ctx:
        rows_in, zeroed, made, turned, out_of = semaphores(
            nc, K, "par_rows_in", "par_zeroed", "const_made", "par_turned", "par_out")
        rows = ctx.enter_context(nc.sbuf_tensor("par_rows", [P, len(PARAM_ROWS), P], FP32))
        n_in = sum(len(g) for g in PARAM_ROWS)
        with nc.Block(no_gpsimd_drain=True) as block:

            @block.sync
            def _(sync):
                sync.wait_ge(zeroed, 1)
                at = 0
                for t, group in enumerate(PARAM_ROWS):
                    r = 0
                    for name, n in group:
                        K.col[name] = at + r
                        src = K.dram[name]
                        flat = src.rearrange(" a b c -> (a b c)") if len(src.shape) == 3 else (
                            src.rearrange("a b -> (a b)") if len(src.shape) == 2 else src)
                        sync.dma_start(rows[r:r + n, t, :], flat.rearrange("(r c) -> r c", c=P)).then_inc(rows_in, 16)
                        r += n
                    at += P

            @block.gpsimd
            def _(gp):
                gp.memset(rows[:], 0.0).then_inc(zeroed, 1)
                gp.memset(K.ones[:], 1.0)
                gp.memset(K.eps_rms[:], EPS_RMS)
                gp.memset(K.eps_ln[:], EPS_LN)
                gp.memset(K.ident[:], 0.0).then_inc(made, 1)
                gp.memset(K.upper[:], 1.0).then_inc(made, 1)
                gp.memset(K.level[:], 0.0).then_inc(made, 1)
                gp.wait_ge(made, 3)
                gp.affine_select(out=K.ident[:], in_=K.ident[:], compare_op=ALU.not_equal, fill=1.0,
                                 base=0, pattern=[[-1, P]], channel_multiplier=1).then_inc(made, 1)
                gp.affine_select(out=K.upper[:], in_=K.upper[:], compare_op=ALU.is_ge, fill=0.0,
                                 base=0, pattern=[[1, P]], channel_multiplier=-1).then_inc(made, 1)
                n = 5
                for lev in range(1, 8):
                    m = 1 << lev
                    right = K.level[:, lev, :].rearrange("p (b h i) -> p b h i", h=2, i=m // 2)[:, :, 1, :]
                    gp.memset(right, 1.0).then_inc(made, 1)
                    n += 1
                    gp.wait_ge(made, n)
                    gp.affine_select(out=right, in_=right, compare_op=ALU.is_ge, fill=0.0, base=0,
                                     pattern=[[-m, P // m], [0, m // 2]], channel_multiplier=1).then_inc(made, 1)
                    n += 1
                    gp.wait_ge(made, n)
                    gp.affine_select(out=right, in_=right, compare_op=ALU.is_ge, fill=0.0, base=m // 2 - 1,
                                     pattern=[[m, P // m], [0, m // 2]], channel_multiplier=-1).then_inc(made, 1)
                    n += 1
                gp.wait_ge(made, n)
                gp.tensor_copy(K.level[:, 0, :], K.ident[:]).then_inc(made, 1)
                gp.wait_ge(made, n + 1)

            @block.tensor
            def _(pe):
                pe.wait_ge(made, 4)
                pe.wait_ge(rows_in, 16 * n_in)
                for t in range(len(PARAM_ROWS)):
                    last = pe.transpose(K.ps[:, t, 0:P], rows[:, t, :], K.ident[:])
                last.then_inc(turned, 1)

            @block.scalar
            def _(act):
                act.wait_ge(turned, 1)
                for t in range(len(PARAM_ROWS)):
                    act.activation(K.par[:, t * P:(t + 1) * P], K.ps[:, t, 0:P], ACT.Copy).then_inc(out_of, 1)


def param(K, name, i=0):
    c = K.col[name] + i
    return K.par[:, bass.ds(c, 1)]



def stage_load_x(nc, K):
    n_tok = SEQ // P
    with ExitStack() as ctx:
        loaded, turned, freed = semaphores(nc, K, "x_loaded", "x_turned", "x_turned_out")
        rows = ctx.enter_context(nc.sbuf_tensor("x_rows", [P, n_tok, D], FP32))
        with nc.Block(no_gpsimd_drain=True) as block:

            @block.sync
            def _(sync):
                for t in range(n_tok):
                    sync.dma_start(rows[:, t, :], K.dram["x"][0, t * P:(t + 1) * P, :]).then_inc(loaded, 16)
                sync.wait_ge(loaded, 16 * n_tok)

            @block.tensor
            def _(pe):
                pe.wait_ge(loaded, 16 * n_tok)
                for k in range(KD):
                    for g in range(2):
                        n = 2 * k + g
                        if n >= 8:
                            pe.wait_ge(freed, n - 7)
                        for t in range(4):
                            last = pe.transpose(K.ps[:, n % 8, t * P:(t + 1) * P],
                                                rows[:, 4 * g + t, k * P:(k + 1) * P], K.ident[:])
                        last.then_inc(turned, 1)

            @block.scalar
            def _(act):
                for n in range(2 * KD):
                    act.wait_ge(turned, n + 1)
                    act.activation(K.xT[:, n // 2, (n % 2) * HALF:(n % 2 + 1) * HALF], K.ps[:, n % 8, :],
                                   ACT.Copy).then_inc(freed, 1)


class RmsNorm:

    def __init__(self, nc, K, ctx, tag, gain, parts, split=True, room=None):
        self.K, self.parts, self.gain, self.split = K, parts, gain, split
        self.squared, self.summed, self.rooted, self.inverted, self.scaled, self.rounded, self.ready = semaphores(
            nc, K, *[f"{tag}_{n}" for n in ("squared", "summed", "rooted", "inverted", "scaled", "rounded", "ready")])
        if room is None:
            room = ctx.enter_context(nc.sbuf_tensor(f"{tag}_room", [P, 6, HALF], FP32))
        self.sq, self.root, self.inv, self.tmp = room[:, 0:2], room[:, 2], room[:, 3], room[:, 4:6]

    def scalar(self, act):
        def squares(g):
            s, s_at, _, _, n = self.parts[g]
            for k in range(KD):
                m = g * KD + k
                if m >= 2:
                    act.wait_ge(self.summed, m - 1)
                act.activation(self.sq[:, m % 2, 0:n], s[:, k, s_at:s_at + n], ACT.Square).then_inc(self.squared, 1)

        def root(g):
            act.wait_ge(self.summed, (g + 1) * KD)
            if g:
                act.wait_ge(self.inverted, g)
            act.activation(self.root[:, 0:self.parts[g][4]], self.K.ps[:, 7 - g, 0:self.parts[g][4]], ACT.Sqrt,
                           bias=self.K.eps_rms[:, 0:1], scale=1.0 / D).then_inc(self.rooted, 1)
        squares(0)
        root(0)
        for g, (_, _, d, d_at, n) in enumerate(self.parts):
            if g + 1 < len(self.parts):
                squares(g + 1)
            if self.split:
                for k in range(KD):
                    m = g * KD + k
                    act.wait_ge(self.scaled, m + 1)
                    act.activation(d.hi[:, k, d_at:d_at + n], self.tmp[:, m % 2, 0:n], ACT.Copy).then_inc(self.rounded, 1)
            if g + 1 < len(self.parts):
                root(g + 1)

    def tensor(self, pe):
        for g, (_, _, _, _, n) in enumerate(self.parts):
            for k in range(KD):
                m = g * KD + k
                pe.wait_ge(self.squared, m + 1)
                pe.matmul(self.K.ps[:, 7 - g, 0:n], self.K.ones[:], self.sq[:, m % 2, 0:n], start=(k == 0),
                          stop=(k == KD - 1)).then_inc(self.summed, 1)

    def vector(self, dve):
        for g, (s, s_at, d, d_at, n) in enumerate(self.parts):
            dve.wait_ge(self.rooted, g + 1)
            if g:
                dve.wait_ge(self.scaled, g * KD)
            dve.reciprocal(self.inv[:, 0:n], self.root[:, 0:n]).then_inc(self.inverted, 1)
            dve.wait_ge(self.inverted, g + 1)
            for k in range(KD):
                m = g * KD + k
                out = d[:, k, d_at:d_at + n]if not self.split else self.tmp[:, m % 2, 0:n]
                if self.split and m >= 2:
                    dve.wait_ge(self.ready, m - 1)
                dve.scalar_tensor_tensor(out=out, in0=s[:, k, s_at:s_at + n], scalar=param(self.K, self.gain, k),
                                         in1=self.inv[:, 0:n], op0=ALU.mult, op1=ALU.mult).then_inc(self.scaled, 1)
        dve.wait_ge(self.scaled, len(self.parts) * KD)

    def gpsimd(self, gp):
        for g, (_, _, d, d_at, n) in enumerate(self.parts):
            for k in range(KD):
                m = g * KD + k
                gp.wait_ge(self.rounded, m + 1)
                gp.tensor_tensor(d.lo[:, k, d_at:d_at + n], self.tmp[:, m % 2, 0:n], d.hi[:, k, d_at:d_at + n],
                                 ALU.subtract).then_inc(self.ready, 1)


def stage_rmsnorm(nc, K, tag, gain, parts):
    with ExitStack() as ctx:
        norm = RmsNorm(nc, K, ctx, tag, gain, parts, split=False)
        with nc.Block(no_gpsimd_drain=True) as block:

            @block.scalar
            def _(act):
                norm.scalar(act)

            @block.tensor
            def _(pe):
                norm.tensor(pe)

            @block.vector
            def _(dve):
                norm.vector(dve)


def halves(src, dst):
    return [(src, h * HALF, dst, h * HALF, HALF) for h in range(2)]


def stage_mixer(nc, K, hT, y):
    TAPS = 31
    PAD = TAPS // 2
    with ExitStack() as ctx:
        norm = RmsNorm(nc, K, ctx, "n1", "norm_mix_g", halves(K.xT, hT),
                       room=y[:, 0:3].rearrange("p k (h n) -> p (k h) n", n=HALF))
        free = semaphores(nc, K, *[f"mx_free{q}" for q in range(4)])
        padded, step = semaphores(nc, K, "mx_padded", "mx_step")
        W = Weights(nc, K, ctx, "mx", 4, KD)
        sg = ctx.enter_context(nc.sbuf_tensor("mx_sg", [P, 2, SEQ], FP32))
        u = ctx.enter_context(nc.sbuf_tensor("mx_u", [P, 2, SEQ + 2 * PAD], FP32))
        ca = ctx.enter_context(nc.sbuf_tensor("mx_ca", [P, SEQ], FP32))
        w_v = K.dram["w_in"][0].rearrange("(k p) e -> p k e", p=P)
        GATED = (12, 16)
        SHORT = (0, 8, 4)
        with nc.Block(no_gpsimd_drain=True) as block:

            @block.sync
            def _(sync):
                W.start(sync)
                with sync.Fori(0, 2) as it:
                    for q in range(4):
                        W.load(sync, q, it, w_v[:, :, bass.ds((GATED[q % 2] + q // 2) * P + it * (2 * P), P)])
                with sync.Fori(0, 4) as i:
                    for q in range(3):
                        W.load(sync, q, i + 2, w_v[:, :, bass.ds(SHORT[q] * P + i * P, P)])

            @block.gpsimd
            def _(gp):
                gp.memset(u[:, :, 0:PAD], 0.0)
                gp.memset(u[:, :, PAD + SEQ:], 0.0).then_inc(padded, 1)
                for q in range(4):
                    W.rest(gp, q, 0)
                norm.gpsimd(gp)
                for q in range(4):
                    W.rest(gp, q, 1)
                with gp.Fori(0, 4) as i:
                    for q in range(3):
                        W.rest(gp, q, i + 2)

            @block.tensor
            def _(pe):
                norm.tensor(pe)
                with pe.Fori(0, 2) as it:
                    for q in range(4):
                        pe.wait_ge(free[q], it + 1)
                        project(pe, K.ps, 2 * q, W, q, it, hT, [HALF, HALF], ready=norm.ready)
                with pe.Fori(0, 4) as i:
                    for q in range(3):
                        pe.wait_ge(free[q], i + 3)
                        project(pe, K.ps, 2 * q, W, q, i + 2, hT, [HALF, HALF])

            @block.scalar
            def _(act):
                for q in range(4):
                    W.round(act, q, 0)
                norm.scalar(act)
                for it in range(2):
                    for v in range(2):
                        act.wait_ge(W.done[2 * v + 1], it + 2)
                        if it:
                            act.wait_ge(free[2 * v], it + 1)
                        act.activation(sg[:, v, :], pair(K.ps, 2 * v + 1), ACT.Sigmoid).then_inc(free[2 * v + 1], 1)
                        W.round(act, 2 * v, it + 1)
                        if v == 0 or it == 0:
                            W.round(act, 2 * v + 1, it + 1)
                with act.Fori(0, 3) as i:
                    act.wait_ge(W.done[0], i + 4)
                    act.wait_ge(free[1], i + 3)
                    act.activation(sg[:, 0, :], pair(K.ps, 0), ACT.Copy).then_inc(free[0], 1)
                    for q in range(3):
                        W.round(act, q, i + 3)
                act.wait_ge(W.done[0], 7)
                act.wait_ge(free[1], 6)
                act.activation(sg[:, 0, :], pair(K.ps, 0), ACT.Copy).then_inc(free[0], 1)

            @block.vector
            def _(dve):
                for q in range(4):
                    dve.sem_inc(free[q], 1)
                norm.vector(dve)
                dve.wait_ge(padded, 1)
                with dve.Fori(0, 2) as it:
                    for v in range(2):
                        dve.wait_ge(W.done[2 * v], it + 2)
                        dve.wait_ge(free[2 * v + 1], it + 2)
                        dve.tensor_tensor(u[:, v, PAD:PAD + SEQ], pair(K.ps, 2 * v), sg[:, v, :],
                                          ALU.mult).then_inc(free[2 * v], 1)
                        dve.wait_ge(free[2 * v], it + 2)
                        acc = y[:, bass.ds(4 + v + 2 * it, 1), :]
                        for k in range(TAPS):
                            src = u[:, v:v + 1, k:k + SEQ]
                            tap = K.par[:, bass.ds(K.col["conv_b_w"] + 4 * k + v + 2 * it, 1)]
                            if k == 0:
                                bias = K.par[:, bass.ds(K.col["conv_b_b"] + v + 2 * it, 1)]
                                dve.tensor_scalar(acc, src, tap, bias, ALU.mult, ALU.add).then_inc(step, 1)
                            else:
                                dve.scalar_tensor_tensor(out=acc, in0=src, scalar=tap, in1=acc, op0=ALU.mult,
                                                         op1=ALU.add).then_inc(step, 1)
                            dve.wait_ge(step, (2 * it + v) * TAPS + k + 1)
                with dve.Fori(0, 4) as i:
                    n0 = 4 * TAPS
                    dve.wait_ge(W.done[1], i + 4)
                    dve.wait_ge(free[0], i + 4)
                    dve.tensor_tensor(ca[:], pair(K.ps, 1), sg[:, 0, :], ALU.mult).then_inc(free[1], 1)
                    dve.wait_ge(free[1], i + 4)
                    conv3(dve, K, sg[:, 1, :], ca[:], "conv_a_w", 4, i, step, n0 + 3 * i)
                    dve.wait_ge(W.done[2], i + 4)
                    dve.tensor_tensor(y[:, bass.ds(i, 1), :], pair(K.ps, 2), sg[:, 1, :], ALU.mult).then_inc(free[2], 1)
                    dve.wait_ge(free[2], i + 4)


def conv3(dve, K, out, src, name, tiles, i, step, at):
    n = SEQ

    def tap(k):
        return K.par[:, bass.ds(K.col[name] + tiles * k + i, 1)]
    dve.tensor_scalar(out, src, tap(1), None, ALU.mult).then_inc(step, 1)
    dve.wait_ge(step, at + 1)
    dve.scalar_tensor_tensor(out=out[:, 1:n], in0=src[:, 0:n - 1], scalar=tap(0), in1=out[:, 1:n],
                             op0=ALU.mult, op1=ALU.add).then_inc(step, 1)
    dve.wait_ge(step, at + 2)
    dve.scalar_tensor_tensor(out=out[:, 0:n - 1], in0=src[:, 1:n], scalar=tap(2), in1=out[:, 0:n - 1],
                             op0=ALU.mult, op1=ALU.add).then_inc(step, 1)
    dve.wait_ge(step, at + 3)


def stage_layernorm_silu(nc, K, yb):
    NT = 4
    W = NT * P
    with ExitStack() as ctx:
        summed, meaned, centred, squared, ssummed, rooted, inverted, normed, out = semaphores(
            nc, K, "ln_summed", "ln_meaned", "ln_centred", "ln_squared", "ln_ssummed", "ln_rooted",
            "ln_inverted", "ln_normed", "ln_out")
        mu = ctx.enter_context(nc.sbuf_tensor("ln_mu", [P, 2, HALF], FP32))
        sq = ctx.enter_context(nc.sbuf_tensor("ln_sq", [P, 2, NT, HALF], FP32))
        inv = ctx.enter_context(nc.sbuf_tensor("ln_inv", [P, 2, 2, HALF], FP32))
        part = [[yb[:, i, h * HALF:(h + 1) * HALF] for i in range(NT)] for h in range(2)]
        with nc.Block(no_gpsimd_drain=True) as block:

            @block.tensor
            def _(pe):
                for h in range(2):
                    for i in range(NT):
                        last = pe.matmul(K.ps[:, h, :], K.ones[:], part[h][i], start=(i == 0), stop=(i == NT - 1))
                    last.then_inc(summed, 1)
                for h in range(2):
                    for i in range(NT):
                        pe.wait_ge(squared, h * NT + i + 1)
                        last = pe.matmul(K.ps[:, 2 + h, :], K.ones[:], sq[:, h, i, :], start=(i == 0),
                                         stop=(i == NT - 1))
                    last.then_inc(ssummed, 1)

            @block.scalar
            def _(act):
                for h in range(2):
                    for i in range(NT):
                        act.wait_ge(centred, h * NT + i + 1)
                        act.activation(sq[:, h, i, :], part[h][i], ACT.Square).then_inc(squared, 1)
                for h in range(2):
                    act.wait_ge(ssummed, h + 1)
                    act.activation(inv[:, h, 0, :], K.ps[:, 2 + h, :], ACT.Sqrt, bias=K.eps_ln[:, 0:1],
                                   scale=1.0 / W).then_inc(rooted, 1)
                for h in range(2):
                    for i in range(NT):
                        act.wait_ge(normed, h * NT + i + 1)
                        act.activation(part[h][i], part[h][i], ACT.Silu, bias=param(K, "ln_b_b", i),
                                       scale=param(K, "ln_b_g", i)).then_inc(out, 1)

            @block.vector
            def _(dve):
                for h in range(2):
                    dve.wait_ge(summed, h + 1)
                    dve.tensor_scalar(mu[:, h, :], K.ps[:, h, :], 1.0 / W, None, ALU.mult).then_inc(meaned, 1)
                    dve.wait_ge(meaned, h + 1)
                    for i in range(NT):
                        dve.tensor_tensor(part[h][i], part[h][i], mu[:, h, :], ALU.subtract).then_inc(centred, 1)
                for h in range(2):
                    dve.wait_ge(rooted, h + 1)
                    dve.reciprocal(inv[:, h, 1, :], inv[:, h, 0, :]).then_inc(inverted, 1)
                    dve.wait_ge(inverted, h + 1)
                    dve.wait_ge(squared, (h + 1) * NT)
                    for i in range(NT):
                        dve.tensor_tensor(part[h][i], part[h][i], inv[:, h, 1, :], ALU.mult).then_inc(normed, 1)


def stage_residual(nc, K, tag, src, at, part, w_dram):
    with ExitStack() as ctx:
        free = semaphores(nc, K, *[f"{tag}_free{q}" for q in range(2)])
        rounded, ready = semaphores(nc, K, f"{tag}_src_rounded", f"{tag}_src_ready")
        W = Weights(nc, K, ctx, tag, 2, KD)
        w_v = w_dram.rearrange("(k p) e -> p k e", p=P)
        n_it = KD // 2
        with nc.Block(no_gpsimd_drain=True) as block:

            @block.sync
            def _(sync):
                W.start(sync)
                with sync.Fori(0, n_it) as it:
                    for q in range(2):
                        W.load(sync, q, it, w_v[:, :, bass.ds(q * P + it * (2 * P), P)])

            @block.scalar
            def _(act):
                for g in range(2):
                    for k in range(KD):
                        cols = slice(g * HALF, (g + 1) * HALF)
                        act.activation(part.hi[:, k, cols], src[:, k, at + g * HALF:at + (g + 1) * HALF], ACT.Copy
                                       ).then_inc(rounded, 1)
                    W.round(act, g, 0)
                with act.Fori(1, n_it) as it:
                    for q in range(2):
                        W.round(act, q, it)

            @block.gpsimd
            def _(gp):
                with gp.Fori(0, n_it) as it:
                    for q in range(2):
                        W.rest(gp, q, it)

            @block.tensor
            def _(pe):
                with pe.Fori(0, n_it) as it:
                    for q in range(2):
                        pe.wait_ge(free[q], it + 1)
                        project(pe, K.ps, 2 * q, W, q, it, part, [HALF, HALF], ready=ready)

            @block.vector
            def _(dve):
                for q in range(2):
                    dve.sem_inc(free[q], 1)
                for g in range(2):
                    for k in range(KD):
                        cols = slice(g * HALF, (g + 1) * HALF)
                        dve.wait_ge(rounded, g * KD + k + 1)
                        dve.tensor_tensor(part.lo[:, k, cols], src[:, k, at + g * HALF:at + (g + 1) * HALF],
                                          part.hi[:, k, cols], ALU.subtract).then_inc(ready, 1)
                with dve.Fori(0, n_it) as it:
                    for q in range(2):
                        dve.wait_ge(W.done[q], it + 2)
                        x = K.xT[:, bass.ds(2 * it + q, 1), :]
                        dve.tensor_tensor(x, pair(K.ps, q), x, ALU.add).then_inc(free[q], 1)


def stage_ffn(nc, K, hT):
    n_it = NF // 2
    with ExitStack() as ctx:
        norm = RmsNorm(nc, K, ctx, "n2", "norm_ffn_g", halves(K.xT, hT))
        free = semaphores(nc, K, *[f"ff_free{q}" for q in range(4)])
        stored = semaphores(nc, K, "ff_stored0", "ff_stored1")
        step, silu, zeroed, y_filled = semaphores(nc, K, "ff_step", "ff_silu", "ff_zeroed", "ff_y_filled")
        W = Weights(nc, K, ctx, "ff", 4, KD)
        zero = ctx.enter_context(nc.sbuf_tensor("ff_zero", [P, D], FP32))
        g = ctx.enter_context(nc.sbuf_tensor("ff_g", [P, 2, SEQ], FP32))
        p = ctx.enter_context(nc.sbuf_tensor("ff_p", [P, 2, SEQ], FP32))
        w_v = [K.dram[n][0].rearrange("(k p) e -> p k e", p=P) for n in ("w_gate", "w_up")]
        with nc.Block(no_gpsimd_drain=True) as block:

            @block.sync
            def _(sync):
                W.start(sync)
                with sync.Fori(0, n_it) as it:
                    for q in range(4):
                        W.load(sync, q, it, w_v[q % 2][:, :, bass.ds(q // 2 * P + it * (2 * P), P)])

            @block.gpsimd
            def _(gp):
                gp.memset(zero[:], 0.0).then_inc(zeroed, 1)
                gp.wait_ge(zeroed, 1)
                gp.dma_start(K.scr["y"].rearrange("(j p) d -> p j d", p=P),
                             zero[:].rearrange("p (a d) -> p a d", a=1).to_broadcast([P, N_BLOCK, D])).then_inc(y_filled, 16)
                for q in range(4):
                    W.rest(gp, q, 0)
                norm.gpsimd(gp)
                with gp.Fori(1, n_it) as it:
                    for q in range(4):
                        W.rest(gp, q, it)
                gp.wait_ge(y_filled, 16)

            @block.tensor
            def _(pe):
                norm.tensor(pe)
                with pe.Fori(0, n_it) as it:
                    for q in range(4):
                        pe.wait_ge(free[q], it + 1)
                        project(pe, K.ps, 2 * q, W, q, it, hT, [HALF, HALF], ready=norm.ready)

            @block.scalar
            def _(act):
                for v in range(2):
                    act.sem_inc(stored[v], 16)
                for q in range(4):
                    W.round(act, q, 0)
                norm.scalar(act)

                def body(it, more):
                    for v in range(2):
                        act.wait_ge(free[2 * v], it + 2)
                        act.activation(g[:, v, :], g[:, v, :], ACT.Silu).then_inc(silu, 1)
                        if more:
                            W.round(act, 2 * v, it + 1)
                            W.round(act, 2 * v + 1, it + 1)
                        act.wait_ge(free[2 * v + 1], it + 2)
                        act.dma_start(K.scr["p"][bass.ds(it * (2 * P) + v * P, P), :], p[:, v, :]).then_inc(stored[v], 16)
                with act.Fori(0, n_it - 1) as it:
                    body(it, True)
                body(n_it - 1, False)
                for v in range(2):
                    act.wait_ge(stored[v], 16 * (n_it + 1))

            @block.vector
            def _(dve):
                for q in range(4):
                    dve.sem_inc(free[q], 1)
                norm.vector(dve)
                with dve.Fori(0, n_it) as it:
                    for v in range(2):
                        dve.wait_ge(W.done[2 * v], it + 2)
                        conv3(dve, K, g[:, v, :], pair(K.ps, 2 * v), "conv_ffn_w", NF, 2 * it + v, step,
                              6 * it + 3 * v)
                        dve.sem_inc(free[2 * v], 1)
                        dve.wait_ge(W.done[2 * v + 1], it + 2)
                        dve.wait_ge(silu, 2 * it + v + 1)
                        dve.wait_ge(stored[v], 16 * it + 16)
                        dve.tensor_tensor(p[:, v, :], pair(K.ps, 2 * v + 1), g[:, v, :],
                                          ALU.mult).then_inc(free[2 * v + 1], 1)
                        dve.wait_ge(free[2 * v + 1], it + 2)


def stage_down(nc, K):
    S = 4
    with ExitStack() as ctx:
        loaded = semaphores(nc, K, *[f"dn_in{q}" for q in range(S)])
        rounded, split, used, summed, out = semaphores(nc, K, "dn_rounded", "dn_split", "dn_used", "dn_summed", "dn_out")
        raw_w = ctx.enter_context(nc.sbuf_tensor("dn_w", [P, S, D], FP32))
        raw_p = ctx.enter_context(nc.sbuf_tensor("dn_p", [P, S, HALF], FP32))
        w = Halves(nc, ctx, "dn_w", [P, S, D])
        p = Halves(nc, ctx, "dn_p", [P, S, HALF])
        w_v = K.dram["w_down"][0]
        PEEL = NF - 5 * S
        assert PEEL == 2 and S % 2 == 0

        def chunks(eng, body):
            for g in range(2):
                base = g * NF
                for k in range(PEEL):
                    body(g, k, base + k, (base + k) % S, k == 0, False)
                with eng.Fori(0, (NF - PEEL) // S - 1) as it:
                    for j in range(S):
                        body(g, it * S + (PEEL + j), it * S + (base + PEEL + j), (base + PEEL + j) % S, False, False)
                for j in range(S):
                    k = NF - S + j
                    body(g, k, base + k, (base + k) % S, False, j == S - 1)

        with nc.Block(no_gpsimd_drain=True) as block:

            @block.sync
            def _(sync):
                sync.sem_inc(split, S)
                seen = [0] * S

                def body(g, k, n, q, *_):
                    sync.wait_ge(split, n + 1)
                    sync.dma_start(raw_w[:, q, :], w_v[bass.ds(k * P, P), :]).then_inc(loaded[q], 16)
                    sync.dma_start(raw_p[:, q, :], K.scr["p"][bass.ds(k * P, P), g * HALF:(g + 1) * HALF]).then_inc(loaded[q], 16)
                chunks(sync, body)

            @block.scalar
            def _(act):
                act.sem_inc(used, S)

                def body(g, k, n, q, *_):
                    act.wait_ge(loaded[q], (n - q) * (32 // S) + 32)
                    act.wait_ge(used, n + 1)
                    act.activation(p.hi[:, q, :], raw_p[:, q, :], ACT.Copy)
                    act.activation(w.hi[:, q, :], raw_w[:, q, :], ACT.Copy).then_inc(rounded, 1)
                chunks(act, body)

            @block.tensor
            def _(pe):
                def body(g, k, n, q, first, last):
                    pe.wait_ge(split, n + (S + 1))
                    for j in range(KD):
                        if first:
                            pe.wait_ge(out, 8 * g + j + 1)
                        cols = slice(j * P, (j + 1) * P)
                        ins = three_products(pe, K.ps[:, j, :], w.hi[:, q, cols], w.lo[:, q, cols], p.hi[:, q, :],
                                             p.lo[:, q, :], first, last)
                        if last:
                            ins.then_inc(summed, 1)
                    if not last:
                        ins.then_inc(used, 1)
                chunks(pe, body)

            @block.vector
            def _(dve):
                dve.sem_inc(out, KD)

                def body(g, k, n, q, first, last):
                    dve.wait_ge(rounded, n + 1)
                    dve.tensor_tensor(p.lo[:, q, :], raw_p[:, q, :], p.hi[:, q, :], ALU.subtract)
                    dve.tensor_tensor(w.lo[:, q, :], raw_w[:, q, :], w.hi[:, q, :], ALU.subtract).then_inc(split, 1)
                    if last:
                        for j in range(KD):
                            dve.wait_ge(summed, 8 * g + j + 1)
                            x = K.xT[:, j, g * HALF:(g + 1) * HALF]
                            dve.tensor_tensor(x, K.ps[:, j, :], x, ALU.add).then_inc(out, 1)
                            if j == KD - 1:
                                dve.sem_inc(used, 1)
                chunks(dve, body)


def common(nc, ctx, K):
    def sb(name, shape, dt=FP32):
        return ctx.enter_context(nc.sbuf_tensor(name, shape, dt))
    K.col = {}
    K.sems = []
    K.ps = ctx.enter_context(nc.psum_tensor("ps", [P, 8, HALF], FP32))
    K.ones = sb("ones", [P, P])
    K.ident = sb("ident", [P, P])
    K.upper = sb("upper", [P, P])
    K.level = sb("level", [P, 8, P])
    K.eps_rms = sb("eps_rms", [P, 1])
    K.eps_ln = sb("eps_ln", [P, 1])
    K.par = sb("par", [P, len(PARAM_ROWS) * P])
    K.xT = sb("xT", [P, KD, SEQ])


def first_block(nc, K):
    stage_load_x(nc, K)
    with ExitStack() as ctx:
        hT = Halves(nc, ctx, "hT", [P, KD, SEQ])
        with ExitStack() as inner:
            y = inner.enter_context(nc.sbuf_tensor("y", [P, KD, SEQ], FP32))
            stage_mixer(nc, K, hT, y)
            stage_layernorm_silu(nc, K, y[:, 4:8, :])
            stage_residual(nc, K, "wo", y, 0, hT, K.dram["w_out"][0])
        stage_ffn(nc, K, hT)
    stage_down(nc, K)
    stage_rmsnorm(nc, K, "n3", "norm_final_g", halves(K.xT, K.xT))



META = 16
N_CHUNK = 1 + SEQ // P
LEN = N_CHUNK * P
LEAD = P - META
HEADS = 4
HW = HEADS * P
COL = dict(hq=0, hf=512, hi=1024, hg=1536, gq=2048, gk=2560, gv=3072, gz=3584, beta=4096, pre_ga=4104, pre_gb=5128)
QUART = (META + SEQ) // 4


def stage_meta(nc, K, metaT):
    with ExitStack() as ctx:
        loaded, turned, out = semaphores(nc, K, "meta_loaded", "meta_turned", "meta_out")
        rows = ctx.enter_context(nc.sbuf_tensor("meta_rows", [META, D], FP32))
        with nc.Block(no_gpsimd_drain=True) as block:

            @block.sync
            def _(sync):
                sync.dma_start(rows[:], K.dram["meta_tokens_2"]).then_inc(loaded, 16)

            @block.tensor
            def _(pe):
                pe.wait_ge(loaded, 16)
                for k in range(KD):
                    last = pe.transpose(K.ps[:, 0, k * META:(k + 1) * META], rows[:, k * P:(k + 1) * P],
                                        K.ident[0:META, 0:META])
                last.then_inc(turned, 1)

            @block.scalar
            def _(act):
                act.wait_ge(turned, 1)
                act.activation(metaT[:].rearrange("p k t -> p (k t)"), K.ps[:, 0, 0:KD * META], ACT.Copy).then_inc(out, 1)


def stage_lower_bounds(nc, K, lb):
    with ExitStack() as ctx:
        step, exped = semaphores(nc, K, "lb_step", "lb_exped")
        t = ctx.enter_context(nc.sbuf_tensor("lb_t", [P, 6, HEADS], FP32))
        c = K.col["hg_lb_logits_2"]
        with nc.Block(no_gpsimd_drain=True) as block:

            @block.vector
            def _(dve):
                row = [K.par[:, c + 4 * r:c + 4 * r + 4] for r in range(2)]
                dve.tensor_tensor(t[:, 0, :], row[0], row[1], ALU.max).then_inc(step, 1)
                dve.wait_ge(step, 1)
                dve.tensor_tensor(t[:, 1, :], row[0], t[:, 0, :], ALU.subtract)
                dve.tensor_tensor(t[:, 2, :], row[1], t[:, 0, :], ALU.subtract).then_inc(step, 1)
                dve.wait_ge(exped, 1)
                dve.tensor_tensor(t[:, 5, :], t[:, 3, :], t[:, 4, :], ALU.add).then_inc(step, 1)
                dve.wait_ge(step, 3)
                dve.reciprocal(t[:, 0, :], t[:, 5, :]).then_inc(step, 1)
                dve.wait_ge(step, 4)
                dve.tensor_tensor(lb[:, 0:4], t[:, 3, :], t[:, 0, :], ALU.mult).then_inc(step, 1)
                dve.wait_ge(step, 5)
                dve.tensor_scalar(lb[:, 4:8], lb[:, 0:4], -1.0, 1.0, ALU.mult, ALU.add)

            @block.scalar
            def _(act):
                act.wait_ge(step, 2)
                act.activation(t[:, 3:5, :], t[:, 1:3, :], ACT.Exp).then_inc(exped, 1)


def stage_forget(nc, K, hT, lb):
    with ExitStack() as ctx:
        free = semaphores(nc, K, "fg_free0", "fg_free1")
        padded, zero_out, forget, keyed, logged, summed, stored = semaphores(
            nc, K, "fg_padded", "fg_zero_out", "fg_forget", "fg_keyed", "fg_logged", "fg_summed", "fg_stored")
        W = Weights(nc, K, ctx, "fg", 2, KD)
        keep = ctx.enter_context(nc.sbuf_tensor("fg_keep", [P, LEN], FP32))
        f = ctx.enter_context(nc.sbuf_tensor("fg_f", [P, 2, LEN - LEAD], FP32))
        k_st = ctx.enter_context(nc.sbuf_tensor("fg_k", [P, 2, LEN], FP32))
        b_st = ctx.enter_context(nc.sbuf_tensor("fg_b", [P, 2, LEN], FP32))
        lf = ctx.enter_context(nc.sbuf_tensor("fg_lf", [P, 2, LEN], FP32))
        zero = ctx.enter_context(nc.sbuf_tensor("fg_zero", [P, P], FP32))
        w_v = K.dram["w_in_2"][0].rearrange("(k p) e -> p k e", p=P)
        with nc.Block(no_gpsimd_drain=True) as block:

            @block.sync
            def _(sync):
                W.start(sync)
                with sync.Fori(0, 2) as it:
                    for q in range(2):
                        W.load(sync, q, it, w_v[:, :, bass.ds(COL["hf"] + q * P + it * (2 * P), P)])

            @block.tensor
            def _(pe):
                with pe.Fori(0, 2) as it:
                    for q in range(2):
                        pe.wait_ge(free[q], it + 1)
                        project(pe, K.ps, 4 * q, W, q, it, hT, [QUART] * 4, LEAD)

            @block.scalar
            def _(act):
                for q in range(2):
                    act.sem_inc(free[q], 1)
                act.sem_inc(stored, 64)
                for q in range(2):
                    W.round(act, q, 0)
                act.wait_ge(padded, 1)
                for it in range(2):
                    for q in range(2):
                        act.wait_ge(W.done[q], it + 2)
                        act.activation(f[:, q, :].rearrange("p (b n) -> p b n", b=4),
                                       K.ps[:, 4 * q:4 * q + 4, 0:QUART], ACT.Sigmoid).then_inc(free[q], 1)
                        if it == 0:
                            W.round(act, q, 1)
                    for q in range(2):
                        act.wait_ge(forget, 2 * it + q + 1)
                        act.activation(lf[:, q, LEAD:], f[:, q, :], ACT.Ln).then_inc(logged, 1)
                    for q in range(2):
                        rows = bass.ds(q * P + it * (2 * P), P)
                        act.wait_ge(keyed, 2 * it + q + 1)
                        act.dma_start(K.scr["k_a"][rows, :], k_st[:, q, :]).then_inc(stored, 16)
                    for q in range(2):
                        rows = bass.ds(q * P + it * (2 * P), P)
                        act.wait_ge(summed, 2 * it + q + 1)
                        act.dma_start(K.scr["b_a"][rows, :], b_st[:, q, :]).then_inc(stored, 16)
                act.wait_ge(stored, 3 * 64)

            @block.vector
            def _(dve):
                with dve.Fori(0, 2) as it:
                    for q in range(2):
                        dve.wait_ge(free[q], it + 2)
                        i = 2 * it + q
                        dve.tensor_scalar(f[:, q, :], f[:, q, :], lb[:, bass.ds(i + 4, 1)], lb[:, bass.ds(i, 1)],
                                          ALU.mult, ALU.add).then_inc(forget, 1)
                        dve.wait_ge(forget, 2 * it + q + 1)
                        dve.wait_ge(stored, 64 * it + 64)
                        dve.tensor_scalar(k_st[:, q, LEAD:], f[:, q, :], -1.0, 1.0, ALU.mult, ALU.add).then_inc(keyed, 1)
                    for q in range(2):
                        dve.wait_ge(logged, 2 * it + q + 1)
                        dve.tensor_tensor_scan(b_st[:, q, :], keep[:], lf[:, q, :], 0.0, ALU.mult,
                                               ALU.add).then_inc(summed, 1)
                    dve.wait_ge(summed, 2 * it + 2)

            @block.gpsimd
            def _(gp):
                gp.memset(keep[:].rearrange("p (c t) -> p c t", t=P)[:, :, 0:1], 0.0)
                gp.memset(keep[:].rearrange("p (c t) -> p c t", t=P)[:, :, 1:], 1.0)
                gp.memset(zero[:], 0.0)
                gp.memset(k_st[:, :, 0:LEAD], 0.0)
                gp.memset(lf[:, :, 0:LEAD], 0.0).then_inc(padded, 1)
                gp.wait_ge(padded, 1)
                for it in range(2):
                    for q in range(2):
                        W.rest(gp, q, it)
                for i in range(HEADS):
                    gp.dma_start(K.scr["q_a"][i * P:(i + 1) * P, 0:P], zero[:]).then_inc(zero_out, 16)
                gp.wait_ge(zero_out, 16 * HEADS)


def stage_by_tokens(nc, K, hT, G, beta):
    with ExitStack() as ctx:
        wl, sl, done, out, stored, gated, step, acted = semaphores(
            nc, K, "bt_w_in", "bt_small_in", "bt_done", "bt_out", "bt_stored", "bt_gated", "bt_step", "bt_acted")
        w = ctx.enter_context(nc.sbuf_tensor("bt_w", [P, KD, HW], FP32))
        wg = ctx.enter_context(nc.sbuf_tensor("bt_wg", [P, KD, 2 * HEADS], FP32))
        wp = Halves(nc, ctx, "bt_w", [P, KD, HW])
        wgp = Halves(nc, ctx, "bt_wg", [P, KD, 2 * HEADS])
        rounded, split = semaphores(nc, K, "bt_w_rounded", "bt_w_split")
        st = ctx.enter_context(nc.sbuf_tensor("bt_st", [P, 4, HW], FP32))
        a_log = ctx.enter_context(nc.sbuf_tensor("bt_a_log", [P, HEADS], FP32))
        dt = ctx.enter_context(nc.sbuf_tensor("bt_dt", [P, HEADS], FP32))
        t = ctx.enter_context(nc.sbuf_tensor("bt_t", [P, 6, N_CHUNK, HEADS], FP32))
        w_v = K.dram["w_in_2"][0].rearrange("(k p) e -> p k e", p=P)

        def over_chunks(x):
            return x[:].rearrange("p (a h) -> p a h", a=1).to_broadcast([P, N_CHUNK, HEADS])
        with nc.Block(no_gpsimd_drain=True) as block:

            @block.sync
            def _(sync):
                sync.dma_start(w[:], w_v[:, :, COL["hi"]:COL["hi"] + HW]).then_inc(wl, 16)
                sync.dma_start(wg[:], w_v[:, :, COL["beta"]:COL["beta"] + 2 * HEADS]).then_inc(sl, 16)
                sync.dma_start(a_log[:], K.dram["gd_A_log_2"].to_broadcast([P, HEADS])).then_inc(sl, 16)
                sync.dma_start(dt[:], K.dram["gd_dt_bias_2"].to_broadcast([P, HEADS])).then_inc(sl, 16)

            @block.tensor
            def _(pe):
                for c in range(N_CHUNK):
                    if c >= 6:
                        pe.wait_ge(out, c - 5)
                    for k in range(KD):
                        pe.wait_ge(split, k + 1)
                        cols = slice(c * P, (c + 1) * P)
                        last = three_products(pe, K.ps[:, c % 6, :], hT.hi[:, k, cols], hT.lo[:, k, cols],
                                              wp.hi[:, k, :], wp.lo[:, k, :], k == 0, k == KD - 1)
                    last.then_inc(done, 1)
                pe.wait_ge(split, KD + 1)
                for c in range(N_CHUNK):
                    for k in range(KD):
                        cols = slice(c * P, (c + 1) * P)
                        last = three_products(pe, K.ps[:, 7, 8 * c:8 * c + 8], hT.hi[:, k, cols], hT.lo[:, k, cols],
                                              wgp.hi[:, k, :], wgp.lo[:, k, :], k == 0, k == KD - 1)
                last.then_inc(gated, 1)
                pe.wait_ge(step, 5)
                pe.matmul(K.ps[:, 6, 0:N_CHUNK * HEADS], K.upper[:], t[:, 5, :, :].rearrange("p c h -> p (c h)"),
                          start=True, stop=True).then_inc(gated, 1)

            @block.scalar
            def _(act):
                act.wait_ge(wl, 16)
                for k in range(KD):
                    act.activation(wp.hi[:, k, :], w[:, k, :], ACT.Copy).then_inc(rounded, 1)
                act.wait_ge(sl, 48)
                act.activation(wgp.hi[:], wg[:], ACT.Copy).then_inc(rounded, 1)
                for c in range(N_CHUNK):
                    act.wait_ge(done, c + 1)
                    if c >= 4:
                        act.wait_ge(stored, 16 * (c - 3))
                    act.activation(st[:, c % 4, :], K.ps[:, c % 6, :], ACT.Copy).then_inc(out, 1)
                act.wait_ge(gated, 1)
                view = K.ps[:, 7, 0:8 * N_CHUNK].rearrange("p (c j) -> p c j", j=8)
                act.wait_ge(step, 1)
                act.activation(beta[:], view[:, :, 0:HEADS], ACT.Sigmoid).then_inc(acted, 1)
                act.wait_ge(step, 2)
                act.activation(t[:, 2, :, :], t[:, 1, :, :], ACT.Exp).then_inc(acted, 1)
                act.activation(a_log[:], a_log[:], ACT.Exp).then_inc(acted, 1)
                act.wait_ge(acted, 3)
                act.activation(t[:, 3, :, :], t[:, 2, :, :], ACT.Ln, bias=K.ones[:, 0:1]).then_inc(acted, 1)
                act.wait_ge(gated, 2)
                act.activation(G[:].rearrange("p c h -> p (c h)"), K.ps[:, 6, 0:N_CHUNK * HEADS], ACT.Copy).then_inc(acted, 1)

            @block.vector
            def _(dve):
                for k in range(KD):
                    dve.wait_ge(rounded, k + 1)
                    dve.tensor_tensor(wp.lo[:, k, :], w[:, k, :], wp.hi[:, k, :], ALU.subtract).then_inc(split, 1)
                dve.wait_ge(rounded, KD + 1)
                dve.tensor_tensor(wgp.lo[:], wg[:], wgp.hi[:], ALU.subtract).then_inc(split, 1)
                dve.wait_ge(gated, 1)
                view = K.ps[:, 7, 0:8 * N_CHUNK].rearrange("p (c j) -> p c j", j=8)
                dve.tensor_tensor(t[:, 0, :, :], view[:, :, HEADS:], over_chunks(dt), ALU.add).then_inc(step, 1)
                dve.wait_ge(step, 1)
                dve.scalar_tensor_tensor(out=t[:, 1, :, :], in0=t[:, 0, :, :], scalar=-1.0, in1=t[:, 0, :, :],
                                         op0=ALU.mult, op1=ALU.min).then_inc(step, 1)
                dve.wait_ge(acted, 4)
                dve.scalar_tensor_tensor(out=t[:, 4, :, :], in0=t[:, 0, :, :], scalar=0.0, in1=t[:, 3, :, :],
                                         op0=ALU.max, op1=ALU.add).then_inc(step, 1)
                dve.wait_ge(step, 3)
                dve.scalar_tensor_tensor(out=t[:, 5, :, :], in0=t[:, 4, :, :], scalar=-1.0, in1=over_chunks(a_log),
                                         op0=ALU.mult, op1=ALU.mult).then_inc(step, 2)

            @block.gpsimd
            def _(gp):
                for c in range(N_CHUNK):
                    gp.wait_ge(out, c + 1)
                    gp.dma_start(K.scr["v_a"][c * P:(c + 1) * P, :], st[:, c % 4, :]).then_inc(stored, 16)
                    gp.wait_ge(stored, 16 * (c + 1))


def stage_conv_qkv(nc, K, hT):
    TAPS = 4
    N = META + SEQ
    tiles = [(name, i) for name in ("gq", "gk", "gv") for i in range(HEADS)]
    scale = {"gq": P ** -0.5, "gk": 1.0}
    with ExitStack() as ctx:
        copied, conved, silued, squared, norm_done, rooted, inverted, ready, ready_v, stored, step, padded = semaphores(
            nc, K, "cv_copied", "cv_conved", "cv_silued", "cv_squared", "cv_norm_done",
            "cv_rooted", "cv_inverted", "cv_ready", "cv_ready_v", "cv_stored", "cv_step", "cv_padded")
        W = Weights(nc, K, ctx, "cv", 2, KD)
        cin = ctx.enter_context(nc.sbuf_tensor("cv_in", [P, 2, N + TAPS - 1], FP32))
        cv = ctx.enter_context(nc.sbuf_tensor("cv_cv", [P, 2, N], FP32))
        sq = ctx.enter_context(nc.sbuf_tensor("cv_sq", [P, 2, N], FP32))
        inv = ctx.enter_context(nc.sbuf_tensor("cv_inv", [P, N], FP32))
        st = ctx.enter_context(nc.sbuf_tensor("cv_st", [P, 2, LEN], FP32))
        w_v = K.dram["w_in_2"][0].rearrange("(k p) e -> p k e", p=P)
        n_norm = 2 * HEADS

        def banks(x, q):
            return x[:, 4 * q:4 * q + 4, 0:QUART]

        def quarters(x):
            return x.rearrange("p (b n) -> p b n", b=4)
        with nc.Block(no_gpsimd_drain=True) as block:

            @block.sync
            def _(sync):
                W.start(sync)
                for n, (name, i) in enumerate(tiles):
                    at = COL[name] + i * P
                    W.load(sync, n % 2, n // 2, w_v[:, :, at:at + P])

            @block.tensor
            def _(pe):
                for n in range(len(tiles) + 1):
                    if n < len(tiles):
                        if n >= 2:
                            if n - 2 < n_norm:
                                pe.wait_ge(rooted, n - 1)
                            else:
                                pe.wait_ge(copied, n - 1)
                        project(pe, K.ps, 4 * (n % 2), W, n % 2, n // 2, hT, [QUART] * 4, LEAD)
                    m = n - 1
                    if 0 <= m < n_norm:
                        pe.wait_ge(squared, m + 1)
                        for b in range(4):
                            last = pe.matmul(K.ps[:, 4 * (m % 2) + b, 0:QUART], K.ones[:],
                                             sq[:, m % 2, b * QUART:(b + 1) * QUART], start=True, stop=True)
                        last.then_inc(norm_done, 1)

            @block.scalar
            def _(act):
                act.wait_ge(padded, 1)
                W.round(act, 0, 0)
                W.round(act, 1, 0)
                for n in range(len(tiles) + 1):
                    if n < len(tiles):
                        act.wait_ge(W.done[n % 2], n // 2 + 2)
                        if n + 2 < len(tiles):
                            W.round(act, n % 2, n // 2 + 1)
                        if n >= 2:
                            act.wait_ge(conved, n - 1)
                        act.activation(quarters(cin[:, n % 2, TAPS - 1:]), banks(K.ps, n % 2), ACT.Copy).then_inc(copied, 1)
                    m = n - 1
                    if 0 <= m < n_norm:
                        act.wait_ge(norm_done, m + 1)
                        act.activation(quarters(sq[:, m % 2, :]), banks(K.ps, m % 2), ACT.Sqrt,
                                       bias=K.eps_rms[:, 0:1]).then_inc(rooted, 1)
                    if n < len(tiles):
                        act.wait_ge(conved, n + 1)
                        if n < n_norm:
                            act.activation(cv[:, n % 2, :], cv[:, n % 2, :], ACT.Silu).then_inc(silued, 1)
                            act.wait_ge(silued, n + 1)
                            if n >= 2:
                                act.wait_ge(inverted, n - 1)
                            act.activation(sq[:, n % 2, :], cv[:, n % 2, :], ACT.Square).then_inc(squared, 1)
                        else:
                            act.wait_ge(stored, 16 * (n - 1))
                            act.activation(st[:, n % 2, LEAD:], cv[:, n % 2, :], ACT.Silu).then_inc(ready_v, 1)

            @block.vector
            def _(dve):
                for n in range(len(tiles) + 1):
                    if n < len(tiles):
                        name, i = tiles[n]
                        c = 4 * ("gq", "gk", "gv").index(name) + i
                        dve.wait_ge(copied, n + 1)
                        if n >= 2:
                            if n - 2 < n_norm:
                                dve.wait_ge(ready, n - 1)
                            else:
                                dve.wait_ge(ready_v, n - 1 - n_norm)
                        for k in range(TAPS):
                            src = cin[:, n % 2, k:k + N]
                            tap = param(K, "gd_conv_w_2", 12 * k + c)
                            if k == 0:
                                ins = dve.tensor_scalar(cv[:, n % 2, :], src, tap, None, ALU.mult)
                            else:
                                ins = dve.scalar_tensor_tensor(out=cv[:, n % 2, :], in0=src, scalar=tap,
                                                               in1=cv[:, n % 2, :], op0=ALU.mult, op1=ALU.add)
                            if k < TAPS - 1:
                                ins.then_inc(step, 1)
                                dve.wait_ge(step, (TAPS - 1) * n + k + 1)
                            else:
                                ins.then_inc(conved, 1)
                    m = n - 1
                    if 0 <= m < n_norm:
                        dve.wait_ge(rooted, m + 1)
                        dve.reciprocal(inv[:], sq[:, m % 2, :]).then_inc(inverted, 1)
                        dve.wait_ge(inverted, m + 1)
                        if m >= 2:
                            dve.wait_ge(stored, 16 * (m - 1))
                        dve.scalar_tensor_tensor(out=st[:, m % 2, LEAD:], in0=cv[:, m % 2, :], scalar=scale[tiles[m][0]],
                                                 in1=inv[:], op0=ALU.mult, op1=ALU.mult).then_inc(ready, 1)

            @block.gpsimd
            def _(gp):
                gp.memset(cin[:, :, 0:TAPS - 1], 0.0)
                gp.memset(st[:, :, 0:LEAD], 0.0).then_inc(padded, 1)
                gp.wait_ge(padded, 1)
                W.rest(gp, 0, 0)
                W.rest(gp, 1, 0)
                for n, (name, i) in enumerate(tiles):
                    if n + 2 < len(tiles):
                        W.rest(gp, n % 2, n // 2 + 1)
                    if n < n_norm:
                        gp.wait_ge(ready, n + 1)
                    else:
                        gp.wait_ge(ready_v, n + 1 - n_norm)
                    gp.dma_start(K.scr[name][i * P:(i + 1) * P, :], st[:, n % 2, :]).then_inc(stored, 16)
                    gp.wait_ge(stored, 16 * (n + 1))


def stage_gates(nc, K, hT, metaT):
    groups = [("hq", 4, ACT.Silu, K.scr["q_a"][:, P:]), ("hg", 4, ACT.Silu, K.scr["gate"][0:HW, :]),
              ("gz", 4, ACT.Silu, K.scr["gate"][HW:, :]), ("pre_ga", 8, ACT.Sigmoid, K.scr["merge_a"]),
              ("pre_gb", 8, ACT.Sigmoid, K.scr["merge_b"])]
    with ExitStack() as ctx:
        norm = RmsNorm(nc, K, ctx, "n4", "norm_mix_g_2", [(K.xT, 0, hT, P, HALF), (K.xT, HALF, hT, P + HALF, HALF),
                                                          (metaT, 0, hT, LEAD, META)])
        free = semaphores(nc, K, *[f"ga_free{q}" for q in range(4)])
        stored = semaphores(nc, K, *[f"ga_stored{q}" for q in range(4)])
        W = Weights(nc, K, ctx, "ga", 4, KD)
        st = ctx.enter_context(nc.sbuf_tensor("ga_st", [P, 4, SEQ], FP32))
        w_v = K.dram["w_in_2"][0].rearrange("(k p) e -> p k e", p=P)

        def turns(eng, body):
            base = 0
            for g in groups:
                for it in range(g[1] // 4):
                    body(g, it, it + base)
                base += g[1] // 4
        total = sum(g[1] // 4 for g in groups)
        with nc.Block(no_gpsimd_drain=True) as block:

            @block.sync
            def _(sync):
                W.start(sync)

                def body(g, it, n):
                    for q in range(4):
                        W.load(sync, q, n, w_v[:, :, bass.ds(it * (4 * P) + (COL[g[0]] + q * P), P)])
                turns(sync, body)

            @block.gpsimd
            def _(gp):
                for q in range(4):
                    W.rest(gp, q, 0)
                norm.gpsimd(gp)
                with gp.Fori(1, total) as n:
                    for q in range(4):
                        W.rest(gp, q, n)

            @block.tensor
            def _(pe):
                norm.tensor(pe)
                with pe.Fori(0, total) as n:
                    for q in range(4):
                        pe.wait_ge(free[q], n + 1)
                        if q == 2:
                            pe.wait_ge(norm.rooted, 3)
                        project(pe, K.ps, 2 * q, W, q, n, hT, [HALF, HALF], P, ready=norm.ready)

            @block.scalar
            def _(act):
                for q in range(4):
                    act.sem_inc(free[q], 1)
                    act.sem_inc(stored[q], 16)
                for q in range(4):
                    W.round(act, q, 0)
                norm.scalar(act)

                def body(g, it, n):
                    for q in range(4):
                        act.wait_ge(W.done[q], n + 2)
                        act.wait_ge(stored[q], n * 16 + 16)
                        act.activation(st[:, q, :], pair(K.ps, q), g[2]).then_inc(free[q], 1)
                        if not (isinstance(n, int) and n == total - 1):
                            W.round(act, q, n + 1)
                        act.wait_ge(free[q], n + 2)
                        act.dma_start(g[3][bass.ds(it * (4 * P) + q * P, P), :], st[:, q, :]).then_inc(stored[q], 16)
                turns(act, body)
                for q in range(4):
                    act.wait_ge(stored[q], 16 * (total + 1))

            @block.vector
            def _(dve):
                norm.vector(dve)


def second_projections(nc, K, G, beta):
    with ExitStack() as ctx:
        metaT = ctx.enter_context(nc.sbuf_tensor("metaT", [P, KD, META], FP32))
        lb = ctx.enter_context(nc.sbuf_tensor("lb", [P, 2 * HEADS], FP32))
        hT = Halves(nc, ctx, "hT2", [P, KD, LEN])
        zeroed, = semaphores(nc, K, "lead_zeroed")
        stage_meta(nc, K, metaT)
        with nc.Block(no_gpsimd_drain=True) as block:

            @block.gpsimd
            def _(gp):
                gp.memset(hT.hi[:, :, 0:LEAD].bitcast(FP32), 0.0)
                gp.memset(hT.lo[:, :, 0:LEAD].bitcast(FP32), 0.0).then_inc(zeroed, 1)
                gp.wait_ge(zeroed, 1)
        stage_gates(nc, K, hT, metaT)
        stage_lower_bounds(nc, K, lb)
        stage_forget(nc, K, hT, lb)
        stage_by_tokens(nc, K, hT, G, beta)
        stage_conv_qkv(nc, K, hT)


def scratch(nc):
    shapes = dict(q_a=(HW, LEN), k_a=(HW, LEN), b_a=(HW, LEN), v_a=(LEN, HW), gq=(HW, LEN), gk=(HW, LEN), gv=(HW, LEN),
                  gate=(2 * HW, SEQ), p=(DFF, SEQ), merge_a=(D, SEQ), merge_b=(D, SEQ))
    scr = {n: nc.dram_tensor(f"scr_{n}", s, FP32, kind="Internal").ap() for n, s in shapes.items()}
    scr["h2"] = nc.dram_tensor("scr_h2", (SEQ, D), FP32, kind="Internal").ap()
    scr["y"] = nc.dram_tensor("scr_y", (N_BLOCK * P, D), FP32, kind="Internal").ap()
    scr["row_table"] = nc.dram_tensor("scr_row_table", (N_BLOCK * P, 1), I32, kind="Internal").ap()
    return scr



LEVELS = 7

EVENTS = dict(
    in_g=48, in_a=48, in_v=16,
    bc_ready=1, kq_ready=7, m_ready=7, added=7, qeb_ready=1, kdt_ready=1,
    eg_ready=1, rt_exp=1, ege_ready=1, eb_ready=1, e_ready=7, edb_ready=1, kd_ready=1, kda_ready=1,
    pm_ready=6, rs_ready=1, us_ready=1, og_out=1, oa_out=1,
    kb_ready=1, rt_ready=1, vb_ready=1, nk_ready=1, qe_ready=1, rt_masked=1, lt_ready=1, at_ready=1,
    d_ready=7, dbe_ready=1, masked=8, xy=7, sg_ready=1, sa_ready=1,
    bcast_done=1, kk_done=1, kq_done=1, lev_done=8, m1t_done=1, p_done=6, dxy_done=6, kdat_done=1,
    r_done=1, u_done=1, o_done=1, dsg_done=1, oa_done=1, dsa_done=1)
MAKER = dict(sync="in_g in_a in_v", gpsimd="bc_ready kq_ready m_ready added qeb_ready kdt_ready",
             scalar="eg_ready rt_exp ege_ready eb_ready e_ready edb_ready kd_ready kda_ready pm_ready rs_ready us_ready og_out oa_out",
             vector="kb_ready rt_ready vb_ready nk_ready qe_ready rt_masked lt_ready at_ready d_ready dbe_ready masked xy sg_ready sa_ready",
             tensor="bcast_done kk_done kq_done lev_done m1t_done p_done dxy_done kdat_done r_done u_done o_done dsg_done oa_done dsa_done")


def stage_recurrences(nc, K, G, beta, oT):
    C4 = [P, HEADS, P]
    with ExitStack() as ctx:
        ev = {n: semaphores(nc, K, f"rc_{n}")[0] for n in EVENTS}

        def buf(name, n=0):
            shape = [P, n, HEADS, P] if n else C4
            return ctx.enter_context(nc.sbuf_tensor(f"rc_{name}", shape, FP32))

        q_a, k_a, b_a, v_a, q_g, k_g, v_g = [buf(n) for n in ("q_a", "k_a", "b_a", "v_a", "q_g", "k_g", "v_g")]
        Gb, Bb, eG, kb, nkbe, vb, qe = [buf(n) for n in ("Gb", "Bb", "eG", "kb", "nkbe", "vb", "qe")]
        rT, LT, aT, kd, Rs, us, Pm, X, Y = [buf(n) for n in ("rT", "LT", "aT", "kd", "Rs", "us", "Pm", "X", "Y")]
        M = buf("M", LEVELS)
        KQ = buf("KQ", LEVELS)
        Dl = buf("D", 2)
        El = buf("E", 2)
        edb, eb, qeb, kdT, kda, A = [buf(n) for n in ("edb", "eb", "qeb", "kdT", "kda", "A")]
        tmp = buf("tmp", 2)
        Sa, Sg = buf("Sa"), buf("Sg")
        ge = ctx.enter_context(nc.sbuf_tensor("rc_ge", [P, 2, HEADS], FP32))
        s_zero, = semaphores(nc, K, "rc_state_zero")

        def bank(n):
            return K.ps[:, n, :].rearrange("p (h t) -> p h t", h=HEADS)

        def all_heads(m):
            return m.rearrange("p (a t) -> p a t", a=1).to_broadcast(C4)

        def column(x, c):
            return x[:, bass.ds(c, 1), :].rearrange("p a (h b) -> p (a h) b", b=1).to_broadcast(C4)

        def halves_of(x, lev):
            m = 1 << lev
            v = x.rearrange("p h t -> p (h t)").rearrange("p (b s i) -> p b s i", s=2, i=m // 2)
            return v[:, :, 0, :], v[:, :, 1, :]

        def middle(x, lev):
            m = 1 << lev
            v = x.rearrange("p h t -> p (h t)").rearrange("p (b i) -> p b i", i=m)[:, :, m // 2 - 1:m // 2]
            return v.to_broadcast([P, HEADS * P // m, m // 2])

        def start(eng, kind):
            for n in MAKER[kind].split():
                eng.sem_inc(ev[n], EVENTS[n])

        def wait(eng, c, name, k=None):
            per = EVENTS[name]
            eng.wait_ge(ev[name], c * per + per + (per if k is None else k))

        def wait_before(eng, c, *names):
            for name in names:
                eng.wait_ge(ev[name], c * EVENTS[name] + EVENTS[name])

        LAST = ("dsa_done", "sa_ready", "oa_out", "kdt_ready", "qeb_ready", "added")

        def over_chunks(eng, kind, body):
            start(eng, kind)
            with eng.Fori(0, N_CHUNK) as c:
                if kind != "sync":
                    wait_before(eng, c, *LAST)
                body(c)

        with nc.Block(no_gpsimd_drain=True) as block:

            @block.sync
            def _(sync):
                def by_channels(name, c):
                    return K.scr[name].rearrange("(h p) t -> p h t", p=P)[:, :, bass.ds(c * P, P)]

                def body(c):
                    wait_before(sync, c, "kq_done", "kb_ready", "vb_ready", "qe_ready")
                    for x, n in ((q_g, "gq"), (k_g, "gk"), (v_g, "gv")):
                        sync.dma_start(x[:], by_channels(n, c)).then_inc(ev["in_g"], 16)
                    wait_before(sync, c, "lev_done", "kq_ready", "dbe_ready", "d_ready", "qeb_ready", "kdt_ready", "eb_ready")
                    for x, n in ((q_a, "q_a"), (k_a, "k_a"), (b_a, "b_a")):
                        sync.dma_start(x[:], by_channels(n, c)).then_inc(ev["in_a"], 16)
                    wait_before(sync, c, "dsa_done")
                    sync.dma_start(v_a[:].rearrange("p h v -> p (h v)"), K.scr["v_a"][bass.ds(c * P, P), :]
                                   ).then_inc(ev["in_v"], 16)
                over_chunks(sync, "sync", body)

            @block.gpsimd
            def _(gp):
                gp.memset(Sa[:], 0.0)
                gp.memset(Sg[:], 0.0).then_inc(s_zero, 1)

                def body(c):
                    gp.tensor_copy(Gb[:], column(G, c))
                    gp.tensor_copy(Bb[:], column(beta, c)).then_inc(ev["bc_ready"], 1)

                    def kq(lev):
                        wait(gp, c, "e_ready", lev)
                        if lev == 1:
                            wait(gp, c, "in_a")
                        e = halves_of(El[:, lev % 2], lev)
                        for half, src in ((0, k_a), (1, q_a)):
                            ins = gp.tensor_tensor(halves_of(KQ[:, lev - 1], lev)[half], halves_of(src[:], lev)[half],
                                                   e[half], ALU.mult)
                        ins.then_inc(ev["kq_ready"], 1)

                    def m_level(lev):
                        if lev == 1:
                            wait(gp, c, "lt_ready")
                        gp.tensor_tensor(M[:, lev - 1], LT[:], all_heads(K.level[:, lev, :]), ALU.mult
                                         ).then_inc(ev["m_ready"], 1)

                    def add(lev):
                        wait(gp, c, "masked", lev + 1)
                        if lev > 1:
                            wait(gp, c, "added", lev - 1)
                        gp.tensor_tensor(A[:], A[:], tmp[:, lev % 2], ALU.add).then_inc(ev["added"], 1)

                    kq(1)
                    kq(2)
                    m_level(1)
                    m_level(2)
                    for lev in range(3, LEVELS + 1):
                        kq(lev)
                        add(lev - 2)
                        m_level(lev)
                    wait(gp, c, "eb_ready")
                    gp.tensor_tensor(qeb[:], q_a[:], eb[:], ALU.mult).then_inc(ev["qeb_ready"], 1)
                    wait(gp, c, "edb_ready")
                    gp.tensor_tensor(kdT[:], k_a[:], edb[:], ALU.mult).then_inc(ev["kdt_ready"], 1)
                    add(LEVELS - 1)
                    add(LEVELS)
                over_chunks(gp, "gpsimd", body)

            @block.scalar
            def _(act):
                def body(c):
                    def exp_level(lev):
                        wait(act, c, "d_ready", lev)
                        if lev > 2:
                            wait(act, c, "kq_ready", lev - 2)
                        act.activation(El[:, lev % 2], Dl[:, lev % 2], ACT.Exp).then_inc(ev["e_ready"], 1)

                    wait(act, c, "bcast_done")
                    act.activation(eG[:], bank(0), ACT.Exp).then_inc(ev["eg_ready"], 1)
                    wait(act, c, "rt_ready")
                    act.activation(rT[:], rT[:], ACT.Exp).then_inc(ev["rt_exp"], 1)
                    act.activation(ge[:, 1, :], ge[:, 0, :], ACT.Exp).then_inc(ev["ege_ready"], 1)
                    exp_level(1)
                    exp_level(2)
                    wait(act, c, "kq_done")
                    wait(act, c, "ege_ready")
                    for h in range(HEADS):
                        ins = act.activation(kd[:, h, :], bank(4)[:, h, :], ACT.Copy, scale=ge[:, 1, h:h + 1])
                    ins.then_inc(ev["kd_ready"], 1)
                    wait(act, c, "in_a")
                    act.activation(eb[:], b_a[:], ACT.Exp).then_inc(ev["eb_ready"], 1)
                    exp_level(3)
                    wait(act, c, "r_done")
                    act.activation(Rs[:], bank(2), ACT.Copy).then_inc(ev["rs_ready"], 1)
                    for lev in range(2, LEVELS + 1):
                        wait(act, c, "p_done", lev - 1)
                        if lev > 2:
                            wait(act, c, "dxy_done", lev - 2)
                        act.activation(Pm[:], bank(5), ACT.Copy).then_inc(ev["pm_ready"], 1)
                        if lev + 2 <= LEVELS:
                            exp_level(lev + 2)
                        if lev == 5:
                            wait(act, c, "dbe_ready")
                            act.activation(edb[:], edb[:], ACT.Exp, scale=-1.0).then_inc(ev["edb_ready"], 1)
                    wait(act, c, "kdat_done")
                    act.activation(kda[:], bank(0), ACT.Copy).then_inc(ev["kda_ready"], 1)
                    wait(act, c, "u_done")
                    act.activation(us[:], bank(3), ACT.Copy).then_inc(ev["us_ready"], 1)
                    wait(act, c, "o_done")
                    act.activation(oT[:, HEADS:, bass.ds(c * P, P)], bank(4), ACT.Copy).then_inc(ev["og_out"], 1)
                    wait(act, c, "oa_done")
                    act.activation(oT[:, 0:HEADS, bass.ds(c * P, P)], bank(1), ACT.Copy).then_inc(ev["oa_out"], 1)
                over_chunks(act, "scalar", body)

            @block.vector
            def _(dve):
                def body(c):
                    def exponents(lev):
                        if lev == 1:
                            wait(dve, c, "in_a")
                        if lev > 2:
                            wait(dve, c, "e_ready", lev - 2)
                        left, right = halves_of(Dl[:, lev % 2], lev)
                        b_left, b_right = halves_of(b_a[:], lev)
                        dve.tensor_tensor(left, middle(b_a[:], lev), b_left, ALU.subtract)
                        dve.tensor_tensor(right, b_right, middle(b_a[:], lev), ALU.subtract).then_inc(ev["d_ready"], 1)

                    def mask(lev):
                        wait(dve, c, "lev_done", lev + 1)
                        if lev > 2:
                            wait(dve, c, "added", lev - 2)
                        dst = A[:] if lev == 0 else tmp[:, lev % 2]
                        dve.tensor_tensor(dst, bank(lev % 2), all_heads(K.level[:, lev, :]), ALU.mult
                                          ).then_inc(ev["masked"], 1)

                    wait(dve, c, "eg_ready")
                    wait(dve, c, "in_g")
                    dve.tensor_tensor(kb[:], k_g[:], bank(1), ALU.mult).then_inc(ev["kb_ready"], 1)
                    for h in range(HEADS):
                        dve.tensor_scalar(rT[:, h, :], bank(0)[:, h, :],
                                          G[:, bass.ds(c, 1), h:h + 1].rearrange("p a b -> p (a b)"), 0.0,
                                          ALU.subtract, ALU.min)
                    dve.tensor_tensor(ge[:, 0, :], K.ps[:, 0, P - 1::P], G[:, bass.ds(c, 1), :].rearrange("p a h -> p (a h)"),
                                      ALU.subtract).then_inc(ev["rt_ready"], 1)
                    dve.tensor_tensor(vb[:], v_g[:], bank(1), ALU.mult).then_inc(ev["vb_ready"], 1)
                    wait(dve, c, "kb_ready")
                    dve.scalar_tensor_tensor(out=nkbe[:], in0=kb[:], scalar=-1.0, in1=eG[:], op0=ALU.mult,
                                             op1=ALU.mult).then_inc(ev["nk_ready"], 1)
                    dve.tensor_tensor(qe[:], q_g[:], eG[:], ALU.mult).then_inc(ev["qe_ready"], 1)
                    exponents(1)
                    exponents(2)
                    wait(dve, c, "rt_exp")
                    dve.tensor_tensor(rT[:], rT[:], all_heads(K.upper[:]), ALU.mult).then_inc(ev["rt_masked"], 1)
                    wait(dve, c, "kk_done")
                    wait(dve, c, "rt_masked")
                    dve.tensor_tensor(LT[:], bank(2), rT[:], ALU.mult).then_inc(ev["lt_ready"], 1)
                    wait(dve, c, "kq_done")
                    dve.tensor_tensor(aT[:], bank(3), rT[:], ALU.mult).then_inc(ev["at_ready"], 1)
                    mask(0)
                    mask(1)
                    exponents(3)
                    wait(dve, c, "m_ready", 1)
                    wait(dve, c, "m1t_done")
                    dve.tensor_tensor(Y[:], all_heads(K.ident[:]), M[:, 0], ALU.subtract)
                    dve.tensor_tensor(X[:], all_heads(K.ident[:]), bank(5), ALU.subtract).then_inc(ev["xy"], 1)
                    for lev in range(2, LEVELS + 1):
                        mask(lev)
                        if lev + 2 <= LEVELS:
                            exponents(lev + 2)
                        if lev == 4:
                            for h in range(HEADS):
                                ins = dve.tensor_scalar(edb[:, h, :], b_a[:, h, :], b_a[:, h, P - 1:P], None, ALU.subtract)
                            ins.then_inc(ev["dbe_ready"], 1)
                        wait(dve, c, "dxy_done", lev - 1)
                        wait(dve, c, "xy", lev - 1)
                        if lev < LEVELS:
                            dve.tensor_tensor(X[:], X[:], bank(6), ALU.subtract)
                        dve.tensor_tensor(Y[:], Y[:], bank(7), ALU.subtract).then_inc(ev["xy"], 1)
                    for name, S, e, b in (("g", Sg, eG, 5), ("a", Sa, eb, 0)):
                        wait(dve, c, f"ds{name}_done")
                        for h in range(HEADS):
                            ins = dve.scalar_tensor_tensor(out=S[:, h, :], in0=S[:, h, :], scalar=e[:, h, P - 1:P],
                                                           in1=bank(b)[:, h, :], op0=ALU.mult, op1=ALU.add)
                        ins.then_inc(ev[f"s{name}_ready"], 1)
                over_chunks(dve, "vector", body)

            @block.tensor
            def _(pe):
                ident = K.ident[:]

                def heads(b, *terms):
                    for h in range(HEADS):
                        for n, (lhsT, rhs) in enumerate(terms):
                            r = ident if rhs is None else rhs[:, h, :]
                            last = pe.matmul(bank(b)[:, h, :], lhsT[:, h, :], r, start=(n == 0), stop=(n == len(terms) - 1))
                    return last

                def turn(b, x):
                    for h in range(HEADS):
                        last = pe.transpose(bank(b)[:, h, :], x[:, h, :], ident)
                    return last

                def body(c):
                    def level(lev):
                        if lev == 0:
                            wait(pe, c, "in_a")
                            wait(pe, c, "rt_ready")
                            heads(0, (k_a, q_a)).then_inc(ev["lev_done"], 1)
                            return
                        if lev == 1:
                            wait(pe, c, "vb_ready")
                        else:
                            wait(pe, c, "masked", lev - 1)
                        wait(pe, c, "kq_ready", lev)
                        x = KQ[:, lev - 1]
                        heads(lev % 2, (x, x)).then_inc(ev["lev_done"], 1)

                    wait(pe, c, "bc_ready")
                    heads(0, (Gb, None))
                    heads(1, (Bb, None)).then_inc(ev["bcast_done"], 1)
                    wait(pe, c, "in_g")
                    wait(pe, c, "kb_ready")
                    heads(2, (k_g, kb)).then_inc(ev["kk_done"], 1)
                    heads(3, (k_g, q_g))
                    turn(4, k_g).then_inc(ev["kq_done"], 1)
                    level(0)
                    level(1)
                    wait(pe, c, "m_ready", 1)
                    turn(5, M[:, 0]).then_inc(ev["m1t_done"], 1)
                    wait(pe, c, "nk_ready")
                    wait(pe, c, "lt_ready")
                    heads(2, (vb, None), (nkbe, Sg)).then_inc(ev["r_done"], 1)
                    for lev in range(2, LEVELS + 1):
                        wait(pe, c, "xy", lev - 1)
                        wait(pe, c, "m_ready", lev)
                        heads(5, (M[:, lev - 1], X)).then_inc(ev["p_done"], 1)
                        level(lev)
                        wait(pe, c, "pm_ready", lev - 1)
                        if lev < LEVELS:
                            heads(6, (Y, Pm))
                        heads(7, (Pm, Y)).then_inc(ev["dxy_done"], 1)
                    wait(pe, c, "kdt_ready")
                    wait(pe, c, "masked", LEVELS)
                    turn(0, kdT).then_inc(ev["kdat_done"], 1)
                    wait(pe, c, "xy")
                    wait(pe, c, "rs_ready")
                    wait(pe, c, "at_ready")
                    heads(3, (Y, Rs)).then_inc(ev["u_done"], 1)
                    wait(pe, c, "qeb_ready")
                    wait(pe, c, "added")
                    wait(pe, c, "masked")
                    wait(pe, c, "in_v")
                    heads(1, (Sa, qeb), (v_a, A)).then_inc(ev["oa_done"], 1)
                    wait(pe, c, "us_ready")
                    wait(pe, c, "qe_ready")
                    wait(pe, c, "kd_ready")
                    heads(4, (Sg, qe), (us, aT)).then_inc(ev["o_done"], 1)
                    heads(5, (kd, us)).then_inc(ev["dsg_done"], 1)
                    wait(pe, c, "kda_ready")
                    heads(0, (kda, v_a)).then_inc(ev["dsa_done"], 1)
                pe.wait_ge(s_zero, 1)
                over_chunks(pe, "tensor", body)


def stage_head_norm(nc, K, oT):
    n_tiles = 2 * HEADS
    with ExitStack() as ctx:
        squared, summed, rooted, inverted, scaled, gated = semaphores(
            nc, K, "hn_squared", "hn_summed", "hn_rooted", "hn_inverted", "hn_scaled", "hn_gated")
        gate_in = semaphores(nc, K, *[f"hn_gate_in{i}" for i in range(n_tiles)])
        gate = ctx.enter_context(nc.sbuf_tensor("hn_gate", [P, n_tiles, SEQ], FP32))
        sq = ctx.enter_context(nc.sbuf_tensor("hn_sq", [P, 2, HALF], FP32))
        root = ctx.enter_context(nc.sbuf_tensor("hn_root", [P, 2, HALF], FP32))
        inv = ctx.enter_context(nc.sbuf_tensor("hn_inv", [P, 2, HALF], FP32))
        units = [(i, P + h * HALF) for i in range(n_tiles) for h in range(2)]
        with nc.Block(no_gpsimd_drain=True) as block:

            @block.sync
            def _(sync):
                for i in range(n_tiles):
                    sync.dma_start(gate[:, i, :], K.scr["gate"][i * P:(i + 1) * P, :]).then_inc(gate_in[i], 16)

            @block.scalar
            def _(act):
                for n in range(len(units) + 1):
                    if n < len(units):
                        i, at = units[n]
                        if n >= 2:
                            act.wait_ge(summed, n - 1)
                        act.activation(sq[:, n % 2, :], oT[:, i, at:at + HALF], ACT.Square).then_inc(squared, 1)
                    if n >= 1:
                        m = n - 1
                        act.wait_ge(summed, m + 1)
                        if m >= 2:
                            act.wait_ge(inverted, m - 1)
                        act.activation(root[:, m % 2, :], K.ps[:, m % 8, :], ACT.Sqrt, bias=K.eps_rms[:, 0:1],
                                       scale=1.0 / P).then_inc(rooted, 1)

            @block.tensor
            def _(pe):
                for n in range(len(units)):
                    pe.wait_ge(squared, n + 1)
                    if n >= 8:
                        pe.wait_ge(rooted, n - 7)
                    pe.matmul(K.ps[:, n % 8, :], K.ones[:], sq[:, n % 2, :], start=True, stop=True).then_inc(summed, 1)

            @block.vector
            def _(dve):
                for n, (i, at) in enumerate(units):
                    dve.wait_ge(rooted, n + 1)
                    if n >= 2:
                        dve.wait_ge(scaled, n - 1)
                    dve.reciprocal(inv[:, n % 2, :], root[:, n % 2, :]).then_inc(inverted, 1)
                    dve.wait_ge(inverted, n + 1)
                    dve.scalar_tensor_tensor(out=oT[:, i, at:at + HALF], in0=oT[:, i, at:at + HALF],
                                             scalar=param(K, "hg_norm_g_2" if i < HEADS else "gd_norm_g_2"),
                                             in1=inv[:, n % 2, :], op0=ALU.mult, op1=ALU.mult).then_inc(scaled, 1)

            @block.gpsimd
            def _(gp):
                for n, (i, at) in enumerate(units):
                    gp.wait_ge(gate_in[i], 16)
                    gp.wait_ge(scaled, n + 1)
                    gp.tensor_tensor(oT[:, i, at:at + HALF], oT[:, i, at:at + HALF], gate[:, i, at - P:at - P + HALF],
                                     ALU.mult).then_inc(gated, 1)
                gp.wait_ge(gated, len(units))


def stage_merge(nc, K, oT, part):
    n_it = KD // 2
    with ExitStack() as ctx:
        gl = semaphores(nc, K, *[f"mg_gate_in{q}" for q in range(4)])
        free = semaphores(nc, K, *[f"mg_free{q}" for q in range(4)])
        merged, rounded, ready = semaphores(nc, K, "mg_merged", "mg_src_rounded", "mg_src_ready")
        W = Weights(nc, K, ctx, "mg", 4, HEADS)
        g = ctx.enter_context(nc.sbuf_tensor("mg_g", [P, 4, SEQ], FP32))
        w_v = [K.dram[n][0].rearrange("(k p) e -> p k e", p=P) for n in ("hg_up_2", "gd_up_2")]
        g_v = [K.scr[n] for n in ("merge_a", "merge_b")]
        with nc.Block(no_gpsimd_drain=True) as block:

            @block.sync
            def _(sync):
                W.start(sync)
                with sync.Fori(0, n_it) as it:
                    for q in range(4):
                        cols = bass.ds(q // 2 * P + it * (2 * P), P)
                        W.load(sync, q, it, w_v[q % 2][:, :, cols])
                        sync.wait_ge(merged, 2 * it + q // 2 + 1)
                        sync.dma_start(g[:, q, :], g_v[q % 2][cols, :]).then_inc(gl[q], 16)

            @block.scalar
            def _(act):
                for q in range(4):
                    W.round(act, q, 0)
                for k in range(2 * HEADS):
                    act.activation(part.hi[:, k, :], oT[:, k, P:], ACT.Copy).then_inc(rounded, 1)
                with act.Fori(1, n_it) as it:
                    for q in range(4):
                        W.round(act, q, it)

            @block.tensor
            def _(pe):
                pe.wait_ge(ready, 2 * HEADS)
                with pe.Fori(0, n_it) as it:
                    for q in range(4):
                        pe.wait_ge(free[q], it + 1)
                        side = slice(q % 2 * HEADS, (q % 2 + 1) * HEADS)
                        pe.wait_ge(W.split[q], it + 2)
                        for n in range(2):
                            cols = slice(n * HALF, (n + 1) * HALF)
                            for k in range(HEADS):
                                last = three_products(pe, K.ps[:, 2 * q + n, :], W.part.hi[:, q, k, :], W.part.lo[:, q, k, :],
                                                      part.hi[:, side, :][:, k, cols], part.lo[:, side, :][:, k, cols],
                                                      k == 0, k == HEADS - 1)
                        last.then_inc(W.done[q], 1)

            @block.vector
            def _(dve):
                for q in range(4):
                    dve.sem_inc(free[q], 1)
                for k in range(2 * HEADS):
                    dve.wait_ge(rounded, k + 1)
                    dve.tensor_tensor(part.lo[:, k, :], oT[:, k, P:], part.hi[:, k, :], ALU.subtract).then_inc(ready, 1)
                dve.wait_ge(ready, 2 * HEADS)
                with dve.Fori(0, n_it) as it:
                    for v in range(2):
                        for q in (2 * v, 2 * v + 1):
                            dve.wait_ge(W.done[q], it + 2)
                            dve.wait_ge(gl[q], 16 * it + 16)
                            dve.tensor_tensor(g[:, q, :], pair(K.ps, q), g[:, q, :], ALU.mult).then_inc(free[q], 1)
                        dve.wait_ge(free[2 * v + 1], it + 2)
                        dve.tensor_tensor(oT[:, bass.ds(2 * it + v, 1), P:], g[:, 2 * v:2 * v + 1, :],
                                          g[:, 2 * v + 1:2 * v + 2, :], ALU.add).then_inc(merged, 1)
                dve.wait_ge(merged, 2 + KD)

            @block.gpsimd
            def _(gp):
                gp.sem_inc(merged, 2)
                with gp.Fori(0, n_it) as it:
                    for q in range(4):
                        W.rest(gp, q, it)



N_TILE = SEQ // P
N_GROUP = 4
N_EXPERT = 32
PER_GROUP = N_EXPERT // N_GROUP
N_LOGIT = N_GROUP + N_EXPERT
FE = 512
KE = FE // P
N_BLOCK = (2 * SEQ + N_EXPERT * (P - 1)) // P
N_BLOCK += N_BLOCK % 2
FAR = 1e30


def stage_to_tokens(nc, K, xt, L):
    with ExitStack() as ctx:
        turned, out, squared, inv_r, inv_i, normed, stored, in_, wscaled, logits, added = semaphores(
            nc, K, "tk_turned", "tk_out", "tk_squared", "tk_rooted", "tk_inverted", "tk_normed", "tk_stored", "tk_in",
            "tk_w_scaled", "tk_logits", "tk_added")
        gain = ctx.enter_context(nc.sbuf_tensor("tk_gain", [P, D], FP32))
        rw = ctx.enter_context(nc.sbuf_tensor("tk_rw", [P, KD, N_LOGIT], FP32))
        rb = ctx.enter_context(nc.sbuf_tensor("tk_rb", [P, N_LOGIT], FP32))
        junk = ctx.enter_context(nc.sbuf_tensor("tk_junk", [P, D], FP32))
        h = ctx.enter_context(nc.sbuf_tensor("tk_h", [P, 2, D], FP32))
        ss = ctx.enter_context(nc.sbuf_tensor("tk_ss", [P, 3, N_TILE], FP32))
        with nc.Block(no_gpsimd_drain=True) as block:

            @block.sync
            def _(sync):
                sync.dma_start(gain[:], K.dram["norm_ffn_g_2"].to_broadcast([P, D])).then_inc(in_, 16)
                sync.dma_start(rw[:, :, 0:N_GROUP], K.dram["router_group_w_2"][0].rearrange("(k p) e -> p k e", p=P)).then_inc(in_, 16)
                sync.dma_start(rw[:, :, N_GROUP:], K.dram["router_expert_w_2"][0].rearrange("(k p) e -> p k e", p=P)).then_inc(in_, 16)
                sync.dma_start(rb[:, 0:N_GROUP], K.dram["router_group_b_2"].to_broadcast([P, N_GROUP])).then_inc(in_, 16)
                sync.dma_start(rb[:, N_GROUP:], K.dram["router_expert_b_2"].to_broadcast([P, N_EXPERT])).then_inc(in_, 16)
                for t in range(N_TILE):
                    sync.wait_ge(normed, t + 1)
                    sync.dma_start(K.scr["h2"][t * P:(t + 1) * P, :], h[:, t % 2, :]).then_inc(stored, 16)
                    sync.wait_ge(stored, 16 * (t + 1))

            @block.tensor
            def _(pe):
                for n in range(2 * N_TILE):
                    t, g = n // 2, n % 2
                    if n >= 6:
                        pe.wait_ge(out, n - 5)
                    for k in range(4):
                        last = pe.transpose(K.ps[:, n % 6, k * P:(k + 1) * P], K.xT[:, 4 * g + k, t * P:(t + 1) * P], K.ident[:])
                    last.then_inc(turned, 1)
                pe.wait_ge(wscaled, 1)
                for t in range(N_TILE):
                    for k in range(KD):
                        last = pe.matmul(K.ps[:, 7, t * N_LOGIT:(t + 1) * N_LOGIT], K.xT[:, k, t * P:(t + 1) * P], rw[:, k, :],
                                         start=(k == 0), stop=(k == KD - 1))
                last.then_inc(logits, 1)

            @block.scalar
            def _(act):
                for n in range(2 * N_TILE):
                    t, g = n // 2, n % 2
                    act.wait_ge(turned, n + 1)
                    act.activation(xt[:, t, g * HALF:(g + 1) * HALF], K.ps[:, n % 6, :], ACT.Copy).then_inc(out, 1)
                for t in range(N_TILE):
                    act.wait_ge(out, 2 * (t + 1))
                    if t:
                        act.wait_ge(squared, t)
                    act.activation(junk[:], xt[:, t, :], ACT.Square, accum_out=ss[:, 0, t:t + 1]).then_inc(squared, 1)
                act.wait_ge(squared, N_TILE)
                act.activation(ss[:, 1, :], ss[:, 0, :], ACT.Sqrt, bias=K.eps_rms[:, 0:1], scale=1.0 / D).then_inc(inv_r, 1)

            @block.vector
            def _(dve):
                dve.wait_ge(in_, 16 * 5)
                for k in range(KD):
                    ins = dve.tensor_scalar(rw[:, k, :], rw[:, k, :], param(K, "norm_ffn_g_2", k), None, ALU.mult)
                ins.then_inc(wscaled, 1)
                dve.wait_ge(inv_r, 1)
                dve.reciprocal(ss[:, 2, :], ss[:, 1, :]).then_inc(inv_i, 1)
                dve.wait_ge(inv_i, 1)
                for t in range(N_TILE):
                    if t >= 2:
                        dve.wait_ge(stored, 16 * (t - 1))
                    dve.scalar_tensor_tensor(out=h[:, t % 2, :], in0=xt[:, t, :], scalar=ss[:, 2, t:t + 1], in1=gain[:],
                                             op0=ALU.mult, op1=ALU.mult).then_inc(normed, 1)
                dve.wait_ge(logits, 1)
                for t in range(N_TILE):
                    dve.scalar_tensor_tensor(out=L[:, t, :], in0=K.ps[:, 7, t * N_LOGIT:(t + 1) * N_LOGIT],
                                             scalar=ss[:, 2, t:t + 1], in1=rb[:], op0=ALU.mult, op1=ALU.add).then_inc(added, 1)
                dve.wait_ge(added, N_TILE)


def stage_route(nc, K, L, dest, weight, row_ids, experts):
    with ExitStack() as ctx:
        step, exped, ranked, filled, tok_made, scattered, tab_in, tab_f, turned = semaphores(
            nc, K, "rt_step", "rt_exped", "rt_ranked", "rt_filled", "rt_tok_made", "rt_scattered", "rt_tab_in", "rt_tab_f",
            "rt_turned")

        def sb(name, *shape, dt=FP32):
            return ctx.enter_context(nc.sbuf_tensor(f"rt_{name}", [P, *shape], dt))
        T, E, NG = N_TILE, N_EXPERT, N_GROUP
        gm, pg, s1, s2 = sb("gm", T), sb("pg", T), sb("s1", T), sb("s2", T)
        g4, g5, oh4 = sb("g4", T, NG), sb("g5", T, NG), sb("oh4", T, NG)
        Em, e1, e2 = sb("Em", T, E), sb("e1", T, E), sb("e2", T, E)
        oh = sb("oh", 2, T, E)
        both = sb("both", T, E)
        m = sb("m", 2, T)
        first = sb("first", E, dt=I32)
        firstf = sb("firstf", E)
        strict = sb("strict", P)
        tot, base = sb("tot", T, E), sb("base", T + 1, E)
        thr, thrf = sb("thr", T, dt=I32), sb("thrf", T)
        cmp = sb("cmp", E, T)
        nblk, cend, pstart = sb("nblk", E), sb("cend", E), sb("pstart", E)
        blk, blkf = sb("blk", N_BLOCK, dt=I32), sb("blkf", N_BLOCK)
        bcmp, bexp = sb("bcmp", N_BLOCK, E), sb("bexp", N_BLOCK)
        slot, pick = sb("slot", T, E), sb("pick", T, E)
        destf = sb("destf", T, 2)
        tok = sb("tok", T, dt=I32)
        zero = sb("zero", N_BLOCK, dt=I32)
        tab = ctx.enter_context(nc.sbuf_tensor("rt_tab", [N_BLOCK, P], I32))
        tabf = ctx.enter_context(nc.sbuf_tensor("rt_tabf", [N_BLOCK, P], FP32))

        def last_dim(x, shape):
            n = len(x.shape)
            v = x.rearrange("p (t a) -> p t a", a=1) if n == 2 else x.rearrange("p t (g a) -> p t g a", a=1)
            return v.to_broadcast(shape)

        def mid_dim(x, shape):
            return x.rearrange("p (a n) -> p a n", a=1).to_broadcast(shape)
        with nc.Block(no_gpsimd_drain=True) as block:

            @block.gpsimd
            def _(gp):
                gp.memset(zero[:], 0).then_inc(tok_made, 1)
                gp.wait_ge(tok_made, 1)
                gp.dma_start(K.scr["row_table"].rearrange("(p j) a -> p (j a)", p=P), zero[:]).then_inc(filled, 16)
                gp.iota(tok[:], pattern=[[P, T]], base=0, channel_multiplier=1)
                gp.iota(first[:], pattern=[[-1, E]], base=E, channel_multiplier=0)
                gp.iota(thr[:], pattern=[[P, T]], base=0, channel_multiplier=0)
                gp.iota(blk[:], pattern=[[1, N_BLOCK]], base=0, channel_multiplier=0)
                gp.memset(base[:, 0, :], 0.0)
                gp.tensor_tensor(strict[:], K.upper[:], K.ident[:], ALU.subtract).then_inc(tok_made, 1)
                gp.wait_ge(filled, 16)
                gp.wait_ge(ranked, 1)
                for c in range(2):
                    for t in range(T):
                        gp.indirect_dma_start(out=K.scr["row_table"], out_offset=bass.IndirectOffsetOnAxis(ap=dest[:, c, t:t + 1], axis=0),
                                              in_=tok[:, t:t + 1], in_offset=None).then_inc(scattered, 16)
                gp.wait_ge(scattered, 16 * 2 * T)
                gp.dma_start(tab[:], K.scr["row_table"].rearrange("(j p) a -> j (p a)", p=P)).then_inc(tab_in, 16)
                gp.wait_ge(tab_in, 16)

            @block.scalar
            def _(act):
                act.wait_ge(exped, 1)
                act.activation(g5[:], g4[:], ACT.Exp).then_inc(exped, 1)
                act.wait_ge(exped, 3)
                act.activation(s2[:], s1[:], ACT.Exp).then_inc(exped, 1)

            @block.tensor
            def _(pe):
                pe.wait_ge(tok_made, 2)
                pe.wait_ge(turned, 1)
                flat = both[:].rearrange("p t e -> p (t e)")
                pe.matmul(K.ps[:, 0, 0:T * E], strict[:], flat, start=True, stop=True)
                pe.matmul(K.ps[:, 1, 0:T * E], K.ones[:], flat, start=True, stop=True).then_inc(turned, 1)
                pe.wait_ge(tab_f, 1)
                pe.transpose(K.ps[:, 2, 0:N_BLOCK], tabf[:], K.ident[0:N_BLOCK, 0:N_BLOCK]).then_inc(turned, 1)

            @block.vector
            def _(dve):
                n = [0]

                def link(ins):
                    n[0] += 1
                    ins.then_inc(step, 1)
                    dve.wait_ge(step, n[0])

                Lg = L[:, :, 0:NG]
                Le = L[:, :, NG:]
                dve.wait_ge(tok_made, 2)
                link(dve.tensor_copy(firstf[:], first[:]))
                link(dve.tensor_copy(thrf[:], thr[:]))
                link(dve.tensor_copy(blkf[:], blk[:]))
                link(dve.tensor_reduce(gm[:], Lg, AX.X, ALU.max))
                dve.tensor_tensor(g4[:], Lg, last_dim(gm[:], [P, T, NG]), ALU.subtract).then_inc(exped, 1)
                dve.wait_ge(exped, 2)
                link(dve.tensor_reduce(pg[:], g5[:], AX.X, ALU.add))
                link(dve.reciprocal(pg[:], pg[:]))

                def first_largest(out, x, top, width, tie):
                    shape = [P, T, width]
                    link(dve.tensor_tensor(out, x, last_dim(top, shape), ALU.is_equal))
                    link(dve.tensor_tensor(tie, out, mid_dim(firstf[:, 0:width], shape), ALU.mult))
                    link(dve.tensor_reduce(s1[:], tie, AX.X, ALU.max))
                    link(dve.tensor_tensor(out, tie, last_dim(s1[:], shape), ALU.is_equal))

                first_largest(oh4[:], Lg, gm[:], NG, g4[:])
                link(dve.tensor_scalar(g4[:], oh4[:], -1.0, FAR, ALU.add, ALU.mult))
                view = [P, T, NG, PER_GROUP]
                link(dve.tensor_tensor(Em[:].rearrange("p t (g e) -> p t g e", g=NG), Le.rearrange("p t (g e) -> p t g e", g=NG),
                                       last_dim(g4[:], view), ALU.add))
                link(dve.tensor_reduce(m[:, 0, :], Em[:], AX.X, ALU.max))
                first_largest(oh[:, 0], Em[:], m[:, 0, :], E, e1[:])
                link(dve.scalar_tensor_tensor(out=e2[:], in0=oh[:, 0], scalar=-3.0 * FAR, in1=Em[:], op0=ALU.mult, op1=ALU.add))
                link(dve.tensor_reduce(m[:, 1, :], e2[:], AX.X, ALU.max))
                first_largest(oh[:, 1], e2[:], m[:, 1, :], E, e1[:])
                dve.tensor_tensor(both[:], oh[:, 0], oh[:, 1], ALU.add).then_inc(turned, 1)
                dve.tensor_tensor(s1[:], m[:, 1, :], m[:, 0, :], ALU.subtract).then_inc(exped, 1)
                dve.wait_ge(exped, 4)
                link(dve.tensor_scalar(gm[:], s2[:], 1.0, None, ALU.add))
                link(dve.reciprocal(s1[:], gm[:]))
                link(dve.tensor_tensor(weight[:, 0, :], pg[:], s1[:], ALU.mult))
                link(dve.tensor_tensor(weight[:, 1, :], weight[:, 0, :], s2[:], ALU.mult))
                dve.wait_ge(turned, 2)
                link(dve.tensor_copy(tot[:], K.ps[:, 1, 0:T * E].rearrange("p (t e) -> p t e", e=E)))
                for t in range(T):
                    link(dve.tensor_tensor(base[:, t + 1, :], base[:, t, :], tot[:, t, :], ALU.add))
                link(dve.tensor_tensor(cmp[:], last_dim(base[:, T, :], [P, E, T]), mid_dim(thrf[:], [P, E, T]), ALU.is_gt))
                link(dve.tensor_reduce(nblk[:], cmp[:], AX.X, ALU.add))
                link(dve.tensor_tensor_scan(cend[:], K.ones[:, 0:E], nblk[:], 0.0, ALU.mult, ALU.add))
                link(dve.tensor_tensor(pstart[:], cend[:], nblk[:], ALU.subtract))
                link(dve.tensor_scalar(pstart[:], pstart[:], float(P), None, ALU.mult))
                link(dve.tensor_tensor(slot[:], K.ps[:, 0, 0:T * E].rearrange("p (t e) -> p t e", e=E), base[:, 0:T, :], ALU.add))
                link(dve.tensor_tensor(slot[:], slot[:], mid_dim(pstart[:], [P, T, E]), ALU.add))
                for c in range(2):
                    link(dve.tensor_tensor(pick[:], slot[:], oh[:, c], ALU.mult))
                    link(dve.tensor_reduce(destf[:, :, c], pick[:], AX.X, ALU.add))
                    link(dve.tensor_copy(dest[:, c, :], destf[:, :, c]))
                dve.sem_inc(ranked, 1)
                shape = [P, N_BLOCK, E]
                link(dve.tensor_tensor(bcmp[:], mid_dim(cend[:], shape), last_dim(blkf[:], shape), ALU.is_le))
                link(dve.tensor_reduce(bexp[:], bcmp[:], AX.X, ALU.add))
                link(dve.tensor_scalar(bexp[:], bexp[:], float(E - 1), None, ALU.min))
                link(dve.tensor_copy(experts[:, 0:N_BLOCK], bexp[0:1, :]))
                even = blkf[0:1, 0::2]
                link(dve.tensor_tensor(bexp[0:1, 0::2], even, cend[0:1, E - 1:E].to_broadcast([1, N_BLOCK // 2]), ALU.is_lt))
                link(dve.tensor_reduce(nblk[0:1, 0:1], bexp[0:1, 0::2], AX.X, ALU.add))
                link(dve.tensor_copy(experts[:, N_BLOCK:], nblk[0:1, 0:1]))
                dve.wait_ge(tab_in, 16)
                dve.tensor_copy(tabf[:], tab[:]).then_inc(tab_f, 1)
                dve.wait_ge(turned, 3)
                link(dve.tensor_copy(row_ids[:], K.ps[:, 2, 0:N_BLOCK]))


def stage_experts(nc, K, row_ids, experts):
    with ExitStack() as ctx:
        def two(name):
            return semaphores(nc, K, f"ex_{name}0", f"ex_{name}1")
        wg_in, wu_in, wd_in, gathered, stored = two("wg_in"), two("wu_in"), two("wd_in"), two("gathered"), two("stored")
        x_turned, x_out, gu_done, silued, acted, a_turned, a_out, y_done, y_out = semaphores(
            nc, K, *[f"ex_{n}" for n in ("x_turned", "x_out", "gu_done", "silued", "acted", "a_turned", "a_out", "y_done", "y_out")])
        x_out_b, y_out_b, all_stored = semaphores(nc, K, "ex_x_out_b", "ex_y_out_b", "ex_all_stored")
        wg = ctx.enter_context(nc.sbuf_tensor("ex_wg", [P, 2, KD, FE], FP32))
        wu = ctx.enter_context(nc.sbuf_tensor("ex_wu", [P, 2, KD, FE], FP32))
        wd = ctx.enter_context(nc.sbuf_tensor("ex_wd", [P, 2, KE, D], FP32))
        xg = ctx.enter_context(nc.sbuf_tensor("ex_xg", [P, 2, D], FP32))
        XT = ctx.enter_context(nc.sbuf_tensor("ex_XT", [P, 2, KD, P], FP32))
        sg = ctx.enter_context(nc.sbuf_tensor("ex_sg", [P, FE], FP32))
        ac = ctx.enter_context(nc.sbuf_tensor("ex_ac", [P, FE], FP32))
        AT = ctx.enter_context(nc.sbuf_tensor("ex_AT", [P, KE, P], FP32))
        yo = ctx.enter_context(nc.sbuf_tensor("ex_yo", [P, 2, D], FP32))
        g_v = K.dram["w_gate_2"][0].rearrange("e (p k) f -> p e (k f)", k=KD)
        u_v = K.dram["w_up_2"][0].rearrange("e (p k) f -> p e (k f)", k=KD)
        d_v = K.dram["w_down_2"][0].rearrange("e (p k) f -> p e (k f)", k=KE)

        def pairs(eng, body):
            used = eng.value_load(experts[0:1, N_BLOCK:N_BLOCK + 1], min_val=1, max_val=N_BLOCK // 2)
            with eng.Fori(0, N_BLOCK // 2) as it:
                with eng.If(it < used):
                    body(it)
            return used

        with nc.Block(no_gpsimd_drain=True) as block:

            @block.sync
            def _(sync):
                def body(it):
                    for q in range(2):
                        e = sync.value_load(experts[0:1, bass.ds(2 * it + q, 1)], min_val=0, max_val=N_EXPERT - 1)
                        sync.wait_ge(gu_done, 2 * it + q + 1)
                        sync.dma_start(wg[:, q, :, :].rearrange("p (a k) f -> p a (k f)", a=1), g_v[:, bass.ds(e, 1), :]).then_inc(wg_in[q], 16)
                        sync.dma_start(wu[:, q, :, :].rearrange("p (a k) f -> p a (k f)", a=1), u_v[:, bass.ds(e, 1), :]).then_inc(wu_in[q], 16)
                        sync.wait_ge(y_done, 2 * it + q + 1)
                        sync.dma_start(wd[:, q, :, :].rearrange("p (a k) f -> p a (k f)", a=1), d_v[:, bass.ds(e, 1), :]).then_inc(wd_in[q], 16)
                pairs(sync, body)

            @block.gpsimd
            def _(gp):
                used = gp.value_load(experts[0:1, N_BLOCK:N_BLOCK + 1], min_val=1, max_val=N_BLOCK // 2)
                for it in range(N_BLOCK // 2):
                    with gp.If(used > it):
                        for q in range(2):
                            b = 2 * it + q
                            if b >= 2:
                                gp.wait_ge(x_turned, b - 1)
                            gp.indirect_dma_start(out=xg[:, q, :], out_offset=None, in_=K.scr["h2"],
                                                  in_offset=bass.IndirectOffsetOnAxis(ap=row_ids[:, b:b + 1], axis=0)
                                                  ).then_inc(gathered[q], 16)

            @block.tensor
            def _(pe):
                pe.sem_inc(gu_done, 2)
                pe.sem_inc(y_done, 2)

                def turn_x(b, it, q):
                    pe.wait_ge(gathered[q], 16 * it + 16)
                    pe.wait_ge(x_out, b + 1)
                    pe.wait_ge(x_out_b, b + 1)
                    for k in range(KD):
                        last = pe.transpose(K.ps[:, k // 4, (k % 4) * P:(k % 4 + 1) * P], xg[:, q, k::KD], K.ident[:])
                    last.then_inc(x_turned, 1)

                def body(it):
                    turn_x(2 * it, it, 0)
                    for q in range(2):
                        b = 2 * it + q
                        pe.wait_ge(x_out, b + 2)
                        pe.wait_ge(x_out_b, b + 2)
                        for w, loaded, bank in ((wg, wg_in, 2), (wu, wu_in, 3)):
                            pe.wait_ge(loaded[q], 16 * it + 16)
                            pe.wait_ge(acted, b + 1)
                            for k in range(KD):
                                last = pe.matmul(K.ps[:, bank, :], XT[:, q, k, :], w[:, q, k, :], start=(k == 0), stop=(k == KD - 1))
                        last.then_inc(gu_done, 1)
                        if q == 0:
                            turn_x(b + 1, it, 1)
                        pe.wait_ge(acted, b + 2)
                        pe.wait_ge(a_out, b + 1)
                        for k in range(KE):
                            last = pe.transpose(K.ps[:, 4, k * P:(k + 1) * P], ac[:, k::KE], K.ident[:])
                        last.then_inc(a_turned, 1)
                        pe.wait_ge(a_out, b + 2)
                        pe.wait_ge(wd_in[q], 16 * it + 16)
                        pe.wait_ge(y_out, b + 1)
                        pe.wait_ge(y_out_b, b + 1)
                        for n in range(2):
                            for k in range(KE):
                                last = pe.matmul(K.ps[:, 5 + n, :], AT[:, k, :], wd[:, q, k, n * HALF:(n + 1) * HALF],
                                                 start=(k == 0), stop=(k == KE - 1))
                        last.then_inc(y_done, 1)
                pairs(pe, body)

            @block.scalar
            def _(act):
                act.sem_inc(x_out, 1)
                act.sem_inc(silued, 1)
                act.sem_inc(y_out, 1)
                act.sem_inc(stored[0], 16)
                act.sem_inc(stored[1], 16)

                def x_half(b, q):
                    act.wait_ge(x_turned, b + 1)
                    act.wait_ge(gu_done, b + 1)
                    act.activation(XT[:, q, 0:4, :].rearrange("p k t -> p (k t)"), K.ps[:, 0, :], ACT.Copy).then_inc(x_out, 1)

                def body(it):
                    x_half(2 * it, 0)
                    for q in range(2):
                        b = 2 * it + q
                        act.wait_ge(gu_done, b + 3)
                        act.wait_ge(acted, b + 1)
                        act.activation(sg[:], K.ps[:, 2, :], ACT.Silu).then_inc(silued, 1)
                        if q == 0:
                            x_half(b + 1, 1)
                        act.wait_ge(y_done, b + 3)
                        act.wait_ge(stored[q], 16 * it + 16)
                        act.activation(yo[:, q, 0:HALF], K.ps[:, 5, :], ACT.Copy).then_inc(y_out, 1)
                        act.wait_ge(y_out, b + 2)
                        act.wait_ge(y_out_b, b + 2)
                        act.dma_start(K.scr["y"][bass.ds(b * P, P), :], yo[:, q, :]).then_inc(stored[q], 16)
                used = pairs(act, body)
                for q in range(2):
                    act.wait_ge(stored[q], used * 16 + 16)
                    act.sem_inc(all_stored, 1)

            @block.vector
            def _(dve):
                dve.sem_inc(x_out_b, 1)
                dve.sem_inc(acted, 1)
                dve.sem_inc(a_out, 1)
                dve.sem_inc(y_out_b, 1)

                def x_half(b, q):
                    dve.wait_ge(x_turned, b + 1)
                    dve.wait_ge(gu_done, b + 1)
                    dve.tensor_copy(XT[:, q, 4:8, :].rearrange("p k t -> p (k t)"), K.ps[:, 1, :]).then_inc(x_out_b, 1)

                def body(it):
                    x_half(2 * it, 0)
                    for q in range(2):
                        b = 2 * it + q
                        dve.wait_ge(silued, b + 2)
                        dve.wait_ge(a_out, b + 1)
                        dve.tensor_tensor(ac[:], K.ps[:, 3, :], sg[:], ALU.mult).then_inc(acted, 1)
                        if q == 0:
                            x_half(b + 1, 1)
                        dve.wait_ge(a_turned, b + 1)
                        dve.wait_ge(y_done, b + 2)
                        dve.tensor_copy(AT[:].rearrange("p k t -> p (k t)"), K.ps[:, 4, :]).then_inc(a_out, 1)
                        dve.wait_ge(y_done, b + 3)
                        dve.wait_ge(stored[q], 16 * it + 16)
                        dve.tensor_copy(yo[:, q, HALF:], K.ps[:, 6, :]).then_inc(y_out_b, 1)
                pairs(dve, body)


def stage_combine(nc, K, xt, dest, weight, out):
    with ExitStack() as ctx:
        g_in = semaphores(nc, K, *[f"cb_gathered{t}" for t in range(N_TILE)])
        gain_in, mixed, squared, rooted, inverted, scaled, stored = semaphores(
            nc, K, "cb_gain_in", "cb_mixed", "cb_squared", "cb_rooted", "cb_inverted", "cb_scaled", "cb_stored")
        gain = ctx.enter_context(nc.sbuf_tensor("cb_gain", [P, D], FP32))
        y = ctx.enter_context(nc.sbuf_tensor("cb_y", [P, N_TILE, 2, D], FP32))
        junk = ctx.enter_context(nc.sbuf_tensor("cb_junk", [P, D], FP32))
        ss = ctx.enter_context(nc.sbuf_tensor("cb_ss", [P, 3, N_TILE], FP32))
        with nc.Block(no_gpsimd_drain=True) as block:

            @block.gpsimd
            def _(gp):
                for t in range(N_TILE):
                    for c in range(2):
                        gp.indirect_dma_start(out=y[:, t, c, :], out_offset=None, in_=K.scr["y"],
                                              in_offset=bass.IndirectOffsetOnAxis(ap=dest[:, c, t:t + 1], axis=0)
                                              ).then_inc(g_in[t], 16)

            @block.sync
            def _(sync):
                sync.dma_start(gain[:], K.dram["final_norm_g_2"].rearrange("(a n) -> a n", a=1).to_broadcast([P, D])).then_inc(gain_in, 16)
                for t in range(N_TILE):
                    sync.wait_ge(scaled, t + 1)
                    sync.dma_start(out[t * P:(t + 1) * P, :], xt[:, t, :]).then_inc(stored, 16)
                sync.wait_ge(stored, 16 * N_TILE)

            @block.vector
            def _(dve):
                for t in range(N_TILE):
                    dve.wait_ge(g_in[t], 32)
                    for c in range(2):
                        dve.scalar_tensor_tensor(out=xt[:, t, :], in0=y[:, t, c, :], scalar=weight[:, c, t:t + 1],
                                                 in1=xt[:, t, :], op0=ALU.mult, op1=ALU.add).then_inc(mixed, 1)
                        dve.wait_ge(mixed, 2 * t + c + 1)
                dve.wait_ge(gain_in, 16)
                for t in range(N_TILE):
                    dve.wait_ge(rooted, t + 1)
                    dve.reciprocal(ss[:, 2, t:t + 1], ss[:, 1, t:t + 1]).then_inc(inverted, 1)
                    dve.wait_ge(inverted, t + 1)
                    dve.scalar_tensor_tensor(out=xt[:, t, :], in0=xt[:, t, :], scalar=ss[:, 2, t:t + 1], in1=gain[:],
                                             op0=ALU.mult, op1=ALU.mult).then_inc(scaled, 1)

            @block.scalar
            def _(act):
                for t in range(N_TILE):
                    act.wait_ge(mixed, 2 * (t + 1))
                    if t:
                        act.wait_ge(squared, t)
                    act.activation(junk[:], xt[:, t, :], ACT.Square, accum_out=ss[:, 0, t:t + 1]).then_inc(squared, 1)
                    act.wait_ge(squared, t + 1)
                    act.activation(ss[:, 1, t:t + 1], ss[:, 0, t:t + 1], ACT.Sqrt, bias=K.eps_rms[:, 0:1],
                                   scale=1.0 / D).then_inc(rooted, 1)


def second_mixer(nc, K):
    with ExitStack() as ctx:
        G = ctx.enter_context(nc.sbuf_tensor("G", [P, N_CHUNK, HEADS], FP32))
        beta = ctx.enter_context(nc.sbuf_tensor("beta", [P, N_CHUNK, HEADS], FP32))
        second_projections(nc, K, G, beta)
        retire_semaphores(nc, K)
        oT = ctx.enter_context(nc.sbuf_tensor("oT", [P, 2 * HEADS, LEN], FP32))
        stage_recurrences(nc, K, G, beta, oT)
        stage_head_norm(nc, K, oT)
        part = Halves(nc, ctx, "o_parts", [P, KD, SEQ])
        stage_merge(nc, K, oT, part)
        stage_residual(nc, K, "wo2", oT, P, part, K.dram["w_out_2"][0])


def second_moe(nc, K, out):
    with ExitStack() as ctx:
        xt = ctx.enter_context(nc.sbuf_tensor("xt", [P, N_TILE, D], FP32))
        dest = ctx.enter_context(nc.sbuf_tensor("dest", [P, 2, N_TILE], I32))
        weight = ctx.enter_context(nc.sbuf_tensor("weight", [P, 2, N_TILE], FP32))
        row_ids = ctx.enter_context(nc.sbuf_tensor("row_ids", [P, N_BLOCK], I32))
        experts = ctx.enter_context(nc.sbuf_tensor("experts", [1, N_BLOCK + 1], I32))
        with ExitStack() as inner:
            L = inner.enter_context(nc.sbuf_tensor("logits", [P, N_TILE, N_LOGIT], FP32))
            stage_to_tokens(nc, K, xt, L)
            stage_route(nc, K, L, dest, weight, row_ids, experts)
        stage_experts(nc, K, row_ids, experts)
        stage_combine(nc, K, xt, dest, weight, out)


def program(nc, dram, out):
    K = Pack()
    K.dram = dram
    with ExitStack() as ctx:
        common(nc, ctx, K)
        K.scr = scratch(nc)
        stage_constants(nc, K)
        first_block(nc, K)
        retire_semaphores(nc, K)
        second_mixer(nc, K)
        retire_semaphores(nc, K)
        second_moe(nc, K, out)


_INS = ["x", "norm_mix_g", "w_in", "conv_a_w", "conv_b_w", "conv_b_b", "ln_b_g", "ln_b_b", "w_out", "norm_ffn_g",
        "w_gate", "w_up", "conv_ffn_w", "w_down", "norm_final_g", "meta_tokens_2", "hg_lb_logits_2", "norm_mix_g_2",
        "w_in_2", "gd_conv_w_2", "gd_A_log_2", "gd_dt_bias_2", "hg_norm_g_2", "gd_norm_g_2", "hg_up_2", "gd_up_2",
        "w_out_2", "norm_ffn_g_2", "router_group_w_2", "router_group_b_2", "router_expert_w_2", "router_expert_b_2",
        "w_gate_2", "w_up_2", "w_down_2", "final_norm_g_2"]


def kernel(**inputs):
    import concourse.bacc as _bacc
    from concourse.bass_utils import run_bass_kernel_spmd as _run

    nc = _bacc.Bacc("TRN2", target_bir_lowering=False, num_devices=1)
    arrays, dram = {}, {}
    for name in _INS:
        a = np.ascontiguousarray(inputs[name])
        arrays[f"in_{name}_dram"] = a
        dram[name] = nc.dram_tensor(f"in_{name}_dram", a.shape, mybir.dt.from_np(a.dtype), kind="ExternalInput").ap()
    out = nc.dram_tensor("out_0_dram", (1, SEQ, D), FP32, kind="ExternalOutput").ap()
    program(nc, dram, out[0])
    r = _run(nc, [arrays], core_ids=[0])
    return r.results[0]["out_0_dram"]
```

```python
import numpy as np
import concourse.bass as bass
from concourse import mybir
from contextlib import ExitStack

FP32 = mybir.dt.float32
FP32R = mybir.dt.float32r
I32 = mybir.dt.int32
ALU = mybir.AluOpType
ACT = mybir.ActivationFunctionType
AX = mybir.AxisListType

P = 128
D = 1024
KD = D // P
SEQ = 1024
HALF = 512
DFF = 2816
NF = DFF // P
EPS_RMS = 1e-6
EPS_LN = 1e-5


class Pack:
    pass


def semaphores(nc, K, *names):
    got = [nc.alloc_semaphore(name=n) for n in names]
    K.sems.extend(got)
    return got


def retire_semaphores(nc, K):
    nc.clear_and_free_semaphores(K.sems)
    nc.all_engine_barrier()
    K.sems = []


def pair(ps, slot):
    return ps[:, 2 * slot:2 * slot + 2, :].rearrange("p b n -> p (b n)")


class Halves:

    def __init__(self, nc, ctx, name, shape):
        self.hi = ctx.enter_context(nc.sbuf_tensor(f"{name}_hi", shape, FP32R))
        self.lo = ctx.enter_context(nc.sbuf_tensor(f"{name}_lo", shape, FP32R))


class Weights:

    def __init__(self, nc, K, ctx, tag, slots, nk, cols=P, raw=None):
        self.nk = nk
        self.raw = ctx.enter_context(nc.sbuf_tensor(f"{tag}_w", [P, slots, nk, cols], FP32)) if raw is None else raw
        self.part = Halves(nc, ctx, f"{tag}_w", [P, slots, nk, cols])
        self.loaded = semaphores(nc, K, *[f"{tag}_w_in{q}" for q in range(slots)])
        self.rounded = semaphores(nc, K, *[f"{tag}_w_rounded{q}" for q in range(slots)])
        self.split = semaphores(nc, K, *[f"{tag}_w_split{q}" for q in range(slots)])
        self.done = semaphores(nc, K, *[f"{tag}_done{q}" for q in range(slots)])

    def start(self, sync):
        for q in range(len(self.split)):
            sync.sem_inc(self.split[q], 1)
            sync.sem_inc(self.done[q], 1)

    def first(self, kind, eng, src=None):
        for q in range(len(self.split)):
            if kind == "load":
                self.load(eng, q, 0, src(q))
            elif kind == "round":
                self.round(eng, q, 0)
            else:
                self.rest(eng, q, 0)

    def load(self, sync, q, n, src, counted=None):
        sync.wait_ge(self.split[q], n + 1)
        if counted is not None:
            sync.sem_inc(counted, 1)
        sync.dma_start(self.raw[:, q], src).then_inc(self.loaded[q], 16)

    def round(self, act, q, n):
        act.wait_ge(self.loaded[q], n * 16 + 16)
        act.wait_ge(self.done[q], n + 1)
        act.activation(self.part.hi[:, q], self.raw[:, q], ACT.Copy).then_inc(self.rounded[q], 1)

    def rest(self, gp, q, n):
        gp.wait_ge(self.rounded[q], n + 1)
        gp.tensor_tensor(self.part.lo[:, q], self.raw[:, q], self.part.hi[:, q], ALU.subtract).then_inc(self.split[q], 1)


def three_products(pe, out, w_hi, w_lo, x_hi, x_lo, start, stop):
    pe.matmul(out, w_hi, x_hi, start=start, stop=False)
    pe.matmul(out, w_hi, x_lo, start=False, stop=False)
    return pe.matmul(out, w_lo, x_hi, start=False, stop=stop)


def project(pe, ps, bank0, W, q, n, src, groups, lo=0, ready=None, before_last=None):
    pe.wait_ge(W.split[q], n + 2)
    for g, cols in enumerate(groups):
        if before_last is not None and g == len(groups) - 1:
            before_last()
        at = lo + sum(groups[:g])
        for k in range(W.nk):
            if ready is not None:
                pe.wait_ge(ready, g * W.nk + k + 1)
            last = three_products(pe, ps[:, bank0 + g, 0:cols], W.part.hi[:, q, k, :], W.part.lo[:, q, k, :],
                                  src.hi[:, k, at:at + cols], src.lo[:, k, at:at + cols], k == 0, k == W.nk - 1)
    last.then_inc(W.done[q], 1)



PARAM_ROWS = [
    [("conv_b_w", 124), ("conv_b_b", 4)],
    [("conv_ffn_w", 66), ("conv_a_w", 12), ("norm_mix_g", 8), ("norm_ffn_g", 8), ("norm_final_g", 8),
     ("norm_mix_g_2", 8), ("ln_b_g", 4), ("ln_b_b", 4), ("hg_norm_g_2", 1), ("gd_norm_g_2", 1),
     ("hg_lb_logits_2", 8)],
    [("gd_conv_w_2", 48), ("norm_ffn_g_2", 8)],
]


def stage_constants(nc, K, x_rows=None):
    with ExitStack() as ctx:
        K.x_loaded = semaphores(nc, K, "x_loaded0", "x_loaded1")
        rows_in, zeroed, made, turned, out_of = semaphores(
            nc, K, "par_rows_in", "par_zeroed", "const_made", "par_turned", "par_out")
        rows = ctx.enter_context(nc.sbuf_tensor("par_rows", [P, len(PARAM_ROWS), P], FP32))
        n_in = sum(len(g) for g in PARAM_ROWS)
        with nc.Block(no_gpsimd_drain=True) as block:

            @block.sync
            def _(sync):
                sync.wait_ge(zeroed, 1)
                at = 0
                for t, group in enumerate(PARAM_ROWS):
                    r = 0
                    for name, n in group:
                        K.col[name] = at + r
                        src = K.dram[name]
                        flat = src.rearrange(" a b c -> (a b c)") if len(src.shape) == 3 else (
                            src.rearrange("a b -> (a b)") if len(src.shape) == 2 else src)
                        sync.dma_start(rows[r:r + n, t, :], flat.rearrange("(r c) -> r c", c=P)).then_inc(rows_in, 16)
                        r += n
                    at += P
                if x_rows is not None:
                    for t in range(SEQ // P):
                        sync.dma_start(x_rows[:, t, :], K.dram["x"][0, t * P:(t + 1) * P, :]).then_inc(K.x_loaded[t // 4], 16)

            @block.gpsimd
            def _(gp):
                gp.memset(rows[:], 0.0).then_inc(zeroed, 1)
                gp.memset(K.ones[:], 1.0)
                gp.memset(K.eps_rms[:], EPS_RMS)
                gp.memset(K.eps_ln[:], EPS_LN)
                gp.memset(K.ident[:], 0.0).then_inc(made, 1)
                gp.memset(K.upper[:], 1.0).then_inc(made, 1)
                gp.memset(K.level[:], 0.0).then_inc(made, 1)
                gp.wait_ge(made, 3)
                gp.affine_select(out=K.ident[:], in_=K.ident[:], compare_op=ALU.not_equal, fill=1.0,
                                 base=0, pattern=[[-1, P]], channel_multiplier=1).then_inc(made, 1)
                gp.affine_select(out=K.upper[:], in_=K.upper[:], compare_op=ALU.is_ge, fill=0.0,
                                 base=0, pattern=[[1, P]], channel_multiplier=-1).then_inc(made, 1)
                n = 5
                for lev in range(1, 8):
                    m = 1 << lev
                    right = K.level[:, lev, :].rearrange("p (b h i) -> p b h i", h=2, i=m // 2)[:, :, 1, :]
                    gp.memset(right, 1.0).then_inc(made, 1)
                    n += 1
                    gp.wait_ge(made, n)
                    gp.affine_select(out=right, in_=right, compare_op=ALU.is_ge, fill=0.0, base=0,
                                     pattern=[[-m, P // m], [0, m // 2]], channel_multiplier=1).then_inc(made, 1)
                    n += 1
                    gp.wait_ge(made, n)
                    gp.affine_select(out=right, in_=right, compare_op=ALU.is_ge, fill=0.0, base=m // 2 - 1,
                                     pattern=[[m, P // m], [0, m // 2]], channel_multiplier=-1).then_inc(made, 1)
                    n += 1
                gp.wait_ge(made, n)
                gp.tensor_copy(K.level[:, 0, :], K.ident[:]).then_inc(made, 1)
                gp.wait_ge(made, n + 1)

            @block.tensor
            def _(pe):
                pe.wait_ge(made, 4)
                pe.wait_ge(rows_in, 16 * n_in)
                for t in range(len(PARAM_ROWS)):
                    last = pe.transpose(K.ps[:, t, 0:P], rows[:, t, :], K.ident[:])
                last.then_inc(turned, 1)

            @block.scalar
            def _(act):
                act.wait_ge(turned, 1)
                for t in range(len(PARAM_ROWS)):
                    act.activation(K.par[:, t * P:(t + 1) * P], K.ps[:, t, 0:P], ACT.Copy).then_inc(out_of, 1)


def param(K, name, i=0):
    c = K.col[name] + i
    return K.par[:, bass.ds(c, 1)]



def stage_load_x(nc, K, rows):
    with ExitStack() as ctx:
        turned, freed = semaphores(nc, K, "x_turned", "x_turned_out")
        with nc.Block(no_gpsimd_drain=True) as block:

            @block.tensor
            def _(pe):
                for g in range(2):
                    pe.wait_ge(K.x_loaded[g], 16 * 4)
                    for k in range(KD):
                        n = KD * g + k
                        if n >= 8:
                            pe.wait_ge(freed, n - 7)
                        for t in range(4):
                            last = pe.transpose(K.ps[:, n % 8, t * P:(t + 1) * P],
                                                rows[:, 4 * g + t, k * P:(k + 1) * P], K.ident[:])
                        last.then_inc(turned, 1)

            @block.scalar
            def _(act):
                for n in range(2 * KD):
                    act.wait_ge(turned, n + 1)
                    act.activation(K.xT[:, n % KD, (n // KD) * HALF:(n // KD + 1) * HALF], K.ps[:, n % 8, :],
                                   ACT.Copy).then_inc(freed, 1)


class RmsNorm:

    def __init__(self, nc, K, ctx, tag, gain, parts, split=True, room=None):
        self.K, self.parts, self.gain, self.split = K, parts, gain, split
        self.squared, self.summed, self.rooted, self.inverted, self.scaled, self.rounded, self.ready = semaphores(
            nc, K, *[f"{tag}_{n}" for n in ("squared", "summed", "rooted", "inverted", "scaled", "rounded", "ready")])
        if room is None:
            room = ctx.enter_context(nc.sbuf_tensor(f"{tag}_room", [P, 6, HALF], FP32))
        self.sq, self.root, self.inv, self.tmp = room[:, 0:2], room[:, 2], room[:, 3], room[:, 4:6]

    def scalar(self, act, between):
        def squares(g):
            s, s_at, _, _, n = self.parts[g]
            for k in range(KD):
                m = g * KD + k
                if m >= 2:
                    act.wait_ge(self.summed, m - 1)
                act.activation(self.sq[:, m % 2, 0:n], s[:, k, s_at:s_at + n], ACT.Square).then_inc(self.squared, 1)

        def root(g):
            act.wait_ge(self.summed, (g + 1) * KD)
            if g:
                act.wait_ge(self.inverted, g)
            act.activation(self.root[:, 0:self.parts[g][4]], self.K.ps[:, 7 - g, 0:self.parts[g][4]], ACT.Sqrt,
                           bias=self.K.eps_rms[:, 0:1], scale=1.0 / D).then_inc(self.rooted, 1)
        squares(0)
        root(0)
        between(0)
        for g, (_, _, d, d_at, n) in enumerate(self.parts):
            if g + 1 < len(self.parts):
                squares(g + 1)
            if g:
                between(g)
            if self.split:
                for k in range(KD):
                    m = g * KD + k
                    act.wait_ge(self.scaled, m + 1)
                    act.activation(d.hi[:, k, d_at:d_at + n], self.tmp[:, m % 2, 0:n], ACT.Copy).then_inc(self.rounded, 1)
            if g + 1 < len(self.parts):
                root(g + 1)

    def tensor(self, pe):
        for g, (_, _, _, _, n) in enumerate(self.parts):
            for k in range(KD):
                m = g * KD + k
                pe.wait_ge(self.squared, m + 1)
                pe.matmul(self.K.ps[:, 7 - g, 0:n], self.K.ones[:], self.sq[:, m % 2, 0:n], start=(k == 0),
                          stop=(k == KD - 1)).then_inc(self.summed, 1)

    def vector(self, dve):
        for g, (s, s_at, d, d_at, n) in enumerate(self.parts):
            dve.wait_ge(self.rooted, g + 1)
            if g:
                dve.wait_ge(self.scaled, g * KD)
            dve.reciprocal(self.inv[:, 0:n], self.root[:, 0:n]).then_inc(self.inverted, 1)
            dve.wait_ge(self.inverted, g + 1)
            for k in range(KD):
                m = g * KD + k
                out = d[:, k, d_at:d_at + n]if not self.split else self.tmp[:, m % 2, 0:n]
                if self.split and m >= 2:
                    dve.wait_ge(self.ready, m - 1)
                dve.scalar_tensor_tensor(out=out, in0=s[:, k, s_at:s_at + n], scalar=param(self.K, self.gain, k),
                                         in1=self.inv[:, 0:n], op0=ALU.mult, op1=ALU.mult).then_inc(self.scaled, 1)
        dve.wait_ge(self.scaled, len(self.parts) * KD)

    def gpsimd(self, gp, between):
        for g, (_, _, d, d_at, n) in enumerate(self.parts):
            between(g)
            for k in range(KD):
                m = g * KD + k
                gp.wait_ge(self.rounded, m + 1)
                gp.tensor_tensor(d.lo[:, k, d_at:d_at + n], self.tmp[:, m % 2, 0:n], d.hi[:, k, d_at:d_at + n],
                                 ALU.subtract).then_inc(self.ready, 1)


def stage_rmsnorm(nc, K, tag, gain, parts):
    with ExitStack() as ctx:
        norm = RmsNorm(nc, K, ctx, tag, gain, parts, split=False)
        with nc.Block(no_gpsimd_drain=True) as block:

            @block.scalar
            def _(act):
                norm.scalar(act, lambda g: None)

            @block.tensor
            def _(pe):
                norm.tensor(pe)

            @block.vector
            def _(dve):
                norm.vector(dve)


def halves(src, dst):
    return [(src, h * HALF, dst, h * HALF, HALF) for h in range(2)]


def stage_mixer(nc, K, hT, y):
    TAPS = 31
    PAD = TAPS // 2
    N_TURN = 4
    VAL, GATE, AH, CG, BG = range(5)
    FIRST = (12, 16, 0, 8, 4)
    BANKS = (0, 1, 2, 3, 2)
    with ExitStack() as ctx:
        norm = RmsNorm(nc, K, ctx, "n1", "norm_mix_g", halves(K.xT, hT),
                       room=y[:, 0:3].rearrange("p k (h n) -> p (k h) n", n=HALF))
        free = semaphores(nc, K, *[f"mx_free_{n}" for n in ("val", "gate", "ah", "cg", "bg")])
        padded, step = semaphores(nc, K, "mx_padded", "mx_step")
        W = Weights(nc, K, ctx, "mx", 5, KD)
        sg = ctx.enter_context(nc.sbuf_tensor("mx_sg", [P, SEQ], FP32))
        ah = ctx.enter_context(nc.sbuf_tensor("mx_ah", [P, SEQ], FP32))
        u = ctx.enter_context(nc.sbuf_tensor("mx_u", [P, 1, SEQ + 2 * PAD], FP32))
        w_v = K.dram["w_in"][0].rearrange("(k p) e -> p k e", p=P)
        with nc.Block(no_gpsimd_drain=True) as block:

            @block.sync
            def _(sync):
                W.start(sync)
                for i in range(N_TURN):
                    for q in range(5):
                        W.load(sync, q, i, w_v[:, :, (FIRST[q] + i) * P:(FIRST[q] + i + 1) * P])

            @block.gpsimd
            def _(gp):
                gp.memset(u[:, :, 0:PAD], 0.0)
                gp.memset(u[:, :, PAD + SEQ:], 0.0).then_inc(padded, 1)
                norm.gpsimd(gp, lambda g: W.rest(gp, g, 0))
                for q in range(2, 5):
                    W.rest(gp, q, 0)
                with gp.Fori(1, N_TURN) as i:
                    for q in range(5):
                        W.rest(gp, q, i)

            @block.tensor
            def _(pe):
                norm.tensor(pe)
                with pe.Fori(0, N_TURN) as i:
                    for q in range(5):
                        if q == AH:
                            pe.wait_ge(free[BG], i + 1)
                        elif q == BG:
                            pe.wait_ge(free[AH], i + 2)
                        else:
                            pe.wait_ge(free[q], i + 1)
                        project(pe, K.ps, 2 * BANKS[q], W, q, i, hT, [HALF, HALF], ready=norm.ready)

            @block.scalar
            def _(act):
                norm.scalar(act, lambda g: W.round(act, g, 0))
                for q in range(2, 5):
                    W.round(act, q, 0)

                def body(i, more):
                    def round_next(q):
                        if more:
                            W.round(act, q, i + 1)
                    round_next(VAL)
                    act.wait_ge(W.done[GATE], i + 2)
                    act.wait_ge(free[BG], i + 1)
                    act.activation(sg[:], pair(K.ps, BANKS[GATE]), ACT.Sigmoid).then_inc(free[GATE], 1)
                    round_next(GATE)
                    act.wait_ge(W.done[AH], i + 2)
                    act.activation(ah[:], pair(K.ps, BANKS[AH]), ACT.Copy).then_inc(free[AH], 1)
                    for q in (AH, CG, BG):
                        round_next(q)
                with act.Fori(0, N_TURN - 1) as i:
                    body(i, True)
                body(N_TURN - 1, False)

            @block.vector
            def _(dve):
                for q in range(5):
                    dve.sem_inc(free[q], 1)
                norm.vector(dve)
                dve.wait_ge(padded, 1)
                with dve.Fori(0, N_TURN) as i:
                    at = (TAPS + 3) * i
                    dve.wait_ge(W.done[VAL], i + 2)
                    dve.wait_ge(free[GATE], i + 2)
                    dve.tensor_tensor(u[:, 0, PAD:PAD + SEQ], pair(K.ps, BANKS[VAL]), sg[:], ALU.mult).then_inc(free[VAL], 1)
                    dve.wait_ge(free[VAL], i + 2)
                    acc = y[:, bass.ds(i + 4, 1), :]
                    for k in range(TAPS):
                        src = u[:, :, k:k + SEQ]
                        tap = K.par[:, bass.ds(i + (K.col["conv_b_w"] + 4 * k), 1)]
                        if k == 0:
                            bias = K.par[:, bass.ds(i + K.col["conv_b_b"], 1)]
                            dve.tensor_scalar(acc, src, tap, bias, ALU.mult, ALU.add).then_inc(step, 1)
                        else:
                            dve.scalar_tensor_tensor(out=acc, in0=src, scalar=tap, in1=acc, op0=ALU.mult,
                                                     op1=ALU.add).then_inc(step, 1)
                        dve.wait_ge(step, at + (k + 1))
                    dve.wait_ge(W.done[CG], i + 2)
                    dve.wait_ge(free[AH], i + 2)
                    dve.tensor_tensor(ah[:], pair(K.ps, BANKS[CG]), ah[:], ALU.mult).then_inc(free[CG], 1)
                    dve.wait_ge(free[CG], i + 2)
                    conv3(dve, K, sg[:], ah[:], "conv_a_w", 4, i, step, at + TAPS)
                    dve.wait_ge(W.done[BG], i + 2)
                    dve.tensor_tensor(y[:, bass.ds(i, 1), :], pair(K.ps, BANKS[BG]), sg[:], ALU.mult).then_inc(free[BG], 1)
                    dve.wait_ge(free[BG], i + 2)


def conv3(dve, K, out, src, name, tiles, i, step, at):
    n = SEQ

    def tap(k):
        return K.par[:, bass.ds(K.col[name] + tiles * k + i, 1)]
    dve.tensor_scalar(out, src, tap(1), None, ALU.mult).then_inc(step, 1)
    dve.wait_ge(step, at + 1)
    dve.scalar_tensor_tensor(out=out[:, 1:n], in0=src[:, 0:n - 1], scalar=tap(0), in1=out[:, 1:n],
                             op0=ALU.mult, op1=ALU.add).then_inc(step, 1)
    dve.wait_ge(step, at + 2)
    dve.scalar_tensor_tensor(out=out[:, 0:n - 1], in0=src[:, 1:n], scalar=tap(2), in1=out[:, 0:n - 1],
                             op0=ALU.mult, op1=ALU.add).then_inc(step, 1)
    dve.wait_ge(step, at + 3)


def stage_layernorm_silu(nc, K, yb, W, w_dram):
    NT = 4
    WIDTH = NT * P
    with ExitStack() as ctx:
        summed, meaned, centred, squared, ssummed, rooted, inverted, normed, out = semaphores(
            nc, K, "ln_summed", "ln_meaned", "ln_centred", "ln_squared", "ln_ssummed", "ln_rooted",
            "ln_inverted", "ln_normed", "ln_out")
        mu = ctx.enter_context(nc.sbuf_tensor("ln_mu", [P, 2, HALF], FP32))
        sq = ctx.enter_context(nc.sbuf_tensor("ln_sq", [P, 2, NT, HALF], FP32))
        inv = ctx.enter_context(nc.sbuf_tensor("ln_inv", [P, 2, 2, HALF], FP32))
        part = [[yb[:, i, h * HALF:(h + 1) * HALF] for i in range(NT)] for h in range(2)]
        with nc.Block(no_gpsimd_drain=True) as block:

            @block.sync
            def _(sync):
                W.start(sync)
                W.first("load", sync, residual_weights(w_dram))

            @block.gpsimd
            def _(gp):
                W.first("rest", gp)
                gp.wait_ge(W.split[-1], 2)

            @block.tensor
            def _(pe):
                for h in range(2):
                    for i in range(NT):
                        last = pe.matmul(K.ps[:, h, :], K.ones[:], part[h][i], start=(i == 0), stop=(i == NT - 1))
                    last.then_inc(summed, 1)
                for h in range(2):
                    for i in range(NT):
                        pe.wait_ge(squared, h * NT + i + 1)
                        last = pe.matmul(K.ps[:, 2 + h, :], K.ones[:], sq[:, h, i, :], start=(i == 0),
                                         stop=(i == NT - 1))
                    last.then_inc(ssummed, 1)

            @block.scalar
            def _(act):
                W.first("round", act)
                for h in range(2):
                    for i in range(NT):
                        act.wait_ge(centred, h * NT + i + 1)
                        act.activation(sq[:, h, i, :], part[h][i], ACT.Square).then_inc(squared, 1)
                for h in range(2):
                    act.wait_ge(ssummed, h + 1)
                    act.activation(inv[:, h, 0, :], K.ps[:, 2 + h, :], ACT.Sqrt, bias=K.eps_ln[:, 0:1],
                                   scale=1.0 / WIDTH).then_inc(rooted, 1)
                for h in range(2):
                    for i in range(NT):
                        act.wait_ge(normed, h * NT + i + 1)
                        act.activation(part[h][i], part[h][i], ACT.Silu, bias=param(K, "ln_b_b", i),
                                       scale=param(K, "ln_b_g", i)).then_inc(out, 1)

            @block.vector
            def _(dve):
                for h in range(2):
                    dve.wait_ge(summed, h + 1)
                    dve.tensor_scalar(mu[:, h, :], K.ps[:, h, :], 1.0 / WIDTH, None, ALU.mult).then_inc(meaned, 1)
                    dve.wait_ge(meaned, h + 1)
                    for i in range(NT):
                        dve.tensor_tensor(part[h][i], part[h][i], mu[:, h, :], ALU.subtract).then_inc(centred, 1)
                for h in range(2):
                    dve.wait_ge(rooted, h + 1)
                    dve.reciprocal(inv[:, h, 1, :], inv[:, h, 0, :]).then_inc(inverted, 1)
                    dve.wait_ge(inverted, h + 1)
                    dve.wait_ge(squared, (h + 1) * NT)
                    for i in range(NT):
                        dve.tensor_tensor(part[h][i], part[h][i], inv[:, h, 1, :], ALU.mult).then_inc(normed, 1)


def residual_weights(w_dram):
    w_v = w_dram.rearrange("(k p) e -> p k e", p=P)
    return lambda q: w_v[:, :, q * P:(q + 1) * P]


def stage_residual(nc, K, tag, src, at, part, W, w_dram):
    with ExitStack() as ctx:
        free = semaphores(nc, K, *[f"{tag}_free{q}" for q in range(2)])
        rounded, ready = semaphores(nc, K, f"{tag}_src_rounded", f"{tag}_src_ready")
        w_v = w_dram.rearrange("(k p) e -> p k e", p=P)
        n_it = KD // 2
        with nc.Block(no_gpsimd_drain=True) as block:

            @block.sync
            def _(sync):
                with sync.Fori(1, n_it) as it:
                    for q in range(2):
                        W.load(sync, q, it, w_v[:, :, bass.ds(q * P + it * (2 * P), P)])

            @block.scalar
            def _(act):
                for g in range(2):
                    for k in range(KD):
                        cols = slice(g * HALF, (g + 1) * HALF)
                        act.activation(part.hi[:, k, cols], src[:, k, at + g * HALF:at + (g + 1) * HALF], ACT.Copy
                                       ).then_inc(rounded, 1)
                with act.Fori(1, n_it) as it:
                    for q in range(2):
                        W.round(act, q, it)

            @block.gpsimd
            def _(gp):
                with gp.Fori(1, n_it) as it:
                    for q in range(2):
                        W.rest(gp, q, it)

            @block.tensor
            def _(pe):
                with pe.Fori(0, n_it) as it:
                    for q in range(2):
                        pe.wait_ge(free[q], it + 1)
                        project(pe, K.ps, 2 * q, W, q, it, part, [HALF, HALF], ready=ready)

            @block.vector
            def _(dve):
                for q in range(2):
                    dve.sem_inc(free[q], 1)
                for g in range(2):
                    for k in range(KD):
                        cols = slice(g * HALF, (g + 1) * HALF)
                        dve.wait_ge(rounded, g * KD + k + 1)
                        dve.tensor_tensor(part.lo[:, k, cols], src[:, k, at + g * HALF:at + (g + 1) * HALF],
                                          part.hi[:, k, cols], ALU.subtract).then_inc(ready, 1)
                with dve.Fori(0, n_it) as it:
                    for q in range(2):
                        dve.wait_ge(W.done[q], it + 2)
                        x = K.xT[:, bass.ds(2 * it + q, 1), :]
                        dve.tensor_tensor(x, pair(K.ps, q), x, ALU.add).then_inc(free[q], 1)


def stage_ffn(nc, K, hT):
    n_it = NF // 2
    with ExitStack() as ctx:
        norm = RmsNorm(nc, K, ctx, "n2", "norm_ffn_g", halves(K.xT, hT))
        free = semaphores(nc, K, *[f"ff_free{q}" for q in range(4)])
        stored = semaphores(nc, K, "ff_stored0", "ff_stored1")
        step, silu, zeroed, y_filled = semaphores(nc, K, "ff_step", "ff_silu", "ff_zeroed", "ff_y_filled")
        W = Weights(nc, K, ctx, "ff", 4, KD)
        zero = ctx.enter_context(nc.sbuf_tensor("ff_zero", [P, D], FP32))
        g = ctx.enter_context(nc.sbuf_tensor("ff_g", [P, 2, SEQ], FP32))
        p = ctx.enter_context(nc.sbuf_tensor("ff_p", [P, 2, SEQ], FP32))
        w_v = [K.dram[n][0].rearrange("(k p) e -> p k e", p=P) for n in ("w_gate", "w_up")]
        with nc.Block(no_gpsimd_drain=True) as block:

            @block.sync
            def _(sync):
                W.start(sync)
                with sync.Fori(0, n_it) as it:
                    for q in range(4):
                        W.load(sync, q, it, w_v[q % 2][:, :, bass.ds(q // 2 * P + it * (2 * P), P)])

            @block.gpsimd
            def _(gp):
                gp.memset(zero[:], 0.0).then_inc(zeroed, 1)
                gp.wait_ge(zeroed, 1)
                gp.dma_start(K.scr["y"].rearrange("(j p) d -> p j d", p=P),
                             zero[:].rearrange("p (a d) -> p a d", a=1).to_broadcast([P, N_BLOCK, D])).then_inc(y_filled, 16)
                norm.gpsimd(gp, lambda g: W.rest(gp, g, 0))
                for q in range(2, 4):
                    W.rest(gp, q, 0)
                with gp.Fori(1, n_it) as it:
                    for q in range(4):
                        W.rest(gp, q, it)
                gp.wait_ge(y_filled, 16)

            @block.tensor
            def _(pe):
                norm.tensor(pe)
                with pe.Fori(0, n_it) as it:
                    for q in range(4):
                        pe.wait_ge(free[q], it + 1)
                        project(pe, K.ps, 2 * q, W, q, it, hT, [HALF, HALF], ready=norm.ready)

            @block.scalar
            def _(act):
                for v in range(2):
                    act.sem_inc(stored[v], 16)
                norm.scalar(act, lambda g: W.round(act, g, 0))
                for q in range(2, 4):
                    W.round(act, q, 0)

                def body(it, more):
                    for v in range(2):
                        act.wait_ge(free[2 * v], it + 2)
                        act.activation(g[:, v, :], g[:, v, :], ACT.Silu).then_inc(silu, 1)
                        if more:
                            W.round(act, 2 * v, it + 1)
                            W.round(act, 2 * v + 1, it + 1)
                        act.wait_ge(free[2 * v + 1], it + 2)
                        act.dma_start(K.scr["p"][bass.ds(it * (2 * P) + v * P, P), :], p[:, v, :]).then_inc(stored[v], 16)
                with act.Fori(0, n_it - 1) as it:
                    body(it, True)
                body(n_it - 1, False)
                for v in range(2):
                    act.wait_ge(stored[v], 16 * (n_it + 1))

            @block.vector
            def _(dve):
                for q in range(4):
                    dve.sem_inc(free[q], 1)
                norm.vector(dve)
                with dve.Fori(0, n_it) as it:
                    for v in range(2):
                        dve.wait_ge(W.done[2 * v], it + 2)
                        conv3(dve, K, g[:, v, :], pair(K.ps, 2 * v), "conv_ffn_w", NF, 2 * it + v, step,
                              6 * it + 3 * v)
                        dve.sem_inc(free[2 * v], 1)
                        dve.wait_ge(W.done[2 * v + 1], it + 2)
                        dve.wait_ge(silu, 2 * it + v + 1)
                        dve.wait_ge(stored[v], 16 * it + 16)
                        dve.tensor_tensor(p[:, v, :], pair(K.ps, 2 * v + 1), g[:, v, :],
                                          ALU.mult).then_inc(free[2 * v + 1], 1)
                        dve.wait_ge(free[2 * v + 1], it + 2)


def stage_down(nc, K):
    S = 4
    with ExitStack() as ctx:
        loaded = semaphores(nc, K, *[f"dn_in{q}" for q in range(S)])
        rounded, split, used, summed, out = semaphores(nc, K, "dn_rounded", "dn_split", "dn_used", "dn_summed", "dn_out")
        raw_w = ctx.enter_context(nc.sbuf_tensor("dn_w", [P, S, D], FP32))
        raw_p = ctx.enter_context(nc.sbuf_tensor("dn_p", [P, S, HALF], FP32))
        w = Halves(nc, ctx, "dn_w", [P, S, D])
        p = Halves(nc, ctx, "dn_p", [P, S, HALF])
        w_v = K.dram["w_down"][0]
        PEEL = NF - 5 * S
        assert PEEL == 2 and S % 2 == 0

        def chunks(eng, body):
            for g in range(2):
                base = g * NF
                for k in range(PEEL):
                    body(g, k, base + k, (base + k) % S, k == 0, False)
                with eng.Fori(0, (NF - PEEL) // S - 1) as it:
                    for j in range(S):
                        body(g, it * S + (PEEL + j), it * S + (base + PEEL + j), (base + PEEL + j) % S, False, False)
                for j in range(S):
                    k = NF - S + j
                    body(g, k, base + k, (base + k) % S, False, j == S - 1)

        with nc.Block(no_gpsimd_drain=True) as block:

            @block.sync
            def _(sync):
                sync.sem_inc(split, S)
                seen = [0] * S

                def body(g, k, n, q, *_):
                    sync.wait_ge(split, n + 1)
                    sync.dma_start(raw_w[:, q, :], w_v[bass.ds(k * P, P), :]).then_inc(loaded[q], 16)
                    sync.dma_start(raw_p[:, q, :], K.scr["p"][bass.ds(k * P, P), g * HALF:(g + 1) * HALF]).then_inc(loaded[q], 16)
                chunks(sync, body)

            @block.scalar
            def _(act):
                act.sem_inc(used, S)

                def body(g, k, n, q, *_):
                    act.wait_ge(loaded[q], (n - q) * (32 // S) + 32)
                    act.wait_ge(used, n + 1)
                    act.activation(p.hi[:, q, :], raw_p[:, q, :], ACT.Copy)
                    act.activation(w.hi[:, q, :], raw_w[:, q, :], ACT.Copy).then_inc(rounded, 1)
                chunks(act, body)

            @block.tensor
            def _(pe):
                def body(g, k, n, q, first, last):
                    pe.wait_ge(split, n + (S + 1))
                    for j in range(KD):
                        if first:
                            pe.wait_ge(out, 8 * g + j + 1)
                        cols = slice(j * P, (j + 1) * P)
                        ins = three_products(pe, K.ps[:, j, :], w.hi[:, q, cols], w.lo[:, q, cols], p.hi[:, q, :],
                                             p.lo[:, q, :], first, last)
                        if last:
                            ins.then_inc(summed, 1)
                    if not last:
                        ins.then_inc(used, 1)
                chunks(pe, body)

            @block.vector
            def _(dve):
                dve.sem_inc(out, KD)

                def body(g, k, n, q, first, last):
                    dve.wait_ge(rounded, n + 1)
                    dve.tensor_tensor(p.lo[:, q, :], raw_p[:, q, :], p.hi[:, q, :], ALU.subtract)
                    dve.tensor_tensor(w.lo[:, q, :], raw_w[:, q, :], w.hi[:, q, :], ALU.subtract).then_inc(split, 1)
                    if last:
                        for j in range(KD):
                            dve.wait_ge(summed, 8 * g + j + 1)
                            x = K.xT[:, j, g * HALF:(g + 1) * HALF]
                            dve.tensor_tensor(x, K.ps[:, j, :], x, ALU.add).then_inc(out, 1)
                            if j == KD - 1:
                                dve.sem_inc(used, 1)
                chunks(dve, body)


def common(nc, ctx, K):
    def sb(name, shape, dt=FP32):
        return ctx.enter_context(nc.sbuf_tensor(name, shape, dt))
    K.col = {}
    K.sems = []
    K.ps = ctx.enter_context(nc.psum_tensor("ps", [P, 8, HALF], FP32))
    K.ones = sb("ones", [P, P])
    K.ident = sb("ident", [P, P])
    K.upper = sb("upper", [P, P])
    K.level = sb("level", [P, 8, P])
    K.eps_rms = sb("eps_rms", [P, 1])
    K.eps_ln = sb("eps_ln", [P, 1])
    K.par = sb("par", [P, len(PARAM_ROWS) * P])
    K.xT = sb("xT", [P, KD, SEQ])


def first_block(nc, K):
    with nc.sbuf_tensor("x_rows", [P, SEQ // P, D], FP32) as rows:
        stage_constants(nc, K, rows)
        stage_load_x(nc, K, rows)
    with ExitStack() as ctx:
        hT = Halves(nc, ctx, "hT", [P, KD, SEQ])
        with ExitStack() as inner:
            y = inner.enter_context(nc.sbuf_tensor("y", [P, KD, SEQ], FP32))
            stage_mixer(nc, K, hT, y)
            W = Weights(nc, K, inner, "wo", 2, KD)
            stage_layernorm_silu(nc, K, y[:, 4:8, :], W, K.dram["w_out"][0])
            stage_residual(nc, K, "wo", y, 0, hT, W, K.dram["w_out"][0])
        stage_ffn(nc, K, hT)
    stage_down(nc, K)
    stage_rmsnorm(nc, K, "n3", "norm_final_g", halves(K.xT, K.xT))



META = 16
N_CHUNK = 1 + SEQ // P
LEN = N_CHUNK * P
LEAD = P - META
HEADS = 4
HW = HEADS * P
COL = dict(hq=0, hf=512, hi=1024, hg=1536, gq=2048, gk=2560, gv=3072, gz=3584, beta=4096, pre_ga=4104, pre_gb=5128)
QUART = (META + SEQ) // 4


def stage_meta(nc, K, metaT):
    with ExitStack() as ctx:
        loaded, turned, out = semaphores(nc, K, "meta_loaded", "meta_turned", "meta_out")
        rows = ctx.enter_context(nc.sbuf_tensor("meta_rows", [META, D], FP32))
        with nc.Block(no_gpsimd_drain=True) as block:

            @block.sync
            def _(sync):
                sync.dma_start(rows[:], K.dram["meta_tokens_2"]).then_inc(loaded, 16)

            @block.tensor
            def _(pe):
                pe.wait_ge(loaded, 16)
                for k in range(KD):
                    last = pe.transpose(K.ps[:, 0, k * META:(k + 1) * META], rows[:, k * P:(k + 1) * P],
                                        K.ident[0:META, 0:META])
                last.then_inc(turned, 1)

            @block.scalar
            def _(act):
                act.wait_ge(turned, 1)
                act.activation(metaT[:].rearrange("p k t -> p (k t)"), K.ps[:, 0, 0:KD * META], ACT.Copy).then_inc(out, 1)


def stage_lower_bounds(nc, K, lb, W):
    with ExitStack() as ctx:
        step, exped = semaphores(nc, K, "lb_step", "lb_exped")
        t = ctx.enter_context(nc.sbuf_tensor("lb_t", [P, 6, HEADS], FP32))
        c = K.col["hg_lb_logits_2"]
        w_v = K.dram["w_in_2"][0].rearrange("(k p) e -> p k e", p=P)
        with nc.Block(no_gpsimd_drain=True) as block:

            @block.sync
            def _(sync):
                W.start(sync)
                W.first("load", sync, lambda q: w_v[:, :, COL["hf"] + q * P:COL["hf"] + (q + 1) * P])

            @block.gpsimd
            def _(gp):
                W.first("rest", gp)
                gp.wait_ge(W.split[-1], 2)

            @block.vector
            def _(dve):
                row = [K.par[:, c + 4 * r:c + 4 * r + 4] for r in range(2)]
                dve.tensor_tensor(t[:, 0, :], row[0], row[1], ALU.max).then_inc(step, 1)
                dve.wait_ge(step, 1)
                dve.tensor_tensor(t[:, 1, :], row[0], t[:, 0, :], ALU.subtract)
                dve.tensor_tensor(t[:, 2, :], row[1], t[:, 0, :], ALU.subtract).then_inc(step, 1)
                dve.wait_ge(exped, 1)
                dve.tensor_tensor(t[:, 5, :], t[:, 3, :], t[:, 4, :], ALU.add).then_inc(step, 1)
                dve.wait_ge(step, 3)
                dve.reciprocal(t[:, 0, :], t[:, 5, :]).then_inc(step, 1)
                dve.wait_ge(step, 4)
                dve.tensor_tensor(lb[:, 0:4], t[:, 3, :], t[:, 0, :], ALU.mult).then_inc(step, 1)
                dve.wait_ge(step, 5)
                dve.tensor_scalar(lb[:, 4:8], lb[:, 0:4], -1.0, 1.0, ALU.mult, ALU.add)

            @block.scalar
            def _(act):
                act.wait_ge(step, 2)
                act.activation(t[:, 3:5, :], t[:, 1:3, :], ACT.Exp).then_inc(exped, 1)
                W.first("round", act)


def stage_forget(nc, K, hT, lb, W):
    with ExitStack() as ctx:
        free = semaphores(nc, K, "fg_free0", "fg_free1")
        padded, zero_out, forget, keyed, logged, summed, stored = semaphores(
            nc, K, "fg_padded", "fg_zero_out", "fg_forget", "fg_keyed", "fg_logged", "fg_summed", "fg_stored")
        keep = ctx.enter_context(nc.sbuf_tensor("fg_keep", [P, LEN], FP32))
        f = ctx.enter_context(nc.sbuf_tensor("fg_f", [P, 2, LEN - LEAD], FP32))
        k_st = ctx.enter_context(nc.sbuf_tensor("fg_k", [P, 2, LEN], FP32))
        b_st = ctx.enter_context(nc.sbuf_tensor("fg_b", [P, 2, LEN], FP32))
        lf = ctx.enter_context(nc.sbuf_tensor("fg_lf", [P, 2, LEN], FP32))
        zero = ctx.enter_context(nc.sbuf_tensor("fg_zero", [P, P], FP32))
        w_v = K.dram["w_in_2"][0].rearrange("(k p) e -> p k e", p=P)
        with nc.Block(no_gpsimd_drain=True) as block:

            @block.sync
            def _(sync):
                for q in range(2):
                    W.load(sync, q, 1, w_v[:, :, COL["hf"] + (2 + q) * P:COL["hf"] + (3 + q) * P])

            @block.tensor
            def _(pe):
                with pe.Fori(0, 2) as it:
                    for q in range(2):
                        pe.wait_ge(free[q], it + 1)
                        project(pe, K.ps, 4 * q, W, q, it, hT, [QUART] * 4, LEAD)

            @block.scalar
            def _(act):
                for q in range(2):
                    act.sem_inc(free[q], 1)
                act.sem_inc(stored, 64)
                act.wait_ge(padded, 1)
                for it in range(2):
                    for q in range(2):
                        act.wait_ge(W.done[q], it + 2)
                        act.activation(f[:, q, :].rearrange("p (b n) -> p b n", b=4),
                                       K.ps[:, 4 * q:4 * q + 4, 0:QUART], ACT.Sigmoid).then_inc(free[q], 1)
                        if it == 0:
                            W.round(act, q, 1)
                    for q in range(2):
                        act.wait_ge(forget, 2 * it + q + 1)
                        act.activation(lf[:, q, LEAD:], f[:, q, :], ACT.Ln).then_inc(logged, 1)
                    for q in range(2):
                        rows = bass.ds(q * P + it * (2 * P), P)
                        act.wait_ge(keyed, 2 * it + q + 1)
                        act.dma_start(K.scr["k_a"][rows, :], k_st[:, q, :]).then_inc(stored, 16)
                    for q in range(2):
                        rows = bass.ds(q * P + it * (2 * P), P)
                        act.wait_ge(summed, 2 * it + q + 1)
                        act.dma_start(K.scr["b_a"][rows, :], b_st[:, q, :]).then_inc(stored, 16)
                act.wait_ge(stored, 3 * 64)

            @block.vector
            def _(dve):
                with dve.Fori(0, 2) as it:
                    for q in range(2):
                        dve.wait_ge(free[q], it + 2)
                        i = 2 * it + q
                        dve.tensor_scalar(f[:, q, :], f[:, q, :], lb[:, bass.ds(i + 4, 1)], lb[:, bass.ds(i, 1)],
                                          ALU.mult, ALU.add).then_inc(forget, 1)
                        dve.wait_ge(forget, 2 * it + q + 1)
                        dve.wait_ge(stored, 64 * it + 64)
                        dve.tensor_scalar(k_st[:, q, LEAD:], f[:, q, :], -1.0, 1.0, ALU.mult, ALU.add).then_inc(keyed, 1)
                    for q in range(2):
                        dve.wait_ge(logged, 2 * it + q + 1)
                        dve.tensor_tensor_scan(b_st[:, q, :], keep[:], lf[:, q, :], 0.0, ALU.mult,
                                               ALU.add).then_inc(summed, 1)
                    dve.wait_ge(summed, 2 * it + 2)

            @block.gpsimd
            def _(gp):
                gp.memset(keep[:].rearrange("p (c t) -> p c t", t=P)[:, :, 0:1], 0.0)
                gp.memset(keep[:].rearrange("p (c t) -> p c t", t=P)[:, :, 1:], 1.0)
                gp.memset(zero[:], 0.0)
                gp.memset(k_st[:, :, 0:LEAD], 0.0)
                gp.memset(lf[:, :, 0:LEAD], 0.0).then_inc(padded, 1)
                gp.wait_ge(padded, 1)
                for q in range(2):
                    W.rest(gp, q, 1)
                for i in range(HEADS):
                    gp.dma_start(K.scr["q_a"][i * P:(i + 1) * P, 0:P], zero[:]).then_inc(zero_out, 16)
                gp.wait_ge(zero_out, 16 * HEADS)


def stage_by_tokens(nc, K, hT, G, beta, W_next):
    with ExitStack() as ctx:
        THIRD = LEN // 3
        wl = semaphores(nc, K, *[f"bt_w_in{k}" for k in range(KD)])
        rows_done, rows_out = semaphores(nc, K, "bt_rows_done", "bt_rows_out")
        rows = ctx.enter_context(nc.sbuf_tensor("bt_rows", [2 * HEADS, LEN], FP32))
        sl, done, out, stored, gated, step, acted = semaphores(
            nc, K, "bt_small_in", "bt_done", "bt_out", "bt_stored", "bt_gated", "bt_step", "bt_acted")
        w = ctx.enter_context(nc.sbuf_tensor("bt_w", [P, KD, HW], FP32))
        wg = ctx.enter_context(nc.sbuf_tensor("bt_wg", [P, KD, 2 * HEADS], FP32))
        wp = Halves(nc, ctx, "bt_w", [P, KD, HW])
        wgp = Halves(nc, ctx, "bt_wg", [P, KD, 2 * HEADS])
        rounded, split = semaphores(nc, K, "bt_w_rounded", "bt_w_split")
        st = ctx.enter_context(nc.sbuf_tensor("bt_st", [P, 4, HW], FP32))
        a_log = ctx.enter_context(nc.sbuf_tensor("bt_a_log", [P, HEADS], FP32))
        dt = ctx.enter_context(nc.sbuf_tensor("bt_dt", [P, HEADS], FP32))
        t = ctx.enter_context(nc.sbuf_tensor("bt_t", [P, 6, N_CHUNK, HEADS], FP32))
        w_v = K.dram["w_in_2"][0].rearrange("(k p) e -> p k e", p=P)

        def over_chunks(x):
            return x[:].rearrange("p (a h) -> p a h", a=1).to_broadcast([P, N_CHUNK, HEADS])
        with nc.Block(no_gpsimd_drain=True) as block:

            @block.sync
            def _(sync):
                sync.dma_start(wg[:], w_v[:, :, COL["beta"]:COL["beta"] + 2 * HEADS]).then_inc(sl, 16)
                sync.dma_start(a_log[:], K.dram["gd_A_log_2"].to_broadcast([P, HEADS])).then_inc(sl, 16)
                sync.dma_start(dt[:], K.dram["gd_dt_bias_2"].to_broadcast([P, HEADS])).then_inc(sl, 16)
                for k in range(KD):
                    sync.dma_start(w[:, k, :], w_v[:, k, COL["hi"]:COL["hi"] + HW]).then_inc(wl[k], 16)
                W_next.start(sync)
                W_next.first("load", sync, lambda q: w_v[:, :, COL["gq"] + q * P:COL["gq"] + (q + 1) * P])

            @block.tensor
            def _(pe):
                pe.wait_ge(split, 1)
                for g in range(3):
                    cols = slice(g * THIRD, (g + 1) * THIRD)
                    for k in range(KD):
                        last = three_products(pe, K.ps[0:2 * HEADS, g, 0:THIRD], wgp.hi[:, k, :], wgp.lo[:, k, :],
                                              hT.hi[:, k, cols], hT.lo[:, k, cols], k == 0, k == KD - 1)
                last.then_inc(rows_done, 1)
                pe.wait_ge(rows_out, 1)
                for c in range(N_CHUNK):
                    last = pe.transpose(K.ps[:, 7, 8 * c:8 * c + 8], rows[:, c * P:(c + 1) * P],
                                        K.ident[0:2 * HEADS, 0:2 * HEADS])
                last.then_inc(gated, 1)
                for c in range(N_CHUNK):
                    if c >= 6:
                        pe.wait_ge(out, c - 5)
                    for k in range(KD):
                        pe.wait_ge(split, k + 2)
                        cols = slice(c * P, (c + 1) * P)
                        last = three_products(pe, K.ps[:, c % 6, :], hT.hi[:, k, cols], hT.lo[:, k, cols],
                                              wp.hi[:, k, :], wp.lo[:, k, :], k == 0, k == KD - 1)
                    last.then_inc(done, 1)
                pe.wait_ge(step, 5)
                pe.matmul(K.ps[:, 6, 0:N_CHUNK * HEADS], K.upper[:], t[:, 5, :, :].rearrange("p c h -> p (c h)"),
                          start=True, stop=True).then_inc(gated, 1)

            @block.scalar
            def _(act):
                act.wait_ge(sl, 48)
                act.activation(wgp.hi[:], wg[:], ACT.Copy).then_inc(rounded, 1)
                for k in range(KD):
                    act.wait_ge(wl[k], 16)
                    act.activation(wp.hi[:, k, :], w[:, k, :], ACT.Copy).then_inc(rounded, 1)
                act.wait_ge(gated, 1)
                view = K.ps[:, 7, 0:8 * N_CHUNK].rearrange("p (c j) -> p c j", j=8)
                act.wait_ge(step, 1)
                act.activation(beta[:], view[:, :, 0:HEADS], ACT.Sigmoid).then_inc(acted, 1)
                act.wait_ge(step, 2)
                act.activation(t[:, 2, :, :], t[:, 1, :, :], ACT.Exp).then_inc(acted, 1)
                act.activation(a_log[:], a_log[:], ACT.Exp).then_inc(acted, 1)
                act.wait_ge(acted, 3)
                act.activation(t[:, 3, :, :], t[:, 2, :, :], ACT.Ln, bias=K.ones[:, 0:1]).then_inc(acted, 1)
                for c in range(N_CHUNK):
                    act.wait_ge(done, c + 1)
                    if c >= 4:
                        act.wait_ge(stored, 16 * (c - 3))
                    act.activation(st[:, c % 4, :], K.ps[:, c % 6, :], ACT.Copy).then_inc(out, 1)
                    if c == 5:
                        W_next.first("round", act)
                act.wait_ge(gated, 2)
                act.activation(G[:].rearrange("p c h -> p (c h)"), K.ps[:, 6, 0:N_CHUNK * HEADS], ACT.Copy).then_inc(acted, 1)

            @block.vector
            def _(dve):
                dve.wait_ge(rounded, 1)
                dve.tensor_tensor(wgp.lo[:], wg[:], wgp.hi[:], ALU.subtract).then_inc(split, 1)
                for k in range(KD):
                    if k == 4:
                        dve.wait_ge(rows_done, 1)
                        dve.tensor_copy(rows[:].rearrange("p (g n) -> p g n", g=3), K.ps[0:2 * HEADS, 0:3, 0:THIRD]
                                        ).then_inc(rows_out, 1)
                    dve.wait_ge(rounded, k + 2)
                    dve.tensor_tensor(wp.lo[:, k, :], w[:, k, :], wp.hi[:, k, :], ALU.subtract).then_inc(split, 1)
                dve.wait_ge(gated, 1)
                view = K.ps[:, 7, 0:8 * N_CHUNK].rearrange("p (c j) -> p c j", j=8)
                dve.tensor_tensor(t[:, 0, :, :], view[:, :, HEADS:], over_chunks(dt), ALU.add).then_inc(step, 1)
                dve.wait_ge(step, 1)
                dve.scalar_tensor_tensor(out=t[:, 1, :, :], in0=t[:, 0, :, :], scalar=-1.0, in1=t[:, 0, :, :],
                                         op0=ALU.mult, op1=ALU.min).then_inc(step, 1)
                dve.wait_ge(acted, 4)
                dve.scalar_tensor_tensor(out=t[:, 4, :, :], in0=t[:, 0, :, :], scalar=0.0, in1=t[:, 3, :, :],
                                         op0=ALU.max, op1=ALU.add).then_inc(step, 1)
                dve.wait_ge(step, 3)
                dve.scalar_tensor_tensor(out=t[:, 5, :, :], in0=t[:, 4, :, :], scalar=-1.0, in1=over_chunks(a_log),
                                         op0=ALU.mult, op1=ALU.mult).then_inc(step, 2)

            @block.gpsimd
            def _(gp):
                for c in range(N_CHUNK):
                    gp.wait_ge(out, c + 1)
                    gp.dma_start(K.scr["v_a"][c * P:(c + 1) * P, :], st[:, c % 4, :]).then_inc(stored, 16)
                    gp.wait_ge(stored, 16 * (c + 1))
                    if c == 6:
                        W_next.first("rest", gp)
                gp.wait_ge(W_next.split[-1], 2)


def stage_conv_qkv(nc, K, hT, W):
    TAPS = 4
    N = META + SEQ
    tiles = [(name, i) for name in ("gq", "gk", "gv") for i in range(HEADS)]
    scale = {"gq": P ** -0.5, "gk": 1.0}
    with ExitStack() as ctx:
        copied, conved, silued, squared, norm_done, rooted, inverted, ready, ready_v, stored, step, padded = semaphores(
            nc, K, "cv_copied", "cv_conved", "cv_silued", "cv_squared", "cv_norm_done",
            "cv_rooted", "cv_inverted", "cv_ready", "cv_ready_v", "cv_stored", "cv_step", "cv_padded")
        cin = ctx.enter_context(nc.sbuf_tensor("cv_in", [P, 2, N + TAPS - 1], FP32))
        cv = ctx.enter_context(nc.sbuf_tensor("cv_cv", [P, 2, N], FP32))
        sq = ctx.enter_context(nc.sbuf_tensor("cv_sq", [P, 2, N], FP32))
        inv = ctx.enter_context(nc.sbuf_tensor("cv_inv", [P, N], FP32))
        st = ctx.enter_context(nc.sbuf_tensor("cv_st", [P, 2, LEN], FP32))
        w_v = K.dram["w_in_2"][0].rearrange("(k p) e -> p k e", p=P)
        n_norm = 2 * HEADS

        def banks(x, q):
            return x[:, 4 * q:4 * q + 4, 0:QUART]

        def quarters(x):
            return x.rearrange("p (b n) -> p b n", b=4)
        with nc.Block(no_gpsimd_drain=True) as block:

            @block.sync
            def _(sync):
                for n, (name, i) in enumerate(tiles):
                    at = COL[name] + i * P
                    if n >= 2:
                        W.load(sync, n % 2, n // 2, w_v[:, :, at:at + P])

            @block.tensor
            def _(pe):
                def length(m):
                    if 0 <= m < n_norm:
                        pe.wait_ge(squared, m + 1)
                        for b in range(4):
                            last = pe.matmul(K.ps[:, 4 * (m % 2) + b, 0:QUART], K.ones[:],
                                             sq[:, m % 2, b * QUART:(b + 1) * QUART], start=True, stop=True)
                        last.then_inc(norm_done, 1)

                for n in range(len(tiles) + 1):
                    if n < len(tiles):
                        if n >= 2:
                            if n - 2 < n_norm:
                                pe.wait_ge(rooted, n - 1)
                            else:
                                pe.wait_ge(copied, n - 1)
                        project(pe, K.ps, 4 * (n % 2), W, n % 2, n // 2, hT, [QUART] * 4, LEAD,
                                before_last=lambda: length(n - 1))
                    else:
                        length(n - 1)

            @block.scalar
            def _(act):
                act.wait_ge(padded, 1)
                for n in range(len(tiles) + 1):
                    m = n - 1
                    if 0 <= m < n_norm:
                        act.wait_ge(norm_done, m + 1)
                        act.activation(quarters(sq[:, m % 2, :]), banks(K.ps, m % 2), ACT.Sqrt,
                                       bias=K.eps_rms[:, 0:1]).then_inc(rooted, 1)
                    if n < len(tiles):
                        act.wait_ge(W.done[n % 2], n // 2 + 2)
                        if n >= 2:
                            act.wait_ge(conved, n - 1)
                        act.activation(quarters(cin[:, n % 2, TAPS - 1:]), banks(K.ps, n % 2), ACT.Copy).then_inc(copied, 1)
                        if n + 2 < len(tiles):
                            W.round(act, n % 2, n // 2 + 1)
                    if n < len(tiles):
                        act.wait_ge(conved, n + 1)
                        if n < n_norm:
                            act.activation(cv[:, n % 2, :], cv[:, n % 2, :], ACT.Silu).then_inc(silued, 1)
                            act.wait_ge(silued, n + 1)
                            if n >= 2:
                                act.wait_ge(inverted, n - 1)
                            act.activation(sq[:, n % 2, :], cv[:, n % 2, :], ACT.Square).then_inc(squared, 1)
                        else:
                            act.wait_ge(stored, 16 * (n - 1))
                            act.activation(st[:, n % 2, LEAD:], cv[:, n % 2, :], ACT.Silu).then_inc(ready_v, 1)

            @block.vector
            def _(dve):
                for n in range(len(tiles) + 1):
                    if n < len(tiles):
                        name, i = tiles[n]
                        c = 4 * ("gq", "gk", "gv").index(name) + i
                        dve.wait_ge(copied, n + 1)
                        if n >= 2:
                            if n - 2 < n_norm:
                                dve.wait_ge(ready, n - 1)
                            else:
                                dve.wait_ge(ready_v, n - 1 - n_norm)
                        for k in range(TAPS):
                            src = cin[:, n % 2, k:k + N]
                            tap = param(K, "gd_conv_w_2", 12 * k + c)
                            if k == 0:
                                ins = dve.tensor_scalar(cv[:, n % 2, :], src, tap, None, ALU.mult)
                            else:
                                ins = dve.scalar_tensor_tensor(out=cv[:, n % 2, :], in0=src, scalar=tap,
                                                               in1=cv[:, n % 2, :], op0=ALU.mult, op1=ALU.add)
                            if k < TAPS - 1:
                                ins.then_inc(step, 1)
                                dve.wait_ge(step, (TAPS - 1) * n + k + 1)
                            else:
                                ins.then_inc(conved, 1)
                    m = n - 1
                    if 0 <= m < n_norm:
                        dve.wait_ge(rooted, m + 1)
                        dve.reciprocal(inv[:], sq[:, m % 2, :]).then_inc(inverted, 1)
                        dve.wait_ge(inverted, m + 1)
                        if m >= 2:
                            dve.wait_ge(stored, 16 * (m - 1))
                        dve.scalar_tensor_tensor(out=st[:, m % 2, LEAD:], in0=cv[:, m % 2, :], scalar=scale[tiles[m][0]],
                                                 in1=inv[:], op0=ALU.mult, op1=ALU.mult).then_inc(ready, 1)

            @block.gpsimd
            def _(gp):
                gp.memset(cin[:, :, 0:TAPS - 1], 0.0)
                gp.memset(st[:, :, 0:LEAD], 0.0).then_inc(padded, 1)
                gp.wait_ge(padded, 1)
                for n in range(len(tiles) + 1):
                    if n + 2 < len(tiles):
                        W.rest(gp, n % 2, n // 2 + 1)
                    m = n - 1
                    if m >= 0:
                        name, i = tiles[m]
                        if m < n_norm:
                            gp.wait_ge(ready, m + 1)
                        else:
                            gp.wait_ge(ready_v, m + 1 - n_norm)
                        gp.dma_start(K.scr[name][i * P:(i + 1) * P, :], st[:, m % 2, :]).then_inc(stored, 16)
                        gp.wait_ge(stored, 16 * (m + 1))


def stage_gates(nc, K, hT, metaT):
    groups = [("hq", 4, ACT.Silu, K.scr["q_a"][:, P:]), ("hg", 4, ACT.Silu, K.scr["gate"][0:HW, :]),
              ("gz", 4, ACT.Silu, K.scr["gate"][HW:, :]), ("pre_ga", 8, ACT.Sigmoid, K.scr["merge_a"]),
              ("pre_gb", 8, ACT.Sigmoid, K.scr["merge_b"])]
    with ExitStack() as ctx:
        norm = RmsNorm(nc, K, ctx, "n4", "norm_mix_g_2", [(K.xT, 0, hT, P, HALF), (K.xT, HALF, hT, P + HALF, HALF),
                                                          (metaT, 0, hT, LEAD, META)])
        free = semaphores(nc, K, *[f"ga_free{q}" for q in range(4)])
        stored = semaphores(nc, K, *[f"ga_stored{q}" for q in range(4)])
        W = Weights(nc, K, ctx, "ga", 4, KD)
        st = ctx.enter_context(nc.sbuf_tensor("ga_st", [P, 4, SEQ], FP32))
        w_v = K.dram["w_in_2"][0].rearrange("(k p) e -> p k e", p=P)

        def turns(eng, body):
            base = 0
            for g in groups:
                for it in range(g[1] // 4):
                    body(g, it, it + base)
                base += g[1] // 4
        total = sum(g[1] // 4 for g in groups)
        with nc.Block(no_gpsimd_drain=True) as block:

            @block.sync
            def _(sync):
                W.start(sync)

                def body(g, it, n):
                    for q in range(4):
                        W.load(sync, q, n, w_v[:, :, bass.ds(it * (4 * P) + (COL[g[0]] + q * P), P)])
                turns(sync, body)

            @block.gpsimd
            def _(gp):
                norm.gpsimd(gp, lambda g: W.rest(gp, g, 0))
                W.rest(gp, 3, 0)
                with gp.Fori(1, total) as n:
                    for q in range(4):
                        W.rest(gp, q, n)

            @block.tensor
            def _(pe):
                norm.tensor(pe)
                with pe.Fori(0, total) as n:
                    for q in range(4):
                        pe.wait_ge(free[q], n + 1)
                        if q == 2:
                            pe.wait_ge(norm.rooted, 3)
                        project(pe, K.ps, 2 * q, W, q, n, hT, [HALF, HALF], P, ready=norm.ready)

            @block.scalar
            def _(act):
                for q in range(4):
                    act.sem_inc(free[q], 1)
                    act.sem_inc(stored[q], 16)
                norm.scalar(act, lambda g: W.round(act, g, 0))
                W.round(act, 3, 0)

                def body(g, it, n):
                    for q in range(4):
                        act.wait_ge(W.done[q], n + 2)
                        act.wait_ge(stored[q], n * 16 + 16)
                        act.activation(st[:, q, :], pair(K.ps, q), g[2]).then_inc(free[q], 1)
                        if not (isinstance(n, int) and n == total - 1):
                            W.round(act, q, n + 1)
                        act.wait_ge(free[q], n + 2)
                        act.dma_start(g[3][bass.ds(it * (4 * P) + q * P, P), :], st[:, q, :]).then_inc(stored[q], 16)
                turns(act, body)
                for q in range(4):
                    act.wait_ge(stored[q], 16 * (total + 1))

            @block.vector
            def _(dve):
                norm.vector(dve)


def second_projections(nc, K, G, beta):
    with ExitStack() as ctx:
        metaT = ctx.enter_context(nc.sbuf_tensor("metaT", [P, KD, META], FP32))
        lb = ctx.enter_context(nc.sbuf_tensor("lb", [P, 2 * HEADS], FP32))
        hT = Halves(nc, ctx, "hT2", [P, KD, LEN])
        zeroed, = semaphores(nc, K, "lead_zeroed")
        stage_meta(nc, K, metaT)
        with nc.Block(no_gpsimd_drain=True) as block:

            @block.gpsimd
            def _(gp):
                gp.memset(hT.hi[:, :, 0:LEAD].bitcast(FP32), 0.0)
                gp.memset(hT.lo[:, :, 0:LEAD].bitcast(FP32), 0.0).then_inc(zeroed, 1)
                gp.wait_ge(zeroed, 1)
        stage_gates(nc, K, hT, metaT)
        with ExitStack() as inner:
            W = Weights(nc, K, inner, "fg", 2, KD)
            stage_lower_bounds(nc, K, lb, W)
            stage_forget(nc, K, hT, lb, W)
        W = Weights(nc, K, ctx, "cv", 2, KD)
        stage_by_tokens(nc, K, hT, G, beta, W)
        stage_conv_qkv(nc, K, hT, W)


def scratch(nc):
    shapes = dict(q_a=(HW, LEN), k_a=(HW, LEN), b_a=(HW, LEN), v_a=(LEN, HW), gq=(HW, LEN), gk=(HW, LEN), gv=(HW, LEN),
                  gate=(2 * HW, SEQ), p=(DFF, SEQ), merge_a=(D, SEQ), merge_b=(D, SEQ))
    scr = {n: nc.dram_tensor(f"scr_{n}", s, FP32, kind="Internal").ap() for n, s in shapes.items()}
    scr["h2"] = nc.dram_tensor("scr_h2", (SEQ, D), FP32, kind="Internal").ap()
    scr["y"] = nc.dram_tensor("scr_y", (N_BLOCK * P, D), FP32, kind="Internal").ap()
    scr["row_table"] = nc.dram_tensor("scr_row_table", (N_BLOCK * P, 1), I32, kind="Internal").ap()
    return scr



LEVELS = 7

EVENTS = dict(
    in_g=48, in_a=48, in_v=16,
    kq_ready=7, m_ready=7, added=7, qeb_ready=1, kdt_ready=1,
    bc_ready=1, eg_ready=1, rt_exp=1, ege_ready=1, eb_ready=1, e_ready=7, edb_ready=1, kd_ready=1, kda_ready=1,
    pm_ready=6, rs_ready=1, us_ready=1, og_out=1, oa_out=1,
    kb_ready=1, rt_ready=1, vb_ready=1, nk_ready=1, qe_ready=1, rt_masked=1, lt_ready=1, at_ready=1,
    d_ready=7, dbe_ready=1, masked=8, x_ready=6, y_ready=7, sg_ready=1, sa_ready=1,
    bcast_done=1, kk_done=1, kq_done=1, lev_done=8, m1t_done=1, p_done=6, dx_done=5, dy_done=6, kdat_done=1,
    r_done=1, u_done=1, o_done=1, dsg_done=1, oa_done=1, dsa_done=1)
MAKER = dict(sync="in_g in_a in_v", gpsimd="kq_ready m_ready added qeb_ready kdt_ready",
             scalar="bc_ready eg_ready rt_exp ege_ready eb_ready e_ready edb_ready kd_ready kda_ready pm_ready rs_ready us_ready og_out oa_out",
             vector="kb_ready rt_ready vb_ready nk_ready qe_ready rt_masked lt_ready at_ready d_ready dbe_ready masked x_ready y_ready sg_ready sa_ready",
             tensor="bcast_done kk_done kq_done lev_done m1t_done p_done dx_done dy_done kdat_done r_done u_done o_done dsg_done oa_done dsa_done")


def stage_recurrences(nc, K, G, beta, oT):
    C4 = [P, HEADS, P]
    with ExitStack() as ctx:
        ev = {n: semaphores(nc, K, f"rc_{n}")[0] for n in EVENTS}

        def buf(name, n=0):
            shape = [P, n, HEADS, P] if n else C4
            return ctx.enter_context(nc.sbuf_tensor(f"rc_{name}", shape, FP32))

        q_a, k_a, b_a, v_a, q_g, k_g, v_g = [buf(n) for n in ("q_a", "k_a", "b_a", "v_a", "q_g", "k_g", "v_g")]
        Gb, Bb, kb, rT, LT, Rs, us, Pm, X = [buf(n) for n in ("Gb", "Bb", "kb", "rT", "LT", "Rs", "us", "Pm", "X")]
        eG2, nkbe2, vb2, qe2, aT2, kd2, Y2 = [buf(n, 2) for n in ("eG", "nkbe", "vb", "qe", "aT", "kd", "Y")]
        eb2, qeb2, A2 = [buf(n, 2) for n in ("eb", "qeb", "A")]
        M = buf("M", LEVELS)
        KQ = buf("KQ", LEVELS)
        Dl = buf("D", 2)
        El = buf("E", 2)
        edb, kdT, kda = [buf(n) for n in ("edb", "kdT", "kda")]
        tmp = buf("tmp", 2)
        Sa, Sg = buf("Sa"), buf("Sg")
        ge = ctx.enter_context(nc.sbuf_tensor("rc_ge", [P, 2, HEADS], FP32))
        s_zero, = semaphores(nc, K, "rc_state_zero")

        def bank(n):
            return K.ps[:, n, :].rearrange("p (h t) -> p h t", h=HEADS)

        def all_heads(m):
            return m.rearrange("p (a t) -> p a t", a=1).to_broadcast(C4)

        def column(x, c):
            return x[:, bass.ds(c, 1), :].rearrange("p a (h b) -> p (a h) b", b=1).to_broadcast(C4)

        def halves_of(x, lev):
            m = 1 << lev
            v = x.rearrange("p h t -> p (h t)").rearrange("p (b s i) -> p b s i", s=2, i=m // 2)
            return v[:, :, 0, :], v[:, :, 1, :]

        def middle(x, lev):
            m = 1 << lev
            v = x.rearrange("p h t -> p (h t)").rearrange("p (b i) -> p b i", i=m)[:, :, m // 2 - 1:m // 2]
            return v.to_broadcast([P, HEADS * P // m, m // 2])

        def start(eng, kind):
            for n in MAKER[kind].split():
                eng.sem_inc(ev[n], EVENTS[n])

        def wait(eng, c, name, k=None):
            per = EVENTS[name]
            eng.wait_ge(ev[name], c * per + per + (per if k is None else k))

        def wait_before(eng, c, *names):
            for name in names:
                eng.wait_ge(ev[name], c * EVENTS[name] + EVENTS[name])

        LAST = ("x_ready", "y_ready", "kda_ready", "kdt_ready", "qeb_ready", "added")

        def over_chunks(eng, kind, front_and_tail, ahead=None):
            start(eng, kind)
            if ahead:
                ahead(0)
            front_and_tail(0, 0, True, False)
            with eng.Fori(0, (N_CHUNK - 1) // 2) as it:
                for j in range(2):
                    c = 2 * it + (j + 1)
                    if ahead:
                        ahead(c)
                    wait_before(eng, c, *LAST)
                    front_and_tail(c, (j + 1) % 2, True, True)
            wait_before(eng, N_CHUNK, *LAST)
            front_and_tail(N_CHUNK, N_CHUNK % 2, False, True)
        assert N_CHUNK % 2 == 1

        with nc.Block(no_gpsimd_drain=True) as block:

            @block.sync
            def _(sync):
                def by_channels(name, c):
                    return K.scr[name].rearrange("(h p) t -> p h t", p=P)[:, :, bass.ds(c * P, P)]

                def body(c):
                    wait_before(sync, c, "kq_done", "kb_ready", "vb_ready", "qe_ready")
                    for x, n in ((q_g, "gq"), (k_g, "gk"), (v_g, "gv")):
                        sync.dma_start(x[:], by_channels(n, c)).then_inc(ev["in_g"], 16)
                    wait_before(sync, c, "lev_done", "kq_ready", "dbe_ready", "d_ready", "qeb_ready", "kdt_ready", "eb_ready")
                    for x, n in ((q_a, "q_a"), (k_a, "k_a"), (b_a, "b_a")):
                        sync.dma_start(x[:], by_channels(n, c)).then_inc(ev["in_a"], 16)
                    wait_before(sync, c, "dsa_done")
                    sync.dma_start(v_a[:].rearrange("p h v -> p (h v)"), K.scr["v_a"][bass.ds(c * P, P), :]
                                   ).then_inc(ev["in_v"], 16)
                start(sync, "sync")
                with sync.Fori(0, N_CHUNK) as c:
                    body(c)

            @block.gpsimd
            def _(gp):
                gp.memset(Sa[:], 0.0)
                gp.memset(Sg[:], 0.0).then_inc(s_zero, 1)

                def body(c, p, front, tail):
                    if not front:
                        return
                    eb, qeb, A = eb2[:, p], qeb2[:, p], A2[:, p]

                    def kq(lev):
                        wait(gp, c, "e_ready", lev)
                        if lev == 1:
                            wait(gp, c, "in_a")
                        e = halves_of(El[:, lev % 2], lev)
                        for half, src in ((0, k_a), (1, q_a)):
                            ins = gp.tensor_tensor(halves_of(KQ[:, lev - 1], lev)[half], halves_of(src[:], lev)[half],
                                                   e[half], ALU.mult)
                        ins.then_inc(ev["kq_ready"], 1)

                    def m_level(lev):
                        if lev == 1:
                            wait(gp, c, "lt_ready")
                        gp.tensor_tensor(M[:, lev - 1], LT[:], all_heads(K.level[:, lev, :]), ALU.mult
                                         ).then_inc(ev["m_ready"], 1)

                    def add(lev):
                        wait(gp, c, "masked", lev + 1)
                        if lev > 1:
                            wait(gp, c, "added", lev - 1)
                        right = halves_of(A, lev)[1]
                        gp.tensor_tensor(right, right, halves_of(tmp[:, lev % 2], lev)[1], ALU.add).then_inc(ev["added"], 1)

                    m_level(1)
                    kq(1)
                    m_level(2)
                    kq(2)
                    for lev in range(3, LEVELS + 1):
                        kq(lev)
                        add(lev - 2)
                        m_level(lev)
                    wait(gp, c, "edb_ready")
                    gp.tensor_tensor(kdT[:], k_a[:], edb[:], ALU.mult).then_inc(ev["kdt_ready"], 1)
                    wait(gp, c, "eb_ready")
                    gp.tensor_tensor(qeb[:], q_a[:], eb[:], ALU.mult).then_inc(ev["qeb_ready"], 1)
                    add(LEVELS - 1)
                    add(LEVELS)
                over_chunks(gp, "gpsimd", body)

            @block.scalar
            def _(act):
                def body(c, p, front, tail):
                    eG, kd, eb = eG2[:, p], kd2[:, p], eb2[:, p]

                    def exp_level(lev):
                        wait(act, c, "d_ready", lev)
                        if lev > 2:
                            wait(act, c, "kq_ready", lev - 2)
                        act.activation(El[:, lev % 2], Dl[:, lev % 2], ACT.Exp).then_inc(ev["e_ready"], 1)

                    def tail_copy(done, out, b, ready):
                        if tail:
                            wait(act, c - 1, done)
                            act.activation(out, bank(b), ACT.Copy).then_inc(ev[ready], 1)

                    before = bass.ds((c - 1) * P if tail else 0, P)
                    tail_copy("r_done", Rs[:], 5, "rs_ready")
                    if front:
                        wait(act, c, "bcast_done")
                        act.activation(eG[:], bank(0), ACT.Exp).then_inc(ev["eg_ready"], 1)
                    tail_copy("u_done", us[:], 6, "us_ready")
                    if front:
                        wait(act, c, "rt_ready")
                        act.activation(rT[:], rT[:], ACT.Exp).then_inc(ev["rt_exp"], 1)
                        act.activation(ge[:, 1, :], ge[:, 0, :], ACT.Exp).then_inc(ev["ege_ready"], 1)
                        exp_level(1)
                    tail_copy("o_done", oT[:, HEADS:, before], 7, "og_out")
                    if front:
                        exp_level(2)
                        wait(act, c, "kq_done")
                        wait(act, c, "ege_ready")
                        for h in range(HEADS):
                            ins = act.activation(kd[:, h, :], bank(4)[:, h, :], ACT.Copy, scale=ge[:, 1, h:h + 1])
                        ins.then_inc(ev["kd_ready"], 1)
                        wait(act, c, "in_a")
                        act.activation(eb[:], b_a[:], ACT.Exp).then_inc(ev["eb_ready"], 1)
                        exp_level(3)
                        for lev in range(2, LEVELS + 1):
                            wait(act, c, "p_done", lev - 1)
                            if lev > 2:
                                wait(act, c, "dy_done", lev - 2)
                            act.activation(Pm[:], bank(5), ACT.Copy).then_inc(ev["pm_ready"], 1)
                            if lev + 2 <= LEVELS:
                                exp_level(lev + 2)
                            if lev == 4:
                                tail_copy("oa_done", oT[:, 0:HEADS, before], 2, "oa_out")
                            if lev == 5:
                                wait(act, c, "dbe_ready")
                                act.activation(edb[:], edb[:], ACT.Exp, scale=-1.0).then_inc(ev["edb_ready"], 1)
                        wait(act, c, "kdat_done")
                        act.activation(kda[:], bank(4), ACT.Copy).then_inc(ev["kda_ready"], 1)
                    else:
                        tail_copy("oa_done", oT[:, 0:HEADS, before], 2, "oa_out")

                def ahead(c):
                    wait_before(act, c, "bcast_done")
                    act.activation(Gb[:], column(G, c), ACT.Copy)
                    act.activation(Bb[:], column(beta, c), ACT.Copy).then_inc(ev["bc_ready"], 1)
                over_chunks(act, "scalar", body, ahead)

            @block.vector
            def _(dve):
                def body(c, p, front, tail):
                    eG, nkbe, vb, qe, aT, Y, A = [x[:, p] for x in (eG2, nkbe2, vb2, qe2, aT2, Y2, A2)]

                    def state(name, S, e2, b):
                        if tail:
                            e = e2[:, 1 - p]
                            wait(dve, c - 1, f"ds{name}_done")
                            for h in range(HEADS):
                                ins = dve.scalar_tensor_tensor(out=S[:, h, :], in0=S[:, h, :], scalar=e[:, h, P - 1:P],
                                                               in1=bank(b)[:, h, :], op0=ALU.mult, op1=ALU.add)
                            ins.then_inc(ev[f"s{name}_ready"], 1)

                    if not front:
                        state("g", Sg, eG2, 5)
                        state("a", Sa, eb2, 3)
                        return

                    def exponents(lev):
                        if lev == 1:
                            wait(dve, c, "in_a")
                        if lev > 2:
                            wait(dve, c, "e_ready", lev - 2)
                        left, right = halves_of(Dl[:, lev % 2], lev)
                        b_left, b_right = halves_of(b_a[:], lev)
                        dve.tensor_tensor(left, middle(b_a[:], lev), b_left, ALU.subtract)
                        dve.tensor_tensor(right, b_right, middle(b_a[:], lev), ALU.subtract).then_inc(ev["d_ready"], 1)

                    def mask(lev):
                        wait(dve, c, "lev_done", lev + 1)
                        if lev > 2:
                            wait(dve, c, "added", lev - 2)
                        dst = A[:] if lev == 0 else tmp[:, lev % 2]
                        dve.tensor_tensor(dst, bank(lev % 2), all_heads(K.level[:, lev, :]), ALU.mult
                                          ).then_inc(ev["masked"], 1)

                    wait(dve, c, "eg_ready")
                    wait(dve, c, "in_g")
                    dve.tensor_tensor(kb[:], k_g[:], bank(1), ALU.mult).then_inc(ev["kb_ready"], 1)
                    for h in range(HEADS):
                        dve.tensor_scalar(rT[:, h, :], bank(0)[:, h, :],
                                          G[:, bass.ds(c, 1), h:h + 1].rearrange("p a b -> p (a b)"), 0.0,
                                          ALU.subtract, ALU.min)
                    dve.tensor_tensor(ge[:, 0, :], K.ps[:, 0, P - 1::P], G[:, bass.ds(c, 1), :].rearrange("p a h -> p (a h)"),
                                      ALU.subtract).then_inc(ev["rt_ready"], 1)
                    dve.tensor_tensor(vb[:], v_g[:], bank(1), ALU.mult).then_inc(ev["vb_ready"], 1)
                    wait(dve, c, "kb_ready")
                    dve.scalar_tensor_tensor(out=nkbe[:], in0=kb[:], scalar=-1.0, in1=eG[:], op0=ALU.mult,
                                             op1=ALU.mult).then_inc(ev["nk_ready"], 1)
                    dve.tensor_tensor(qe[:], q_g[:], eG[:], ALU.mult).then_inc(ev["qe_ready"], 1)
                    wait(dve, c, "rt_exp")
                    dve.tensor_tensor(rT[:], rT[:], all_heads(K.upper[:]), ALU.mult).then_inc(ev["rt_masked"], 1)
                    wait(dve, c, "kk_done")
                    wait(dve, c, "rt_masked")
                    dve.tensor_tensor(LT[:], bank(2), rT[:], ALU.mult).then_inc(ev["lt_ready"], 1)
                    exponents(1)
                    wait(dve, c, "kq_done")
                    dve.tensor_tensor(aT[:], bank(3), rT[:], ALU.mult).then_inc(ev["at_ready"], 1)
                    exponents(2)
                    state("g", Sg, eG2, 5)
                    mask(0)
                    mask(1)
                    exponents(3)
                    wait(dve, c, "m_ready", 1)
                    wait(dve, c, "m1t_done")
                    dve.tensor_tensor(X[:], all_heads(K.ident[:]), bank(5), ALU.subtract).then_inc(ev["x_ready"], 1)
                    dve.tensor_tensor(Y[:], all_heads(K.ident[:]), M[:, 0], ALU.subtract).then_inc(ev["y_ready"], 1)
                    for lev in range(2, LEVELS + 1):
                        mask(lev)
                        if lev + 2 <= LEVELS:
                            exponents(lev + 2)
                        if lev == 4:
                            for h in range(HEADS):
                                ins = dve.tensor_scalar(edb[:, h, :], b_a[:, h, :], b_a[:, h, P - 1:P], None, ALU.subtract)
                            ins.then_inc(ev["dbe_ready"], 1)
                        if lev == 6:
                            state("a", Sa, eb2, 3)
                        if lev < LEVELS:
                            wait(dve, c, "dx_done", lev - 1)
                            wait(dve, c, "x_ready", lev - 1)
                            left = halves_of(X[:], lev)[0]
                            dve.tensor_tensor(left, left, halves_of(bank(6), lev)[0], ALU.subtract).then_inc(ev["x_ready"], 1)
                        wait(dve, c, "dy_done", lev - 1)
                        wait(dve, c, "y_ready", lev - 1)
                        right = halves_of(Y, lev)[1]
                        dve.tensor_tensor(right, right, halves_of(bank(7), lev)[1], ALU.subtract).then_inc(ev["y_ready"], 1)
                over_chunks(dve, "vector", body)

            @block.tensor
            def _(pe):
                ident = K.ident[:]

                def heads(b, *terms):
                    for h in range(HEADS):
                        for n, (lhsT, rhs) in enumerate(terms):
                            r = ident if rhs is None else rhs[:, h, :]
                            last = pe.matmul(bank(b)[:, h, :], lhsT[:, h, :], r, start=(n == 0), stop=(n == len(terms) - 1))
                    return last

                def turn(b, x):
                    for h in range(HEADS):
                        last = pe.transpose(bank(b)[:, h, :], x[:, h, :], ident)
                    return last

                def body(c, p, front, tail):
                    nkbe, vb, qe, aT, kd, Y, qeb, A = [x[:, 1 - p] for x in (nkbe2, vb2, qe2, aT2, kd2, Y2, qeb2, A2)]
                    t = c - 1

                    def right_side():
                        heads(5, (vb, None), (nkbe, Sg)).then_inc(ev["r_done"], 1)

                    def solved():
                        wait(pe, t, "rs_ready")
                        heads(6, (Y, Rs)).then_inc(ev["u_done"], 1)

                    def out_g():
                        wait(pe, t, "us_ready")
                        heads(7, (Sg, qe), (us, aT)).then_inc(ev["o_done"], 1)

                    def state_g():
                        heads(5, (kd, us)).then_inc(ev["dsg_done"], 1)

                    def out_a():
                        wait(pe, t, "in_v")
                        heads(2, (Sa, qeb), (v_a, A)).then_inc(ev["oa_done"], 1)

                    def state_a():
                        heads(3, (kda, v_a)).then_inc(ev["dsa_done"], 1)

                    if not front:
                        wait(pe, t - 1, "sg_ready")
                        wait(pe, t - 1, "sa_ready")
                        for step in (right_side, solved, out_g, state_g, out_a, state_a):
                            step()
                        return
                    new_Y = Y2[:, p]

                    def level(lev):
                        if lev == 0:
                            wait(pe, c, "in_a")
                            wait(pe, c, "rt_ready")
                            heads(0, (k_a, q_a)).then_inc(ev["lev_done"], 1)
                            return
                        if lev == 1:
                            wait(pe, c, "vb_ready")
                        else:
                            wait(pe, c, "masked", lev - 1)
                        wait(pe, c, "kq_ready", lev)
                        x = KQ[:, lev - 1]
                        heads(lev % 2, (x, x)).then_inc(ev["lev_done"], 1)

                    if tail:
                        wait(pe, t - 1, "sg_ready")
                        right_side()
                    if tail:
                        solved()
                    wait(pe, c, "in_g")
                    wait(pe, c, "kb_ready")
                    heads(2, (k_g, kb)).then_inc(ev["kk_done"], 1)
                    heads(3, (k_g, q_g))
                    turn(4, k_g).then_inc(ev["kq_done"], 1)
                    if tail:
                        out_g()
                        state_g()
                    level(0)
                    level(1)
                    if tail:
                        wait(pe, t, "sg_ready")
                    wait(pe, c, "m_ready", 1)
                    turn(5, M[:, 0]).then_inc(ev["m1t_done"], 1)
                    for lev in range(2, LEVELS + 1):
                        wait(pe, c, "x_ready", lev - 1)
                        wait(pe, c, "m_ready", lev)
                        heads(5, (M[:, lev - 1], X)).then_inc(ev["p_done"], 1)
                        level(lev)
                        if tail and lev == 2:
                            wait(pe, t, "og_out")
                        if tail and lev == 3:
                            wait(pe, c, "lt_ready")
                            wait(pe, t - 1, "sa_ready")
                            out_a()
                        if tail and lev == 4:
                            wait(pe, c, "at_ready")
                            state_a()
                        wait(pe, c, "pm_ready", lev - 1)
                        wait(pe, c, "y_ready", lev - 1)
                        if lev < LEVELS:
                            heads(6, (new_Y, Pm)).then_inc(ev["dx_done"], 1)
                        heads(7, (Pm, new_Y)).then_inc(ev["dy_done"], 1)
                    wait(pe, c, "kdt_ready")
                    wait(pe, c, "kd_ready")
                    turn(4, kdT).then_inc(ev["kdat_done"], 1)
                pe.wait_ge(s_zero, 1)

                def ahead(c):
                    wait_before(pe, c, "masked")
                    wait(pe, c, "bc_ready")
                    heads(0, (Gb, None))
                    heads(1, (Bb, None)).then_inc(ev["bcast_done"], 1)
                over_chunks(pe, "tensor", body, ahead)


def stage_head_norm(nc, K, oT, part):
    n_tiles = 2 * HEADS
    with ExitStack() as ctx:
        squared, summed, rooted, inverted, spread, scaled, gated, rounded, ready, chosen = semaphores(
            nc, K, "hn_squared", "hn_summed", "hn_rooted", "hn_inverted", "hn_spread", "hn_scaled", "hn_gated",
            "hn_rounded", "hn_ready", "hn_chosen")
        ready_b, inv_rounded, inv_split = semaphores(nc, K, "hn_ready_b", "hn_inv_rounded", "hn_inv_split")
        gate_in = semaphores(nc, K, *[f"hn_gate_in{i}" for i in range(n_tiles)])
        units = [(i, h * HALF) for i in range(n_tiles) for h in range(2)]
        N = len(units)
        gate = ctx.enter_context(nc.sbuf_tensor("hn_gate", [P, n_tiles, SEQ], FP32))
        sq = ctx.enter_context(nc.sbuf_tensor("hn_sq", [P, 4, HALF], FP32))
        to_row = ctx.enter_context(nc.sbuf_tensor("hn_to_row", [P, N, N], FP32))
        from_row = ctx.enter_context(nc.sbuf_tensor("hn_from_row", [N, N, P], FP32R))
        root = ctx.enter_context(nc.sbuf_tensor("hn_root", [N, 2, HALF], FP32))
        inv = Halves(nc, ctx, "hn_inv", [N, HALF])
        BY_VECTOR = [n for n in range(N) if n % 4 == 0]

        def o(n):
            i, at = units[n]
            return oT[:, i, P + at:P + at + HALF]

        def half(x, n):
            i, at = units[n]
            return x[:, i, at:at + HALF]
        with nc.Block(no_gpsimd_drain=True) as block:

            @block.sync
            def _(sync):
                for i in range(n_tiles):
                    sync.dma_start(gate[:, i, :], K.scr["gate"][i * P:(i + 1) * P, :]).then_inc(gate_in[i], 16)

            @block.scalar
            def _(act):
                act.activation(from_row[:], K.ident[0:N, 0:N].rearrange("p (n a) -> p n a", a=1).to_broadcast([N, N, P]),
                               ACT.Copy)
                for n in range(N):
                    if n >= 4:
                        act.wait_ge(summed, n - 3)
                    act.activation(sq[:, n % 4, :], o(n), ACT.Square).then_inc(squared, 1)
                act.wait_ge(summed, N)
                act.activation(root[:, 0, :], K.ps[0:N, 0, :], ACT.Sqrt, bias=K.eps_rms[0:N, 0:1], scale=1.0 / P
                               ).then_inc(rooted, 1)
                act.wait_ge(inverted, 1)
                act.activation(inv.hi[:], root[:, 1, :], ACT.Copy).then_inc(inv_rounded, 1)
                for n in range(N):
                    act.wait_ge(scaled, n + 1)
                    act.activation(half(part.hi, n), o(n), ACT.Copy).then_inc(rounded, 1)

            @block.tensor
            def _(pe):
                pe.wait_ge(chosen, 2)
                for n in range(N):
                    pe.wait_ge(squared, n + 1)
                    pe.matmul(K.ps[0:N, 0, :], to_row[:, n, :], sq[:, n % 4, :], start=(n == 0), stop=(n == N - 1)
                              ).then_inc(summed, 1)
                pe.wait_ge(inv_split, 1)
                for n in range(N):
                    if n >= 7:
                        pe.wait_ge(scaled, n - 6)
                    pe.matmul(K.ps[:, 1 + n % 7, :], from_row[:, n, :], inv.hi[:], start=True, stop=False)
                    pe.matmul(K.ps[:, 1 + n % 7, :], from_row[:, n, :], inv.lo[:], start=False, stop=True
                              ).then_inc(spread, 1)

            @block.vector
            def _(dve):
                dve.wait_ge(rooted, 1)
                dve.reciprocal(root[:, 1, :], root[:, 0, :]).then_inc(inverted, 1)
                dve.wait_ge(inv_rounded, 1)
                dve.tensor_tensor(inv.lo[:], root[:, 1, :], inv.hi[:], ALU.subtract).then_inc(inv_split, 1)
                for n in range(N + 1):
                    if n < N:
                        dve.wait_ge(spread, n + 1)
                        dve.wait_ge(gated, n + 1)
                        dve.scalar_tensor_tensor(out=o(n), in0=o(n), scalar=param(K, "hg_norm_g_2" if n < N // 2 else "gd_norm_g_2"),
                                                 in1=K.ps[:, 1 + n % 7, :], op0=ALU.mult, op1=ALU.mult).then_inc(scaled, 1)
                    m = n - 1
                    if m in BY_VECTOR:
                        dve.wait_ge(rounded, m + 1)
                        dve.tensor_tensor(half(part.lo, m), o(m), half(part.hi, m), ALU.subtract).then_inc(ready_b, 1)

            @block.gpsimd
            def _(gp):
                flat = to_row[:].rearrange("p a b -> p (a b)")
                gp.memset(flat, 0.0).then_inc(chosen, 1)
                gp.wait_ge(chosen, 1)
                gp.memset(flat[:, 0::N + 1], 1.0).then_inc(chosen, 1)
                for n in range(N):
                    gp.wait_ge(gate_in[units[n][0]], 16)
                    gp.wait_ge(squared, n + 1)
                    gp.tensor_tensor(o(n), o(n), half(gate, n), ALU.mult).then_inc(gated, 1)
                for n in range(N):
                    if n not in BY_VECTOR:
                        gp.wait_ge(rounded, n + 1)
                        gp.tensor_tensor(half(part.lo, n), o(n), half(part.hi, n), ALU.subtract).then_inc(ready, 1)
                gp.wait_ge(ready, N - len(BY_VECTOR))


def stage_merge(nc, K, oT, part, W_next, w_next):
    n_it = KD // 2
    with ExitStack() as ctx:
        gl = semaphores(nc, K, *[f"mg_gate_in{q}" for q in range(4)])
        free = semaphores(nc, K, *[f"mg_free{q}" for q in range(4)])
        merged, = semaphores(nc, K, "mg_merged")
        W = Weights(nc, K, ctx, "mg", 4, HEADS)
        g = ctx.enter_context(nc.sbuf_tensor("mg_g", [P, 4, SEQ], FP32))
        w_v = [K.dram[n][0].rearrange("(k p) e -> p k e", p=P) for n in ("hg_up_2", "gd_up_2")]
        g_v = [K.scr[n] for n in ("merge_a", "merge_b")]
        with nc.Block(no_gpsimd_drain=True) as block:

            @block.sync
            def _(sync):
                W.start(sync)
                with sync.Fori(0, n_it) as it:
                    for q in range(4):
                        cols = bass.ds(q // 2 * P + it * (2 * P), P)
                        W.load(sync, q, it, w_v[q % 2][:, :, cols])
                        sync.wait_ge(merged, 2 * it + q // 2 + 1)
                        sync.dma_start(g[:, q, :], g_v[q % 2][cols, :]).then_inc(gl[q], 16)
                W_next.start(sync)
                W_next.first("load", sync, residual_weights(w_next))

            @block.scalar
            def _(act):
                for q in range(4):
                    W.round(act, q, 0)
                with act.Fori(1, n_it) as it:
                    for q in range(4):
                        W.round(act, q, it)
                W_next.first("round", act)

            @block.tensor
            def _(pe):
                with pe.Fori(0, n_it) as it:
                    for q in range(4):
                        pe.wait_ge(free[q], it + 1)
                        side = slice(q % 2 * HEADS, (q % 2 + 1) * HEADS)
                        pe.wait_ge(W.split[q], it + 2)
                        for n in range(2):
                            cols = slice(n * HALF, (n + 1) * HALF)
                            for k in range(HEADS):
                                last = three_products(pe, K.ps[:, 2 * q + n, :], W.part.hi[:, q, k, :], W.part.lo[:, q, k, :],
                                                      part.hi[:, side, :][:, k, cols], part.lo[:, side, :][:, k, cols],
                                                      k == 0, k == HEADS - 1)
                        last.then_inc(W.done[q], 1)

            @block.vector
            def _(dve):
                for q in range(4):
                    dve.sem_inc(free[q], 1)
                with dve.Fori(0, n_it) as it:
                    for v in range(2):
                        for q in (2 * v, 2 * v + 1):
                            dve.wait_ge(W.done[q], it + 2)
                            dve.wait_ge(gl[q], 16 * it + 16)
                            dve.tensor_tensor(g[:, q, :], pair(K.ps, q), g[:, q, :], ALU.mult).then_inc(free[q], 1)
                        dve.wait_ge(free[2 * v + 1], it + 2)
                        dve.tensor_tensor(oT[:, bass.ds(2 * it + v, 1), P:], g[:, 2 * v:2 * v + 1, :],
                                          g[:, 2 * v + 1:2 * v + 2, :], ALU.add).then_inc(merged, 1)
                dve.wait_ge(merged, 2 + KD)

            @block.gpsimd
            def _(gp):
                gp.sem_inc(merged, 2)
                with gp.Fori(0, n_it) as it:
                    for q in range(4):
                        W.rest(gp, q, it)
                W_next.first("rest", gp)
                gp.wait_ge(W_next.split[-1], 2)



N_TILE = SEQ // P
N_GROUP = 4
N_EXPERT = 32
PER_GROUP = N_EXPERT // N_GROUP
N_LOGIT = N_GROUP + N_EXPERT
FE = 512
KE = FE // P
N_BLOCK = (2 * SEQ + N_EXPERT * (P - 1)) // P
N_BLOCK += N_BLOCK % 2
FAR = 1e30


def stage_to_tokens(nc, K, xt, L):
    with ExitStack() as ctx:
        turned, out, squared, inv_r, inv_i, normed, stored, in_, wscaled, logits, added = semaphores(
            nc, K, "tk_turned", "tk_out", "tk_squared", "tk_rooted", "tk_inverted", "tk_normed", "tk_stored", "tk_in",
            "tk_w_scaled", "tk_logits", "tk_added")
        gain = ctx.enter_context(nc.sbuf_tensor("tk_gain", [P, D], FP32))
        rw = ctx.enter_context(nc.sbuf_tensor("tk_rw", [P, KD, N_LOGIT], FP32))
        rb = ctx.enter_context(nc.sbuf_tensor("tk_rb", [P, N_LOGIT], FP32))
        junk = ctx.enter_context(nc.sbuf_tensor("tk_junk", [P, D], FP32))
        h = ctx.enter_context(nc.sbuf_tensor("tk_h", [P, 2, D], FP32))
        ss = ctx.enter_context(nc.sbuf_tensor("tk_ss", [P, 3, N_TILE], FP32))
        with nc.Block(no_gpsimd_drain=True) as block:

            @block.sync
            def _(sync):
                sync.dma_start(gain[:], K.dram["norm_ffn_g_2"].to_broadcast([P, D])).then_inc(in_, 16)
                sync.dma_start(rw[:, :, 0:N_GROUP], K.dram["router_group_w_2"][0].rearrange("(k p) e -> p k e", p=P)).then_inc(in_, 16)
                sync.dma_start(rw[:, :, N_GROUP:], K.dram["router_expert_w_2"][0].rearrange("(k p) e -> p k e", p=P)).then_inc(in_, 16)
                sync.dma_start(rb[:, 0:N_GROUP], K.dram["router_group_b_2"].to_broadcast([P, N_GROUP])).then_inc(in_, 16)
                sync.dma_start(rb[:, N_GROUP:], K.dram["router_expert_b_2"].to_broadcast([P, N_EXPERT])).then_inc(in_, 16)
                for t in range(N_TILE):
                    sync.wait_ge(normed, t + 1)
                    sync.dma_start(K.scr["h2"][t * P:(t + 1) * P, :], h[:, t % 2, :]).then_inc(stored, 16)
                    sync.wait_ge(stored, 16 * (t + 1))

            @block.tensor
            def _(pe):
                for n in range(2 * N_TILE):
                    t, g = n // 2, n % 2
                    if n >= 6:
                        pe.wait_ge(out, n - 5)
                    for k in range(4):
                        last = pe.transpose(K.ps[:, n % 6, k * P:(k + 1) * P], K.xT[:, 4 * g + k, t * P:(t + 1) * P], K.ident[:])
                    last.then_inc(turned, 1)
                pe.wait_ge(wscaled, 1)
                for t in range(N_TILE):
                    for k in range(KD):
                        last = pe.matmul(K.ps[:, 7, t * N_LOGIT:(t + 1) * N_LOGIT], K.xT[:, k, t * P:(t + 1) * P], rw[:, k, :],
                                         start=(k == 0), stop=(k == KD - 1))
                last.then_inc(logits, 1)

            @block.scalar
            def _(act):
                for n in range(2 * N_TILE):
                    t, g = n // 2, n % 2
                    act.wait_ge(turned, n + 1)
                    act.activation(xt[:, t, g * HALF:(g + 1) * HALF], K.ps[:, n % 6, :], ACT.Copy).then_inc(out, 1)
                for t in range(N_TILE):
                    act.wait_ge(out, 2 * (t + 1))
                    if t:
                        act.wait_ge(squared, t)
                    act.activation(junk[:], xt[:, t, :], ACT.Square, accum_out=ss[:, 0, t:t + 1]).then_inc(squared, 1)
                act.wait_ge(squared, N_TILE)
                act.activation(ss[:, 1, :], ss[:, 0, :], ACT.Sqrt, bias=K.eps_rms[:, 0:1], scale=1.0 / D).then_inc(inv_r, 1)

            @block.vector
            def _(dve):
                dve.wait_ge(in_, 16 * 5)
                for k in range(KD):
                    ins = dve.tensor_scalar(rw[:, k, :], rw[:, k, :], param(K, "norm_ffn_g_2", k), None, ALU.mult)
                ins.then_inc(wscaled, 1)
                dve.wait_ge(inv_r, 1)
                dve.reciprocal(ss[:, 2, :], ss[:, 1, :]).then_inc(inv_i, 1)
                dve.wait_ge(inv_i, 1)
                for t in range(N_TILE):
                    if t >= 2:
                        dve.wait_ge(stored, 16 * (t - 1))
                    dve.scalar_tensor_tensor(out=h[:, t % 2, :], in0=xt[:, t, :], scalar=ss[:, 2, t:t + 1], in1=gain[:],
                                             op0=ALU.mult, op1=ALU.mult).then_inc(normed, 1)
                dve.wait_ge(logits, 1)
                for t in range(N_TILE):
                    dve.scalar_tensor_tensor(out=L[:, t, :], in0=K.ps[:, 7, t * N_LOGIT:(t + 1) * N_LOGIT],
                                             scalar=ss[:, 2, t:t + 1], in1=rb[:], op0=ALU.mult, op1=ALU.add).then_inc(added, 1)
                dve.wait_ge(added, N_TILE)


def stage_route(nc, K, L, dest, weight, row_ids, experts):
    with ExitStack() as ctx:
        step, exped, ranked, filled, tok_made, scattered, tab_in, tab_f, turned = semaphores(
            nc, K, "rt_step", "rt_exped", "rt_ranked", "rt_filled", "rt_tok_made", "rt_scattered", "rt_tab_in", "rt_tab_f",
            "rt_turned")

        def sb(name, *shape, dt=FP32):
            return ctx.enter_context(nc.sbuf_tensor(f"rt_{name}", [P, *shape], dt))
        T, E, NG = N_TILE, N_EXPERT, N_GROUP
        gm, pg, s1, s2 = sb("gm", T), sb("pg", T), sb("s1", T), sb("s2", T)
        g4, g5, oh4 = sb("g4", T, NG), sb("g5", T, NG), sb("oh4", T, NG)
        Em, e1, e2 = sb("Em", T, E), sb("e1", T, E), sb("e2", T, E)
        oh = sb("oh", 2, T, E)
        both = sb("both", T, E)
        m = sb("m", 2, T)
        first = sb("first", E, dt=I32)
        firstf = sb("firstf", E)
        strict = sb("strict", P)
        tot, base = sb("tot", T, E), sb("base", T + 1, E)
        thr, thrf = sb("thr", T, dt=I32), sb("thrf", T)
        cmp = sb("cmp", E, T)
        nblk, cend, pstart = sb("nblk", E), sb("cend", E), sb("pstart", E)
        blk, blkf = sb("blk", N_BLOCK, dt=I32), sb("blkf", N_BLOCK)
        bcmp, bexp = sb("bcmp", N_BLOCK, E), sb("bexp", N_BLOCK)
        slot, pick = sb("slot", T, E), sb("pick", T, E)
        destf = sb("destf", T, 2)
        tok = sb("tok", T, dt=I32)
        zero = sb("zero", N_BLOCK, dt=I32)
        tab = ctx.enter_context(nc.sbuf_tensor("rt_tab", [N_BLOCK, P], I32))
        tabf = ctx.enter_context(nc.sbuf_tensor("rt_tabf", [N_BLOCK, P], FP32))

        def last_dim(x, shape):
            n = len(x.shape)
            v = x.rearrange("p (t a) -> p t a", a=1) if n == 2 else x.rearrange("p t (g a) -> p t g a", a=1)
            return v.to_broadcast(shape)

        def mid_dim(x, shape):
            return x.rearrange("p (a n) -> p a n", a=1).to_broadcast(shape)
        with nc.Block(no_gpsimd_drain=True) as block:

            @block.gpsimd
            def _(gp):
                gp.memset(zero[:], 0).then_inc(tok_made, 1)
                gp.wait_ge(tok_made, 1)
                gp.dma_start(K.scr["row_table"].rearrange("(p j) a -> p (j a)", p=P), zero[:]).then_inc(filled, 16)
                gp.iota(tok[:], pattern=[[P, T]], base=0, channel_multiplier=1)
                gp.iota(first[:], pattern=[[-1, E]], base=E, channel_multiplier=0)
                gp.iota(thr[:], pattern=[[P, T]], base=0, channel_multiplier=0)
                gp.iota(blk[:], pattern=[[1, N_BLOCK]], base=0, channel_multiplier=0)
                gp.memset(base[:, 0, :], 0.0)
                gp.tensor_tensor(strict[:], K.upper[:], K.ident[:], ALU.subtract).then_inc(tok_made, 1)
                gp.wait_ge(filled, 16)
                gp.wait_ge(ranked, 1)
                for c in range(2):
                    for t in range(T):
                        gp.indirect_dma_start(out=K.scr["row_table"], out_offset=bass.IndirectOffsetOnAxis(ap=dest[:, c, t:t + 1], axis=0),
                                              in_=tok[:, t:t + 1], in_offset=None).then_inc(scattered, 16)
                gp.wait_ge(scattered, 16 * 2 * T)
                gp.dma_start(tab[:], K.scr["row_table"].rearrange("(j p) a -> j (p a)", p=P)).then_inc(tab_in, 16)
                gp.wait_ge(tab_in, 16)

            @block.scalar
            def _(act):
                act.wait_ge(exped, 1)
                act.activation(g5[:], g4[:], ACT.Exp).then_inc(exped, 1)
                act.wait_ge(exped, 3)
                act.activation(s2[:], s1[:], ACT.Exp).then_inc(exped, 1)

            @block.tensor
            def _(pe):
                pe.wait_ge(tok_made, 2)
                pe.wait_ge(turned, 1)
                flat = both[:].rearrange("p t e -> p (t e)")
                pe.matmul(K.ps[:, 0, 0:T * E], strict[:], flat, start=True, stop=True)
                pe.matmul(K.ps[:, 1, 0:T * E], K.ones[:], flat, start=True, stop=True).then_inc(turned, 1)
                pe.wait_ge(tab_f, 1)
                pe.transpose(K.ps[:, 2, 0:N_BLOCK], tabf[:], K.ident[0:N_BLOCK, 0:N_BLOCK]).then_inc(turned, 1)

            @block.vector
            def _(dve):
                n = [0]

                def link(ins):
                    n[0] += 1
                    ins.then_inc(step, 1)
                    dve.wait_ge(step, n[0])

                Lg = L[:, :, 0:NG]
                Le = L[:, :, NG:]
                dve.wait_ge(tok_made, 2)
                link(dve.tensor_copy(firstf[:], first[:]))
                link(dve.tensor_copy(thrf[:], thr[:]))
                link(dve.tensor_copy(blkf[:], blk[:]))
                link(dve.tensor_reduce(gm[:], Lg, AX.X, ALU.max))
                dve.tensor_tensor(g4[:], Lg, last_dim(gm[:], [P, T, NG]), ALU.subtract).then_inc(exped, 1)
                dve.wait_ge(exped, 2)
                link(dve.tensor_reduce(pg[:], g5[:], AX.X, ALU.add))
                link(dve.reciprocal(pg[:], pg[:]))

                def first_largest(out, x, top, width, tie):
                    shape = [P, T, width]
                    link(dve.tensor_tensor(out, x, last_dim(top, shape), ALU.is_equal))
                    link(dve.tensor_tensor(tie, out, mid_dim(firstf[:, 0:width], shape), ALU.mult))
                    link(dve.tensor_reduce(s1[:], tie, AX.X, ALU.max))
                    link(dve.tensor_tensor(out, tie, last_dim(s1[:], shape), ALU.is_equal))

                first_largest(oh4[:], Lg, gm[:], NG, g4[:])
                link(dve.tensor_scalar(g4[:], oh4[:], -1.0, FAR, ALU.add, ALU.mult))
                view = [P, T, NG, PER_GROUP]
                link(dve.tensor_tensor(Em[:].rearrange("p t (g e) -> p t g e", g=NG), Le.rearrange("p t (g e) -> p t g e", g=NG),
                                       last_dim(g4[:], view), ALU.add))
                link(dve.tensor_reduce(m[:, 0, :], Em[:], AX.X, ALU.max))
                first_largest(oh[:, 0], Em[:], m[:, 0, :], E, e1[:])
                link(dve.scalar_tensor_tensor(out=e2[:], in0=oh[:, 0], scalar=-3.0 * FAR, in1=Em[:], op0=ALU.mult, op1=ALU.add))
                link(dve.tensor_reduce(m[:, 1, :], e2[:], AX.X, ALU.max))
                first_largest(oh[:, 1], e2[:], m[:, 1, :], E, e1[:])
                dve.tensor_tensor(both[:], oh[:, 0], oh[:, 1], ALU.add).then_inc(turned, 1)
                dve.tensor_tensor(s1[:], m[:, 1, :], m[:, 0, :], ALU.subtract).then_inc(exped, 1)
                dve.wait_ge(exped, 4)
                link(dve.tensor_scalar(gm[:], s2[:], 1.0, None, ALU.add))
                link(dve.reciprocal(s1[:], gm[:]))
                link(dve.tensor_tensor(weight[:, 0, :], pg[:], s1[:], ALU.mult))
                link(dve.tensor_tensor(weight[:, 1, :], weight[:, 0, :], s2[:], ALU.mult))
                dve.wait_ge(turned, 2)
                link(dve.tensor_copy(tot[:], K.ps[:, 1, 0:T * E].rearrange("p (t e) -> p t e", e=E)))
                for t in range(T):
                    link(dve.tensor_tensor(base[:, t + 1, :], base[:, t, :], tot[:, t, :], ALU.add))
                link(dve.tensor_tensor(cmp[:], last_dim(base[:, T, :], [P, E, T]), mid_dim(thrf[:], [P, E, T]), ALU.is_gt))
                link(dve.tensor_reduce(nblk[:], cmp[:], AX.X, ALU.add))
                link(dve.tensor_tensor_scan(cend[:], K.ones[:, 0:E], nblk[:], 0.0, ALU.mult, ALU.add))
                link(dve.tensor_tensor(pstart[:], cend[:], nblk[:], ALU.subtract))
                link(dve.tensor_scalar(pstart[:], pstart[:], float(P), None, ALU.mult))
                link(dve.tensor_tensor(slot[:], K.ps[:, 0, 0:T * E].rearrange("p (t e) -> p t e", e=E), base[:, 0:T, :], ALU.add))
                link(dve.tensor_tensor(slot[:], slot[:], mid_dim(pstart[:], [P, T, E]), ALU.add))
                for c in range(2):
                    link(dve.tensor_tensor(pick[:], slot[:], oh[:, c], ALU.mult))
                    link(dve.tensor_reduce(destf[:, :, c], pick[:], AX.X, ALU.add))
                    link(dve.tensor_copy(dest[:, c, :], destf[:, :, c]))
                dve.sem_inc(ranked, 1)
                shape = [P, N_BLOCK, E]
                link(dve.tensor_tensor(bcmp[:], mid_dim(cend[:], shape), last_dim(blkf[:], shape), ALU.is_le))
                link(dve.tensor_reduce(bexp[:], bcmp[:], AX.X, ALU.add))
                link(dve.tensor_scalar(bexp[:], bexp[:], float(E - 1), None, ALU.min))
                link(dve.tensor_copy(experts[:, 0:N_BLOCK], bexp[0:1, :]))
                even = blkf[0:1, 0::2]
                link(dve.tensor_tensor(bexp[0:1, 0::2], even, cend[0:1, E - 1:E].to_broadcast([1, N_BLOCK // 2]), ALU.is_lt))
                link(dve.tensor_reduce(nblk[0:1, 0:1], bexp[0:1, 0::2], AX.X, ALU.add))
                link(dve.tensor_copy(experts[:, N_BLOCK:], nblk[0:1, 0:1]))
                dve.wait_ge(tab_in, 16)
                dve.tensor_copy(tabf[:], tab[:]).then_inc(tab_f, 1)
                dve.wait_ge(turned, 3)
                link(dve.tensor_copy(row_ids[:], K.ps[:, 2, 0:N_BLOCK]))


def stage_experts(nc, K, row_ids, experts):
    PIECE = 4 * FE
    SLOTS = 4
    PIECES = 12
    TURNS = PIECES // SLOTS
    GATE, UP, DOWN = ((0, 1), (4, 5)), ((2, 3), (6, 7)), ((8, 9), (10, 11))
    BY_GPSIMD = (1, 4, 7, 10)
    with ExitStack() as ctx:
        def two(name):
            return semaphores(nc, K, f"ex_{name}0", f"ex_{name}1")
        gathered, stored = two("gathered"), two("stored")
        x_turned, x_hi, x_lo, silued, acted, a_turned, a_hi, a_lo, y_out, y_out_b, all_stored = semaphores(
            nc, K, *[f"ex_{n}" for n in ("x_turned", "x_hi", "x_lo", "silued", "acted", "a_turned", "a_hi", "a_lo",
                                         "y_out", "y_out_b", "all_stored")])
        pieces_begun, = semaphores(nc, K, "ex_pieces_begun")
        raw = K.xT[:].rearrange("p k t -> p (k t)").rearrange("p (s a n) -> p s a n", s=SLOTS, a=1)
        W = Weights(nc, K, ctx, "ex", SLOTS, 1, PIECE, raw=raw)
        xg = ctx.enter_context(nc.sbuf_tensor("ex_xg", [P, 2, D], FP32))
        X = Halves(nc, ctx, "ex_X", [P, 2, KD, P])
        sg = ctx.enter_context(nc.sbuf_tensor("ex_sg", [P, FE], FP32))
        ac = ctx.enter_context(nc.sbuf_tensor("ex_ac", [P, 2, FE], FP32))
        A = Halves(nc, ctx, "ex_A", [P, 2, KE, P])
        yo = ctx.enter_context(nc.sbuf_tensor("ex_yo", [P, 2, D], FP32))
        X_PAIR, Y_PAIR, GATE_BANK, UP_BANK, A_BANK = (0, 2), (0, 3), 2, 3, (4, 5)
        AHEAD = (0, 1, 2)
        g_v = K.dram["w_gate_2"][0].rearrange("e (p k) f -> p e (k f)", k=KD)
        u_v = K.dram["w_up_2"][0].rearrange("e (p k) f -> p e (k f)", k=KD)
        d_v = K.dram["w_down_2"][0].rearrange("e (p k) f -> p e (k f)", k=KE)

        def pairs(eng, body):
            used = eng.value_load(experts[0:1, N_BLOCK:N_BLOCK + 1], min_val=1, max_val=N_BLOCK // 2)
            with eng.Fori(0, N_BLOCK // 2) as it:
                with eng.If(it < used):
                    body(it)
            return used

        def uses(it, i):
            return it * TURNS + i // SLOTS

        def wait_piece(eng, it, i):
            eng.wait_ge(W.done[i % SLOTS], it * TURNS + (i // SLOTS + 2))

        with nc.Block(no_gpsimd_drain=True) as block:

            @block.sync
            def _(sync):
                W.start(sync)
                order = [(GATE, g_v, 0), (UP, u_v, 0), (GATE, g_v, 1), (UP, u_v, 1), (DOWN, d_v, 0), (DOWN, d_v, 1)]
                piece = {i: (view, c, q) for pieces, view, q in order for c, i in enumerate(pieces[q])}

                def expert(b):
                    return sync.value_load(experts[0:1, bass.ds(b, 1)], min_val=0, max_val=N_EXPERT - 1)

                def load(it, i, e):
                    view, c, q = piece[i]
                    W.load(sync, i % SLOTS, uses(it, i), view[:, bass.ds(e[q], 1), c * PIECE:(c + 1) * PIECE],
                           counted=pieces_begun)

                e = [expert(0)]
                for i in AHEAD:
                    load(0, i, e)

                def body(it):
                    e = [expert(2 * it), expert(2 * it + 1)]
                    e_next = [expert(2 * it + 2)]
                    for i in range(len(AHEAD), PIECES):
                        load(it, i, e)
                    for i in AHEAD:
                        load(it + 1, i, e_next)
                pairs(sync, body)

            @block.gpsimd
            def _(gp):
                def gather(it, q):
                    b = 2 * it + q
                    gp.indirect_dma_start(out=xg[:, q, :], out_offset=None, in_=K.scr["h2"],
                                          in_offset=bass.IndirectOffsetOnAxis(ap=row_ids[:, b:b + 1], axis=0)
                                          ).then_inc(gathered[q], 16)
                gather(0, 0)
                gather(0, 1)
                for i in BY_GPSIMD:
                    if i in AHEAD:
                        W.rest(gp, i % SLOTS, uses(0, i))
                used = gp.value_load(experts[0:1, N_BLOCK:N_BLOCK + 1], min_val=1, max_val=N_BLOCK // 2)
                for it in range(N_BLOCK // 2):
                    with gp.If(used > it):
                        for q in range(2):
                            gp.wait_ge(x_turned, 2 * it + q + 1)
                            gather(min(it + 1, N_BLOCK // 2 - 1), q)
                        for i in BY_GPSIMD:
                            if i not in AHEAD:
                                W.rest(gp, i % SLOTS, uses(it, i))
                        for i in BY_GPSIMD:
                            if i in AHEAD:
                                W.rest(gp, i % SLOTS, uses(it + 1, i))
                                gp.wait_ge(W.split[i % SLOTS], uses(it + 1, i) + 2)

            @block.tensor
            def _(pe):
                def turn_x(it, q):
                    b = 2 * it + q
                    pe.wait_ge(gathered[q], 16 * it + 16)
                    if q == 0:
                        pe.wait_ge(y_out, b + 1)
                        pe.wait_ge(y_out_b, b + 1)
                    for k in range(KD):
                        last = pe.transpose(K.ps[:, 2 * X_PAIR[q] + k // 4, (k % 4) * P:(k % 4 + 1) * P],
                                            xg[:, q, k::KD], K.ident[:])
                    last.then_inc(x_turned, 1)

                def turn_a(it, q):
                    pe.wait_ge(acted, 2 * it + q + 2)
                    for k in range(KE):
                        last = pe.transpose(K.ps[:, A_BANK[q], k * P:(k + 1) * P], ac[:, q, k::KE], K.ident[:])
                    last.then_inc(a_turned, 1)

                def hidden(it, q, pieces, bank):
                    for c, i in enumerate(pieces[q]):
                        s = i % SLOTS
                        pe.wait_ge(W.split[s], uses(it, i) + 2)
                        for j in range(4):
                            k = 4 * c + j
                            cols = slice(j * FE, (j + 1) * FE)
                            last = three_products(pe, K.ps[:, bank, :], X.hi[:, q, k, :], X.lo[:, q, k, :],
                                                  W.part.hi[:, s, 0, cols], W.part.lo[:, s, 0, cols], k == 0, k == KD - 1)
                        last.then_inc(W.done[s], 1)

                def down(it, q, c):
                    i = DOWN[q][c]
                    s = i % SLOTS
                    pe.wait_ge(W.split[s], uses(it, i) + 2)
                    pe.wait_ge(a_lo, 2 * it + q + 1)
                    pe.wait_ge(y_out, 2 * it + q + 1)
                    pe.wait_ge(y_out_b, 2 * it + q + 1)
                    for j in range(2):
                        k = 2 * c + j
                        for n in range(2):
                            cols = slice(j * D + n * HALF, j * D + (n + 1) * HALF)
                            last = three_products(pe, K.ps[:, 2 * Y_PAIR[q] + n, :], A.hi[:, q, k, :], A.lo[:, q, k, :],
                                                  W.part.hi[:, s, 0, cols], W.part.lo[:, s, 0, cols], k == 0, k == KE - 1)
                    last.then_inc(W.done[s], 1)

                turn_x(0, 0)
                turn_x(0, 1)

                def body(it):
                    for q in range(2):
                        b = 2 * it + q
                        pe.wait_ge(x_lo, b + 1)
                        pe.wait_ge(silued, b + 1)
                        hidden(it, q, GATE, GATE_BANK)
                        if q == 1:
                            turn_a(it, 0)
                        pe.wait_ge(acted, b + 1)
                        hidden(it, q, UP, UP_BANK)
                    down(it, 0, 0)
                    turn_a(it, 1)
                    down(it, 0, 1)
                    down(it, 1, 0)
                    turn_x(it + 1, 0)
                    turn_x(it + 1, 1)
                    down(it, 1, 1)
                pairs(pe, body)

            @block.scalar
            def _(act):
                act.sem_inc(silued, 1)
                act.sem_inc(y_out, 2)
                act.sem_inc(stored[0], 16)
                act.sem_inc(stored[1], 16)

                def x_part(it, q):
                    act.wait_ge(x_turned, 2 * it + q + 1)
                    act.activation(X.hi[:, q].rearrange("p k t -> p (k t)"), pair(K.ps, X_PAIR[q]), ACT.Copy
                                   ).then_inc(x_hi, 1)

                def split(it, *pieces):
                    for i in pieces:
                        W.round(act, i % SLOTS, uses(it, i))

                def body(it):
                    def a_part(q):
                        act.wait_ge(a_turned, 2 * it + q + 1)
                        act.activation(A.hi[:, q].rearrange("p k t -> p (k t)"), K.ps[:, A_BANK[q], :], ACT.Copy
                                       ).then_inc(a_hi, 1)

                    def silu(q):
                        wait_piece(act, it, GATE[q][1])
                        act.wait_ge(acted, 2 * it + q + 1)
                        act.activation(sg[:], K.ps[:, GATE_BANK, :], ACT.Silu).then_inc(silued, 1)

                    def y_half(q):
                        wait_piece(act, it, DOWN[q][1])
                        act.wait_ge(stored[q], 16 * it + 16)
                        act.activation(yo[:, q, 0:HALF], K.ps[:, 2 * Y_PAIR[q], :], ACT.Copy).then_inc(y_out, 1)

                    def store(q):
                        b = 2 * it + q
                        act.wait_ge(y_out, b + 3)
                        act.wait_ge(y_out_b, b + 3)
                        act.dma_start(K.scr["y"][bass.ds(b * P, P), :], yo[:, q, :]).then_inc(stored[q], 16)

                    split(it, 3, 4)
                    silu(0)
                    split(it, 5, 6, 7, 8)
                    silu(1)
                    split(it, 9)
                    a_part(0)
                    split(it, 10, 11)
                    a_part(1)
                    split(it + 1, 0)
                    y_half(0)
                    store(0)
                    x_part(it + 1, 0)
                    x_part(it + 1, 1)
                    split(it + 1, 1, 2)
                    y_half(1)
                    store(1)
                split(0, *AHEAD)
                x_part(0, 0)
                x_part(0, 1)
                used = pairs(act, body)
                for q in range(2):
                    act.wait_ge(stored[q], used * 16 + 16)
                    act.sem_inc(all_stored, 1)

            @block.vector
            def _(dve):
                dve.sem_inc(acted, 1)
                dve.sem_inc(y_out_b, 2)

                def x_part(it, q):
                    dve.wait_ge(x_hi, 2 * it + q + 1)
                    hi, lo = [x[:, q].rearrange("p k t -> p (k t)") for x in (X.hi, X.lo)]
                    dve.tensor_tensor(lo, pair(K.ps, X_PAIR[q]), hi, ALU.subtract).then_inc(x_lo, 1)

                def split(it, *pieces):
                    for i in pieces:
                        if i not in BY_GPSIMD:
                            W.rest(dve, i % SLOTS, uses(it, i))

                def body(it):
                    def a_part(q):
                        dve.wait_ge(a_hi, 2 * it + q + 1)
                        hi, lo = [x[:, q].rearrange("p k t -> p (k t)") for x in (A.hi, A.lo)]
                        dve.tensor_tensor(lo, K.ps[:, A_BANK[q], :], hi, ALU.subtract).then_inc(a_lo, 1)

                    def gated(q):
                        dve.wait_ge(silued, 2 * it + q + 2)
                        wait_piece(dve, it, UP[q][1])
                        dve.tensor_tensor(ac[:, q, :], K.ps[:, UP_BANK, :], sg[:], ALU.mult).then_inc(acted, 1)

                    def y_half(q):
                        wait_piece(dve, it, DOWN[q][1])
                        dve.wait_ge(stored[q], 16 * it + 16)
                        dve.tensor_copy(yo[:, q, HALF:], K.ps[:, 2 * Y_PAIR[q] + 1, :]).then_inc(y_out_b, 1)

                    split(it, 3, 5, 6)
                    gated(0)
                    split(it, 8, 9)
                    a_part(0)
                    gated(1)
                    split(it, 11)
                    a_part(1)
                    split(it + 1, 0)
                    y_half(0)
                    x_part(it + 1, 0)
                    x_part(it + 1, 1)
                    split(it + 1, 2)
                    y_half(1)
                split(0, *AHEAD)
                x_part(0, 0)
                x_part(0, 1)
                pairs(dve, body)


def stage_combine(nc, K, xt, dest, weight, out):
    with ExitStack() as ctx:
        g_in = semaphores(nc, K, *[f"cb_gathered{t}" for t in range(N_TILE)])
        gain_in, mixed, squared, rooted, inverted, scaled, stored = semaphores(
            nc, K, "cb_gain_in", "cb_mixed", "cb_squared", "cb_rooted", "cb_inverted", "cb_scaled", "cb_stored")
        gain = ctx.enter_context(nc.sbuf_tensor("cb_gain", [P, D], FP32))
        y = ctx.enter_context(nc.sbuf_tensor("cb_y", [P, N_TILE, 2, D], FP32))
        junk = ctx.enter_context(nc.sbuf_tensor("cb_junk", [P, D], FP32))
        ss = ctx.enter_context(nc.sbuf_tensor("cb_ss", [P, 3, N_TILE], FP32))
        with nc.Block(no_gpsimd_drain=True) as block:

            @block.gpsimd
            def _(gp):
                for t in range(N_TILE):
                    for c in range(2):
                        gp.indirect_dma_start(out=y[:, t, c, :], out_offset=None, in_=K.scr["y"],
                                              in_offset=bass.IndirectOffsetOnAxis(ap=dest[:, c, t:t + 1], axis=0)
                                              ).then_inc(g_in[t], 16)

            @block.sync
            def _(sync):
                sync.dma_start(gain[:], K.dram["final_norm_g_2"].rearrange("(a n) -> a n", a=1).to_broadcast([P, D])).then_inc(gain_in, 16)
                for t in range(N_TILE):
                    sync.wait_ge(scaled, t + 1)
                    sync.dma_start(out[t * P:(t + 1) * P, :], xt[:, t, :]).then_inc(stored, 16)
                sync.wait_ge(stored, 16 * N_TILE)

            @block.vector
            def _(dve):
                for t in range(N_TILE):
                    dve.wait_ge(g_in[t], 32)
                    for c in range(2):
                        dve.scalar_tensor_tensor(out=xt[:, t, :], in0=y[:, t, c, :], scalar=weight[:, c, t:t + 1],
                                                 in1=xt[:, t, :], op0=ALU.mult, op1=ALU.add).then_inc(mixed, 1)
                        dve.wait_ge(mixed, 2 * t + c + 1)
                dve.wait_ge(gain_in, 16)
                for t in range(N_TILE):
                    dve.wait_ge(rooted, t + 1)
                    dve.reciprocal(ss[:, 2, t:t + 1], ss[:, 1, t:t + 1]).then_inc(inverted, 1)
                    dve.wait_ge(inverted, t + 1)
                    dve.scalar_tensor_tensor(out=xt[:, t, :], in0=xt[:, t, :], scalar=ss[:, 2, t:t + 1], in1=gain[:],
                                             op0=ALU.mult, op1=ALU.mult).then_inc(scaled, 1)

            @block.scalar
            def _(act):
                for t in range(N_TILE):
                    act.wait_ge(mixed, 2 * (t + 1))
                    if t:
                        act.wait_ge(squared, t)
                    act.activation(junk[:], xt[:, t, :], ACT.Square, accum_out=ss[:, 0, t:t + 1]).then_inc(squared, 1)
                    act.wait_ge(squared, t + 1)
                    act.activation(ss[:, 1, t:t + 1], ss[:, 0, t:t + 1], ACT.Sqrt, bias=K.eps_rms[:, 0:1],
                                   scale=1.0 / D).then_inc(rooted, 1)


def second_mixer(nc, K):
    with ExitStack() as ctx:
        G = ctx.enter_context(nc.sbuf_tensor("G", [P, N_CHUNK, HEADS], FP32))
        beta = ctx.enter_context(nc.sbuf_tensor("beta", [P, N_CHUNK, HEADS], FP32))
        second_projections(nc, K, G, beta)
        retire_semaphores(nc, K)
        oT = ctx.enter_context(nc.sbuf_tensor("oT", [P, 2 * HEADS, LEN], FP32))
        stage_recurrences(nc, K, G, beta, oT)
        part = Halves(nc, ctx, "o_parts", [P, KD, SEQ])
        stage_head_norm(nc, K, oT, part)
        W = Weights(nc, K, ctx, "wo2", 2, KD)
        stage_merge(nc, K, oT, part, W, K.dram["w_out_2"][0])
        stage_residual(nc, K, "wo2", oT, P, part, W, K.dram["w_out_2"][0])


def second_moe(nc, K, out):
    with ExitStack() as ctx:
        xt = ctx.enter_context(nc.sbuf_tensor("xt", [P, N_TILE, D], FP32))
        dest = ctx.enter_context(nc.sbuf_tensor("dest", [P, 2, N_TILE], I32))
        weight = ctx.enter_context(nc.sbuf_tensor("weight", [P, 2, N_TILE], FP32))
        row_ids = ctx.enter_context(nc.sbuf_tensor("row_ids", [P, N_BLOCK], I32))
        experts = ctx.enter_context(nc.sbuf_tensor("experts", [1, N_BLOCK + 1], I32))
        with ExitStack() as inner:
            L = inner.enter_context(nc.sbuf_tensor("logits", [P, N_TILE, N_LOGIT], FP32))
            stage_to_tokens(nc, K, xt, L)
            stage_route(nc, K, L, dest, weight, row_ids, experts)
        stage_experts(nc, K, row_ids, experts)
        stage_combine(nc, K, xt, dest, weight, out)


def program(nc, dram, out):
    K = Pack()
    K.dram = dram
    with ExitStack() as ctx:
        common(nc, ctx, K)
        K.scr = scratch(nc)
        first_block(nc, K)
        retire_semaphores(nc, K)
        second_mixer(nc, K)
        retire_semaphores(nc, K)
        second_moe(nc, K, out)


_INS = ["x", "norm_mix_g", "w_in", "conv_a_w", "conv_b_w", "conv_b_b", "ln_b_g", "ln_b_b", "w_out", "norm_ffn_g",
        "w_gate", "w_up", "conv_ffn_w", "w_down", "norm_final_g", "meta_tokens_2", "hg_lb_logits_2", "norm_mix_g_2",
        "w_in_2", "gd_conv_w_2", "gd_A_log_2", "gd_dt_bias_2", "hg_norm_g_2", "gd_norm_g_2", "hg_up_2", "gd_up_2",
        "w_out_2", "norm_ffn_g_2", "router_group_w_2", "router_group_b_2", "router_expert_w_2", "router_expert_b_2",
        "w_gate_2", "w_up_2", "w_down_2", "final_norm_g_2"]


def kernel(**inputs):
    import concourse.bacc as _bacc
    from concourse.bass_utils import run_bass_kernel_spmd as _run

    nc = _bacc.Bacc("TRN2", target_bir_lowering=False, num_devices=1)
    arrays, dram = {}, {}
    for name in _INS:
        a = np.ascontiguousarray(inputs[name])
        arrays[f"in_{name}_dram"] = a
        dram[name] = nc.dram_tensor(f"in_{name}_dram", a.shape, mybir.dt.from_np(a.dtype), kind="ExternalInput").ap()
    out = nc.dram_tensor("out_0_dram", (1, SEQ, D), FP32, kind="ExternalOutput").ap()
    program(nc, dram, out[0])
    r = _run(nc, [arrays], core_ids=[0])
    return r.results[0]["out_0_dram"]
```
